# Optimizing a Trainium2 kernel written in Bass

```python
import math
import jax, jax.numpy as jnp
from jax import lax
import numpy as np

D_MODEL = 1024
BATCH = 1
SEQ = 128
DEPTH = 2
DEC_BATCH = 1
DEC_SEQ = 256
PAST_LEN = 128

GRID_W = 64
N_HEADS = 4
DK = D_MODEL // 8
DV = D_MODEL // 4
DK_TOT = N_HEADS * DK
DV_TOT = N_HEADS * DV
GATE_RANK = 16
GATE_TAU = 16.0
CHUNK = 64
N_GLA = (DEPTH + 1) // 2
N_MLSTM = DEPTH // 2
GLA_IN = 2 * DK_TOT + 2 * DV_TOT + 2 * GATE_RANK
MLSTM_IN = 2 * DK_TOT + 2 * DV_TOT + 4 * N_HEADS
N_GROUPS = 4
EXPERTS_PER_GROUP = 8
N_EXPERTS = N_GROUPS * EXPERTS_PER_GROUP
D_EXPERT = D_MODEL // 4
TOP_K_IN_GROUP = 2
DN_ALPHA = (2.0 * DEPTH) ** 0.25
DN_BETA = (8.0 * DEPTH) ** -0.25
LN_EPS = 1e-5

kernel_name = "hybrid_gla_mlstm_hmoe_diffusion_step"

F32 = jnp.float32

def _layernorm(x, g, b):
    xf = x.astype(F32)
    mu = jnp.mean(xf, -1, keepdims=True)
    var = jnp.mean(jnp.square(xf - mu), -1, keepdims=True)
    return ((xf - mu) * lax.rsqrt(var + LN_EPS) * g + b).astype(x.dtype)

def _to_heads(a, d):
    B, T, _ = a.shape
    return a.reshape(B, T, N_HEADS, d).transpose(0, 2, 1, 3).astype(F32)

def _flip(a):
    return jnp.flip(a, axis=2)

def _head_norm(o, g):
    mu = jnp.mean(o, -1, keepdims=True)
    var = jnp.mean(jnp.square(o - mu), -1, keepdims=True)
    o = (o - mu) * lax.rsqrt(var + LN_EPS)
    B, H, T, _ = o.shape
    return o.transpose(0, 2, 1, 3).reshape(B, T, H * DV) * g

def _grid_posemb(T):
    rows = T // GRID_W
    r, cidx = jnp.meshgrid(jnp.arange(rows), jnp.arange(GRID_W), indexing="ij")
    nf = D_MODEL // 4
    freqs = jnp.exp(-math.log(10000.0) * jnp.arange(nf, dtype=F32) / nf)

    def emb(p):
        a = p.reshape(-1).astype(F32)[:, None] * freqs
        return jnp.concatenate([jnp.sin(a), jnp.cos(a)], -1)

    return jnp.concatenate([emb(r), emb(cidx)], -1)

def _gla_chunked(q, k, v, g, S0):
    B, H, T, _ = q.shape
    N = T // CHUNK
    q = q.reshape(B, H, N, CHUNK, DK)
    k = k.reshape(B, H, N, CHUNK, DK)
    v = v.reshape(B, H, N, CHUNK, DV)
    b = jnp.cumsum(g.reshape(B, H, N, CHUNK, DK), axis=3)
    b_last = b[:, :, :, -1]
    b_ref = b[:, :, :, CHUNK // 2:CHUNK // 2 + 1]
    mask = jnp.tril(jnp.ones((CHUNK, CHUNK), dtype=bool))
    a = jnp.einsum("bhncd,bhnsd->bhncs", q * jnp.exp(b - b_ref), k * jnp.exp(b_ref - b))
    a = jnp.where(mask, a, 0.0)
    o_intra = jnp.einsum("bhncs,bhnse->bhnce", a, v)
    d_state = jnp.einsum("bhncd,bhnce->bhnde", k * jnp.exp(b_last[:, :, :, None] - b), v)
    decay = jnp.exp(b_last)

    def step(S, inp):
        d, u = inp
        return d[..., None] * S + u, S

    S_f, S_starts = lax.scan(step, S0, (jnp.moveaxis(decay, 2, 0), jnp.moveaxis(d_state, 2, 0)))
    S_starts = jnp.moveaxis(S_starts, 0, 2)
    o_inter = jnp.einsum("bhncd,bhnde->bhnce", q * jnp.exp(b), S_starts)
    return (o_intra + o_inter).reshape(B, H, T, DV), S_f

def _mlstm_chunked(q, k, v, i_pre, log_f, C0, n0, m0):
    B, H, T, _ = q.shape
    N = T // CHUNK
    q = q.reshape(B, H, N, CHUNK, DK)
    k = k.reshape(B, H, N, CHUNK, DK)
    v = v.reshape(B, H, N, CHUNK, DV)
    i_pre = i_pre.reshape(B, H, N, CHUNK)
    b = jnp.cumsum(log_f.reshape(B, H, N, CHUNK), axis=-1)
    b_last = b[..., -1]
    mask = jnp.tril(jnp.ones((CHUNK, CHUNK), dtype=bool))
    d_log = jnp.where(mask, b[..., :, None] - b[..., None, :] + i_pre[..., None, :], -jnp.inf)
    a = b_last[..., None] - b + i_pre
    m_loc = jnp.max(a, -1)
    kw = k * jnp.exp(a - m_loc[..., None])[..., None]
    kv_loc = jnp.einsum("bhncd,bhnce->bhnde", kw, v)
    k_loc = jnp.sum(kw, axis=3)

    def step(carry, inp):
        C, n, m = carry
        bl, ml, kvl, kl = inp
        m_new = jnp.maximum(bl + m, ml)
        s_old = jnp.exp(bl + m - m_new)
        s_loc = jnp.exp(ml - m_new)
        C_new = s_old[..., None, None] * C + s_loc[..., None, None] * kvl
        n_new = s_old[..., None] * n + s_loc[..., None] * kl
        return (C_new, n_new, m_new), (C, n, m)

    mv = lambda t: jnp.moveaxis(t, 2, 0)
    (C_f, n_f, m_f), (C_s, n_s, m_s) = lax.scan(
        step, (C0, n0, m0), (mv(b_last), mv(m_loc), mv(kv_loc), mv(k_loc)))
    C_s = jnp.moveaxis(C_s, 0, 2)
    n_s = jnp.moveaxis(n_s, 0, 2)
    m_s = jnp.moveaxis(m_s, 0, 2)
    l_inter = b + m_s[..., None]
    m_i = jnp.maximum(l_inter, jnp.max(d_log, -1))
    s = jnp.einsum("bhncd,bhnsd->bhncs", q, k) * jnp.exp(d_log - m_i[..., None])
    e_inter = jnp.exp(l_inter - m_i)
    num = jnp.einsum("bhncs,bhnse->bhnce", s, v) + e_inter[..., None] * jnp.einsum("bhncd,bhnde->bhnce", q, C_s)
    den = jnp.sum(s, -1) + e_inter * jnp.einsum("bhncd,bhnd->bhnc", q, n_s)
    h = num / jnp.maximum(jnp.abs(den), jnp.exp(-m_i))[..., None]
    return h.reshape(B, H, T, DV), C_f, n_f, m_f

def _gla_mixer(h, w_in, w_gate, b_gate, norm_g, w_out, S0_f, S0_b):
    B, T, _ = h.shape
    p = h @ w_in
    q, k, v, r, glr = jnp.split(p, [DK_TOT, 2 * DK_TOT, 2 * DK_TOT + DV_TOT, 2 * DK_TOT + 2 * DV_TOT], axis=-1)
    glr = glr.reshape(B, T, 2, GATE_RANK)
    g = jax.nn.log_sigmoid((jnp.einsum("btzr,zrk->btzk", glr, w_gate) + b_gate).astype(F32)) / GATE_TAU
    g_f = _to_heads(g[:, :, 0], DK)
    g_b = _to_heads(g[:, :, 1], DK)
    qh = _to_heads(q, DK) * (DK ** -0.5)
    kh = _to_heads(k, DK)
    vh = _to_heads(v, DV)
    o_f, S_f = _gla_chunked(qh, kh, vh, g_f, S0_f.astype(F32))
    o_b, S_b = _gla_chunked(_flip(qh), _flip(kh), _flip(vh), _flip(g_b), S0_b.astype(F32))
    o = _head_norm(o_f + _flip(o_b), norm_g) * jax.nn.silu(r.astype(F32))
    return o.astype(h.dtype) @ w_out, S_f, S_b

def _mlstm_mixer(h, w_in, b_gates, norm_g, w_out, C0_f, n0_f, m0_f, C0_b, n0_b, m0_b):
    B, T, _ = h.shape
    p = h @ w_in
    q, k, v, og, gt = jnp.split(p, [DK_TOT, 2 * DK_TOT, 2 * DK_TOT + DV_TOT, 2 * DK_TOT + 2 * DV_TOT], axis=-1)
    gt = (gt.reshape(B, T, 4, N_HEADS).astype(F32) + b_gates).transpose(2, 0, 3, 1)
    i_f, f_f, i_b, f_b = gt[0], gt[1], gt[2], gt[3]
    qh = _to_heads(q, DK) * (DK ** -0.5)
    kh = _to_heads(k, DK)
    vh = _to_heads(v, DV)
    h_f, C_f, n_f, m_f = _mlstm_chunked(qh, kh, vh, i_f, jax.nn.log_sigmoid(f_f),
                                        C0_f.astype(F32), n0_f.astype(F32), m0_f.astype(F32))
    h_b, C_b, n_b, m_b = _mlstm_chunked(_flip(qh), _flip(kh), _flip(vh), _flip(i_b), _flip(jax.nn.log_sigmoid(f_b)),
                                        C0_b.astype(F32), n0_b.astype(F32), m0_b.astype(F32))
    o = _head_norm(h_f + _flip(h_b), norm_g) * jax.nn.sigmoid(og.astype(F32))
    return o.astype(h.dtype) @ w_out, (C_f, n_f, m_f), (C_b, n_b, m_b)

def _hier_moe(h, w_group, b_group, w_expert, b_expert, w_gate, w_up, w_down):
    B, T, D = h.shape
    hf = h.reshape(B * T, D)
    glog = (hf @ w_group + b_group).astype(F32)
    gprob = jax.nn.softmax(glog, -1)
    gsel = jnp.argmax(glog, -1)
    gw = jnp.take_along_axis(gprob, gsel[:, None], 1)[:, 0]
    elog = (hf @ w_expert + b_expert).astype(F32).reshape(-1, N_GROUPS, EXPERTS_PER_GROUP)
    elog_sel = jnp.take_along_axis(elog, gsel[:, None, None], 1)[:, 0]
    top_p, top_i = lax.top_k(jax.nn.softmax(elog_sel, -1), TOP_K_IN_GROUP)
    top_p = top_p / jnp.sum(top_p, -1, keepdims=True)
    eid = gsel[:, None] * EXPERTS_PER_GROUP + top_i
    comb = jnp.sum(jax.nn.one_hot(eid, N_EXPERTS, dtype=F32) * (gw[:, None] * top_p)[..., None], axis=1)
    a = jnp.einsum("nd,edf->nef", hf, w_gate)
    u = jnp.einsum("nd,edf->nef", hf, w_up)
    hid = jax.nn.silu(a) * u * comb[..., None].astype(h.dtype)
    return jnp.einsum("nef,efd->nd", hid, w_down).reshape(B, T, D)

def _modulation(cvec, w, b):
    return (jax.nn.silu(cvec) @ w + b).reshape(cvec.shape[0], 6, D_MODEL)

def setup_inputs(seed: int = 0) -> dict:
    key = jax.random.key(seed)
    ks = jax.random.split(key, 32)
    nrm = lambda k, shape, s: jax.random.normal(k, shape, F32) * s
    gla_w_in = nrm(ks[8], (N_GLA, D_MODEL, GLA_IN), D_MODEL ** -0.5)
    gla_w_in = gla_w_in.at[:, :, 2 * DK_TOT:2 * DK_TOT + DV_TOT].multiply(DN_BETA)
    mlstm_w_in = nrm(ks[13], (N_MLSTM, D_MODEL, MLSTM_IN), D_MODEL ** -0.5)
    mlstm_w_in = mlstm_w_in.at[:, :, 2 * DK_TOT:2 * DK_TOT + DV_TOT].multiply(DN_BETA)
    f_base = jnp.linspace(3.0, 6.0, N_HEADS, dtype=F32)
    gate_base = jnp.zeros((4, N_HEADS), F32).at[1].set(f_base).at[3].set(f_base)
    return {
        "x_prompt": nrm(ks[0], (BATCH, SEQ, D_MODEL), 1.0),
        "x_sample": nrm(ks[1], (DEC_BATCH, DEC_SEQ, D_MODEL), 1.0),
        "state_gla_S": nrm(ks[2], (DEC_BATCH, N_GLA, 2, N_HEADS, DK, DV), 0.5),
        "state_mlstm_C": nrm(ks[3], (DEC_BATCH, N_MLSTM, 2, N_HEADS, DK, DV), 0.5),
        "state_mlstm_n": nrm(ks[4], (DEC_BATCH, N_MLSTM, 2, N_HEADS, DK), 0.5),
        "state_mlstm_m": nrm(ks[5], (DEC_BATCH, N_MLSTM, 2, N_HEADS), 1.0),
        "c": nrm(ks[6], (DEC_BATCH, D_MODEL), 1.0),
        "c_ctx": nrm(ks[7], (D_MODEL,), 1.0),
        "gla_w_in": gla_w_in,
        "gla_w_gate": nrm(ks[9], (N_GLA, 2, GATE_RANK, DK_TOT), GATE_RANK ** -0.5),
        "gla_b_gate": nrm(ks[10], (N_GLA, 2, DK_TOT), 0.1),
        "gla_norm_g": 1.0 + nrm(ks[11], (N_GLA, DV_TOT), 0.02),
        "gla_w_out": nrm(ks[12], (N_GLA, DV_TOT, D_MODEL), DV_TOT ** -0.5 * DN_BETA),
        "mlstm_w_in": mlstm_w_in,
        "mlstm_b_gates": gate_base + nrm(ks[14], (N_MLSTM, 4, N_HEADS), 0.1),
        "mlstm_norm_g": 1.0 + nrm(ks[15], (N_MLSTM, DV_TOT), 0.02),
        "mlstm_w_out": nrm(ks[16], (N_MLSTM, DV_TOT, D_MODEL), DV_TOT ** -0.5 * DN_BETA),
        "adaln_w": nrm(ks[17], (DEPTH, D_MODEL, 6 * D_MODEL), 0.5 * D_MODEL ** -0.5),
        "adaln_b": nrm(ks[18], (DEPTH, 6 * D_MODEL), 0.02),
        "ln_g": 1.0 + nrm(ks[19], (DEPTH, 2, D_MODEL), 0.02),
        "ln_b": nrm(ks[20], (DEPTH, 2, D_MODEL), 0.02),
        "moe_w_group": nrm(ks[21], (DEPTH, D_MODEL, N_GROUPS), D_MODEL ** -0.5),
        "moe_b_group": nrm(ks[22], (DEPTH, N_GROUPS), 0.01),
        "moe_w_expert": nrm(ks[23], (DEPTH, D_MODEL, N_EXPERTS), D_MODEL ** -0.5),
        "moe_b_expert": nrm(ks[24], (DEPTH, N_EXPERTS), 0.01),
        "moe_w_gate": nrm(ks[25], (DEPTH, N_EXPERTS, D_MODEL, D_EXPERT), D_MODEL ** -0.5),
        "moe_w_up": nrm(ks[26], (DEPTH, N_EXPERTS, D_MODEL, D_EXPERT), D_MODEL ** -0.5),
        "moe_w_down": nrm(ks[27], (DEPTH, N_EXPERTS, D_EXPERT, D_MODEL), D_EXPERT ** -0.5 * DN_BETA),
    }

def reference(x_prompt, x_sample, state_gla_S, state_mlstm_C, state_mlstm_n, state_mlstm_m, c, c_ctx,
              gla_w_in, gla_w_gate, gla_b_gate, gla_norm_g, gla_w_out,
              mlstm_w_in, mlstm_b_gates, mlstm_norm_g, mlstm_w_out,
              adaln_w, adaln_b, ln_g, ln_b,
              moe_w_group, moe_b_group, moe_w_expert, moe_b_expert, moe_w_gate, moe_w_up, moe_w_down):
    Bc = x_prompt.shape[0]
    x_ctx = x_prompt
    x_lat = x_sample + _grid_posemb(x_sample.shape[1]).astype(x_sample.dtype)[None]
    gla_states, ml_C, ml_n, ml_m = [], [], [], []
    for l in range(DEPTH):
        s = l // 2
        mod_c = _modulation(c_ctx[None], adaln_w[l], adaln_b[l])[:, None]
        mod_l = _modulation(c, adaln_w[l], adaln_b[l])[:, None]
        h_c = x_ctx * (1.0 + mod_c[:, :, 1]) + mod_c[:, :, 0]
        h_l = x_lat * (1.0 + mod_l[:, :, 1]) + mod_l[:, :, 0]
        if l % 2 == 0:
            z = jnp.zeros((Bc, N_HEADS, DK, DV), F32)
            y_c, S_f, S_b = _gla_mixer(h_c, gla_w_in[s], gla_w_gate[s], gla_b_gate[s], gla_norm_g[s], gla_w_out[s], z, z)
            y_l, _, _ = _gla_mixer(h_l, gla_w_in[s], gla_w_gate[s], gla_b_gate[s], gla_norm_g[s], gla_w_out[s],
                                   state_gla_S[:, s, 0], state_gla_S[:, s, 1])
            gla_states.append(jnp.stack([S_f, S_b], 1))
        else:
            zC = jnp.zeros((Bc, N_HEADS, DK, DV), F32)
            zn = jnp.zeros((Bc, N_HEADS, DK), F32)
            zm = jnp.zeros((Bc, N_HEADS), F32)
            y_c, st_f, st_b = _mlstm_mixer(h_c, mlstm_w_in[s], mlstm_b_gates[s], mlstm_norm_g[s], mlstm_w_out[s],
                                           zC, zn, zm, zC, zn, zm)
            y_l, _, _ = _mlstm_mixer(h_l, mlstm_w_in[s], mlstm_b_gates[s], mlstm_norm_g[s], mlstm_w_out[s],
                                     state_mlstm_C[:, s, 0], state_mlstm_n[:, s, 0], state_mlstm_m[:, s, 0],
                                     state_mlstm_C[:, s, 1], state_mlstm_n[:, s, 1], state_mlstm_m[:, s, 1])
            ml_C.append(jnp.stack([st_f[0], st_b[0]], 1))
            ml_n.append(jnp.stack([st_f[1], st_b[1]], 1))
            ml_m.append(jnp.stack([st_f[2], st_b[2]], 1))
        x_ctx = _layernorm(DN_ALPHA * x_ctx + mod_c[:, :, 2] * y_c, ln_g[l, 0], ln_b[l, 0])
        x_lat = _layernorm(DN_ALPHA * x_lat + mod_l[:, :, 2] * y_l, ln_g[l, 0], ln_b[l, 0])
        h_c = x_ctx * (1.0 + mod_c[:, :, 4]) + mod_c[:, :, 3]
        h_l = x_lat * (1.0 + mod_l[:, :, 4]) + mod_l[:, :, 3]
        moe_args = (moe_w_group[l], moe_b_group[l], moe_w_expert[l], moe_b_expert[l],
                    moe_w_gate[l], moe_w_up[l], moe_w_down[l])
        x_ctx = _layernorm(DN_ALPHA * x_ctx + mod_c[:, :, 5] * _hier_moe(h_c, *moe_args), ln_g[l, 1], ln_b[l, 1])
        x_lat = _layernorm(DN_ALPHA * x_lat + mod_l[:, :, 5] * _hier_moe(h_l, *moe_args), ln_g[l, 1], ln_b[l, 1])
    dt = x_prompt.dtype
    new_gla_S = jnp.stack(gla_states, 1).astype(dt)
    new_mlstm_C = jnp.stack(ml_C, 1).astype(dt)
    new_mlstm_n = jnp.stack(ml_n, 1).astype(dt)
    new_mlstm_m = jnp.stack(ml_m, 1).astype(dt)
    return (x_ctx, x_lat, new_gla_S, new_mlstm_C, new_mlstm_n, new_mlstm_m)


_drawn_inputs = setup_inputs


def setup_inputs(seed=0):
    import zlib

    import numpy as np

    out = dict(_drawn_inputs(seed))
    spreads = {}
    factors = {'state_gla_S': 8.0,
     'state_mlstm_C': 5.97,
     'state_mlstm_n': 8.0,
     'state_mlstm_m': 8.0,
     'gla_norm_g': 30.366,
     'mlstm_norm_g': 51.872,
     'moe_b_group': 35.703,
     'moe_b_expert': 43.125}
    for name, (base, spread) in spreads.items():
        noise = np.random.default_rng([zlib.crc32(name.encode()), seed]).standard_normal(out[name].shape)
        drawn = base * np.exp(spread * noise) if base else spread * noise
        out[name] = __import__('jax').numpy.asarray(drawn.astype(out[name].dtype))
    for name, factor in factors.items():
        out[name] = (out[name] * factor).astype(out[name].dtype)
    return out
```

```python
from contextlib import ExitStack

import numpy as np
import concourse.bass as bass
from concourse import mybir

F32 = mybir.dt.float32
BF16 = mybir.dt.bfloat16
I32 = mybir.dt.int32
ALU = mybir.AluOpType
ACT = mybir.ActivationFunctionType
AX = mybir.AxisListType.X

P = 128
D = 1024
KD = D // P
DEPTH = 2
N_CTX, N_LAT = 128, 256
N = N_CTX + N_LAT
NT = N // P
GRID_W = 64
H = 4
DK, DV = 128, 256
MV = DV // P
RANK = 16
TAU = 16.0
CH = 64
NCH = N // CH
NGRP, EPG = 4, 8
NE = NGRP * EPG
DE = 256
FE = DE // P
EPS = 1e-5
ALPHA = (2.0 * DEPTH) ** 0.25
CAP = 96
NS = 2 * N
NSP = NS + CAP
MAXJ = (NS - 1) // CAP
SC = NS // P
G = 2
PIECE = 2048
BIG = 3.0e38
STREAMS = ((0, 0, N_CTX), (1, N_CTX, N))

G_MOD, G_HEAD, G_OUT, G_EXP = 8, H, 2, NE
G_LAYER = G_MOD + G_HEAD + G_OUT + G_EXP
OUT_W = (256, 128, 128)

N_STATES = 10
CHAIN = {(1, 0): (2, 3, 4, 5), (1, 1): (5, 4, 3, 2), (0, 0): (0, 1), (0, 1): (1, 0)}


def chain_steps(dirs):
    out = []
    for s in range(4):
        for lat, d in CHAIN:
            if d in dirs and s < len(CHAIN[lat, d]):
                out.append((lat, d, s, CHAIN[lat, d][s], (not lat) or s < 3))
    return out


def state_places(l):
    past, out = {}, []
    for dirs in (((0, 1),) if l == 0 else ((0,), (1,))):
        for lat, d, s, n, more in chain_steps(dirs):
            if more:
                out.append((6 + n % 2, past.get(n % 2)))
                past[n % 2] = len(out) - 1
    return out


def is_neg(v):
    return isinstance(v, int) and v < 0


def backbone_step(nc, A, O):
    ctx = ExitStack()
    with ctx:
        def sb(name, shape, dt=F32):
            return ctx.enter_context(nc.sbuf_tensor(name, shape, dt))

        def sem(name):
            return ctx.enter_context(nc.semaphore(name))

        bank = [ctx.enter_context(nc.psum_tensor(f"bank{i}", [P, 512], F32)) for i in range(8)]

        ring = sb("ring", [P, G, 3, PIECE])
        xT = sb("xT", [P, KD, N])
        hT = sb("hT", [P, KD, N])
        zT = sb("zT", [P, KD, N])
        st0 = sb("st0", [P, 2 * H, DV])
        n0 = sb("n0", [P, 2 * H])
        m0 = sb("m0", [H, 2])
        cT = sb("cT", [P, KD, 2])
        scT = sb("scT", [P, KD, 2])
        mod = sb("mod", [P, DEPTH, 6 * KD, 2])
        modb = sb("modb", [P, DEPTH, 6 * KD])
        lng = sb("lng", [P, 2 * DEPTH, KD])
        lnb = sb("lnb", [P, 2 * DEPTH, KD])
        hng = sb("hng", [P, 2, KD])
        wglr = sb("wglr", [P, KD, 2 * RANK])
        bgate = sb("bgate", [P, 2 * H])
        wgt = zT[:, :, 0:P]
        bgt = sb("bgt", [H, 4])
        wrt = sb("wrt", [P, DEPTH, KD, NGRP + NE])
        brt = sb("brt", [1, DEPTH, NGRP + NE])
        ident = sb("ident", [P, P])
        ones_d = sb("ones_d", [P, P])
        ones_v = sb("ones_v", [P, P])
        ones = sb("ones", [P, P])
        onesb = sb("onesb", [P, P], BF16)
        trib = sb("trib", [P, P], BF16)
        rowsel = sb("rowsel", [H, H, P])
        causal = sb("causal", [P, 2, NT, P])
        keep = sb("keep", [P, N])
        fresh = sb("fresh", [H, N])
        slot_f = sb("slot_f", [P, NS])
        ramp = sb("ramp", [P, EPG])
        epst = sb("epst", [P, 1])
        onet = sb("onet", [P, 1])
        jcap = sb("jcap", [1, MAXJ, NE])
        eidx = sb("eidx", [1, MAXJ, NE])
        REGION = 22656
        region = sb("region", [P, REGION])
        taken = {"mix": 0, "moe": 0}

        def part(stage, *dims):
            size = int(np.prod(dims))
            a = taken[stage]
            taken[stage] += size
            assert taken[stage] <= REGION, (stage, taken)
            v = region[:, a:a + size]
            if len(dims) == 2:
                v = v.rearrange("p (a b) -> p a b", a=dims[0])
            if len(dims) == 3:
                v = v.rearrange("p (a b c) -> p a b c", a=dims[0], b=dims[1])
            if len(dims) == 4:
                v = v.rearrange("p (a b c d) -> p a b c d", a=dims[0], b=dims[1], c=dims[2])
            return v

        oT = part("mix", KD, N)
        early = oT.rearrange("p a b -> p (a b)")
        slot_i = early[:, 0:NS].bitcast(I32)
        posc = early[:, NS:NS + KD // 2 * GRID_W].rearrange("p (a b) -> p a b", b=GRID_W)
        posr = early[:, NS + KD // 2 * GRID_W:NS + KD // 2 * (GRID_W + N_LAT // GRID_W)].rearrange("p (a b) -> p a b", a=KD // 2)
        qT = part("mix", 2, N)
        kT = part("mix", 2, N)
        vt = part("mix", 2, NT, DV)
        rT = part("mix", 2, MV, N)
        ktok = part("mix", 2, NT, P)
        am = sb("am", [P, 2, N])
        st = part("mix", 4, 2, DV)
        wgate = st.rearrange("p a b c -> p (a b c)")[0:2 * RANK, 0:2 * H * DK].rearrange("p (a b) -> p a b", a=2)
        sfin = part("mix", 2, 2, DV)
        num = part("mix", MV, N)
        nsq = part("mix", MV, N)
        rs = part("mix", N)
        base_e = taken["mix"]
        ea = part("mix", 2 * H, N)
        eb = part("mix", 2 * H, N)
        ed = part("mix", 2 * H, N)
        ec = zT
        dec = sb("dec", [P, 2 * H, NCH])
        taken["mix"] = base_e
        graw = part("mix", 4, N)
        rows = [part("mix", 2, N) for _ in range(7)]
        lf, bcum, urow, wrow, einr, mir, ulr = rows
        expd, dtmp, emt, rden = (graw[:, i, :] for i in range(4))
        einb = lf
        qe = part("mix", 2, N)
        nb = part("mix", 2, 2, P)
        nb0 = part("mix", P)
        mst = sb("mst", [H, 2, 2, 5])
        decr = sb("decr", [H, 2, NCH])
        cols = sb("cols", [P, 12, H])
        nfin = sb("nfin", [P, 2 * H])
        mfin = sb("mfin", [H, 2])
        xg = part("moe", KD, NSP)
        yg = part("moe", KD, NSP)
        htok = part("moe", NT, D)
        cw = part("moe", SC, N)
        ysl = region[:, 0:SC * D].rearrange("p (a b) -> p a b", a=SC)
        sel = region[:, KD * NSP:KD * NSP + NT * NS].rearrange("p (a b) -> p a b", a=NT)
        pw = zT[:, 0:6, :].rearrange("p a b -> p (a b)").rearrange("p (a b) -> p a b", a=NT)
        htw = hT[:, 0:2, :].rearrange("p a b -> p (a b)")
        sg = part("moe", 2, FE, CAP)
        hid = part("moe", 2, FE, CAP)
        lgt = part("moe", NT, NGRP + NE)
        R = {n: sb("r_" + n, [P, NT]) for n in ("gmax", "gpm", "gsum", "gw", "m1", "m2", "pm", "dd", "den", "w1", "w2", "s1", "s2")}
        gsc = sb("gsc", [P, NT, NGRP])
        goh = sb("goh", [P, NT, NGRP])
        e4 = part("moe", NT, NGRP, EPG)
        es = part("moe", NT, EPG)
        esc = part("moe", NT, EPG)
        eoh = part("moe", 2, NT, EPG)
        o12 = part("moe", 2, NT, NE)
        mb = sb("mb", [P, NT, NE], BF16)
        cnt = sb("cnt", [P, NE])
        cums = sb("cums", [P, NE])
        offs = sb("offs", [P, NE])
        slt = part("moe", NT, NE)
        offi = sb("offi", [1, NE], I32)
        xrow = [hT[0:1, 2 + i, 0:MAXJ * NE].rearrange("p (a b) -> p a b", a=MAXJ) for i in range(4)]
        xone = hT[0:1, 6, 0:MAXJ * NE]
        xlist = sb("xlist", [1, 2 * MAXJ + 1])
        xlisti = sb("xlisti", [1, 2 * MAXJ + 1], I32)

        S = {n: sem(n) for n in (
            "small_in", "x_in", "state_in", "consts", "silu_c", "mod_cols", "mod_ready", "h_ready",
            "pj_ready", "pj_free", "gates_in", "logit_sb", "gate_sp", "gate_d", "e_ready", "heads_in",
            "scaled", "kt_ready", "kt_sb", "sc_ready", "am_ready", "num_ready", "num_sb", "ds_ready",
            "state_ready", "mean_ready", "cent", "sq_ready", "var_ready", "std_ready", "o_ready", "den_free",
            "fin_state", "yscaled", "z_ready", "lmean", "lcent", "lsq", "lvar", "lstd",
            "rt_ready", "rt_done", "gexp_in", "gexp", "assign", "ranks", "slots", "lists", "pw_ready", "xg_ready",
            "cw_ready", "gu_ready", "sg_ready", "hid_ready", "dn_ready", "ya_done", "yd_done", "ysl_ready",
            "rows_ready", "rows_sb", "exp_in", "exp_out", "colps", "colsb", "y_out", "m_out", "fin_m", 
            "dve_step", "act_step", "pool_step", "heads_done", "ext_used", "layer_done", "wgt_in", "wgate_in", "ring_back")}
        out_state = [sem(f"out_state{b}") for b in range(2)]
        used = [sem(f"used{j}") for j in range(3)]
        landed = [[sem(f"landed{u}_{j}") for j in range(3)] for u in range(G)]
        X = [{n: sem(f"x{n}{l}") for n in ("land", "gu", "sg", "hid", "dn", "ya", "yd")} for l in range(DEPTH)]

        SMALL = [(cT[:, :, :], A["cT"]), (modb[:, :, :], A["modb"]), (lng[:, :, :], A["lng"]), (lnb[:, :, :], A["lnb"]),
                 (hng[:, :, :], A["hng"]), (posr[:, :, :], A["posr"]), (posc[:, :, :], A["posc"]),
                 (wglr[:, :, :], A["wglr"]), (bgate[:, :], A["bgate"]), (wrt[:, :, :, :], A["wrt"]), (brt[:, :, :], A["brt"]),
                 (n0[:, :], A["n0"]), (m0[:, :], A["m0"]), (bgt[:, :], A["bgt"])]
        N_SMALL = 16 * len(SMALL)
        N_CONST = 18

        PJ_HEAD = 2 + NT + MV
        N_PJ_L0 = 1 + 2 * H + H * PJ_HEAD + KD + 2 * NT + 2 * KD + SC + 2 * SC + KD
        N_PJ_L1 = [N_PJ_L0 + 1 + PJ_HEAD * min(h + 2, H) + 6 * h for h in range(H)]
        block = ctx.enter_context(nc.Block())

        @block.sync
        def _(sp):
            sp.dma_start(xT[:, :, :], A["xT"]).then_inc(S["x_in"], 16)
            sp.dma_start(st0[:, :, :], A["st_gla"]).then_inc(S["state_in"], 16)

            def load(g, src, widths=(PIECE,) * 3):
                u = g[1]
                for j in range(3):
                    if not is_neg(g[0] - G):
                        sp.wait_ge(used[j], g[0] - G + 1)
                    sp.dma_start(ring[:, u, j, 0:widths[j]], src(j)).then_inc(landed[u][j], 16)

            for l in range(DEPTH):
                g0 = l * G_LAYER

                def mod_group(i, u):
                    g = g0 + G * i + u
                    load((g, u), lambda j: A["w_mod"][bass.ds((l * G_MOD + G * i + u) * 3 + j, 1)].rearrange("a p n -> p (a n)"))

                for u in range(G):
                    mod_group(0, u)
                with sp.Fori(1, G_MOD // G) as i:
                    for u in range(G):
                        mod_group(i, u)
                g0 += G_MOD
                for h in range(H):
                    load((g0 + h, h % G), lambda j: A["w_in"][(l * H + h) * 3 + j])
                g0 += G_HEAD
                for q in range(G_OUT):
                    at = (0, OUT_W[0] * KD, (OUT_W[0] + OUT_W[1]) * KD)
                    load((g0 + q, q % G), lambda j: A["w_out"][l * G_OUT + q, :, at[j]:at[j] + OUT_W[j] * KD],
                         [w * KD for w in OUT_W])
                g0 += G_OUT
                if l == 0:
                    sp.wait_ge(S["heads_done"], 1)
                    sp.dma_start(st0[:, :, :], A["st_ml"]).then_inc(S["state_in"], 16)
                with sp.Fori(0, NE // G) as i:
                    for u in range(G):
                        load((g0 + G * i + u, u),
                             lambda j: A["w_moe"][bass.ds((l * NE + G * i + u) * 3 + j, 1)].rearrange("a p n -> p (a n)"))
                sp.wait_ge(S["lists"], l + 1)
                n_ext = sp.value_load(xlisti[0:1, 2 * MAXJ:2 * MAXJ + 1], min_val=0, max_val=MAXJ)
                with sp.If(n_ext > 0):
                    for j in range(3):
                        sp.wait_ge(used[j], (l + 1) * G_LAYER)
                    with sp.Fori(0, n_ext) as i:
                        e = sp.value_load(xlisti[0:1, bass.ds(i, 1)], min_val=0, max_val=NE - 1)
                        for j in range(3):
                            sp.dma_start(ring[:, 0, j, :],
                                         A["w_moe"][bass.ds((e + l * NE) * 3 + j, 1)].rearrange("a p n -> p (a n)"))\
                              .then_inc(X[l]["land"], 16)
                        sp.wait_ge(X[l]["dn"], i + 1)
                        sp.sem_inc(S["ring_back"], 1)
            sp.wait_ge(S["layer_done"], DEPTH)
            sp.dma_start(O["y"], xT[:, :, :]).then_inc(S["y_out"], 16)
            sp.wait_ge(S["y_out"], 16)

        @block.gpsimd
        def _(pool):
            steps = [0]

            def own(ins):
                steps[0] += 1
                ins.then_inc(S["pool_step"], 1)
                pool.wait_ge(S["pool_step"], steps[0])

            ready = lambda ins: ins.then_inc(S["consts"], 1)
            ready(pool.memset(ones_d[:, :], 1.0 / D))
            ready(pool.memset(ones_v[:, :], 1.0 / DV))
            ready(pool.memset(ones[:, :], 1.0))
            ready(pool.memset(onesb[:, :], 1.0))
            ready(pool.memset(epst[:, :], EPS))
            ready(pool.memset(onet[:, :], 1.0))
            own(pool.memset(wgate[:, :, :], 0.0))
            pool.dma_start(wgate[0:RANK, 0, :], A["wgate"][0]).then_inc(S["wgate_in"], 16)
            pool.dma_start(wgate[RANK:2 * RANK, 1, :], A["wgate"][1]).then_inc(S["wgate_in"], 16)
            own(pool.memset(ident[:, :], 0.0))
            ready(pool.affine_select(out=ident[:, :], in_=ident[:, :], compare_op=ALU.not_equal, fill=1.0,
                                     base=0, pattern=[[-1, P]], channel_multiplier=1))
            own(pool.memset(trib[:, :], 1.0))
            ready(pool.affine_select(out=trib[:, :], in_=trib[:, :], compare_op=ALU.is_gt, fill=0.0,
                                     base=0, pattern=[[1, P]], channel_multiplier=-1))
            own(pool.memset(rowsel[:, :, :], 0.0))
            ready(pool.affine_select(out=rowsel[:, :, :], in_=rowsel[:, :, :], compare_op=ALU.not_equal, fill=1.0,
                                     base=0, pattern=[[-1, H], [0, P]], channel_multiplier=1))
            own(pool.memset(causal[:, :, :, :], 1.0))
            own(pool.affine_select(out=causal[:, 0], in_=causal[:, 0], compare_op=ALU.is_ge, fill=0.0,
                                   base=0, pattern=[[0, NT], [1, P]], channel_multiplier=-1))
            own(pool.affine_select(out=causal[:, 1], in_=causal[:, 1], compare_op=ALU.is_ge, fill=0.0,
                                   base=0, pattern=[[0, NT], [-1, P]], channel_multiplier=1))
            ready(pool.affine_select(out=causal[:, 0, :, CH:P], in_=causal[:, 0, :, CH:P], compare_op=ALU.is_ge, fill=0.0,
                                     base=-CH, pattern=[[0, NT], [0, CH]], channel_multiplier=1))
            ready(pool.affine_select(out=causal[:, 1, :, 0:CH], in_=causal[:, 1, :, 0:CH], compare_op=ALU.is_ge, fill=0.0,
                                     base=CH - 1, pattern=[[0, NT], [0, CH]], channel_multiplier=-1))
            own(pool.memset(keep[:, :], 1.0))
            ready(pool.memset(keep[:, 0:N:CH], 0.0))
            own(pool.memset(fresh[:, :], 0.0))
            ready(pool.memset(fresh[:, 0:N:CH], -BIG))
            own(pool.iota(slot_i[:, :], pattern=[[1, NS]], base=0, channel_multiplier=0))
            ready(pool.tensor_copy(slot_f[:, :], slot_i[:, :]))
            for k in range(EPG):
                ins = pool.memset(ramp[:, k:k + 1], float(EPG - k))
            ready(ins)
            for j in range(MAXJ):
                ins = pool.memset(jcap[:, j, :], float(CAP * (j + 1)))
            ready(ins)
            for e in range(NE):
                ins = pool.memset(eidx[:, :, e:e + 1], float(e))
            ready(ins)
            ready(pool.memset(am[:, :, :], 0.0))

            for l in range(DEPTH):
                for h in range(H):
                    pool.wait_ge(S["fin_state"], l * H + h + 1)
                    for d in range(2):
                        dst = (O["new_S"] if l == 0 else O["new_C"])[d, h]
                        pool.dma_start(dst, sfin[:, h % 2, d, :]).then_inc(out_state[h % 2], 16)
                if l == 0:
                    pool.wait_ge(S["layer_done"], 1)
                    own(pool.memset(wgt, 0.0))
                    for y in range(4):
                        pool.dma_start(wgt[:, :, 32 * y:32 * y + H], A["wgt"][y]).then_inc(S["wgt_in"], 16)
            pool.wait_ge(S["fin_m"], 1)
            pool.dma_start(O["new_n"], nfin[:, :]).then_inc(S["m_out"], 16)
            pool.dma_start(O["new_m"], mfin[:, :]).then_inc(S["m_out"], 16)
            pool.wait_ge(S["m_out"], 32)
            for b in range(2):
                pool.wait_ge(out_state[b], 16 * DEPTH * H)

        @block.tensor
        def _(pe):
            n_pj = [0]

            def pj():
                n = n_pj[0]
                n_pj[0] += 1
                if n >= 2:
                    pe.wait_ge(S["pj_free"], n - 1)
                return bank[n % 2]

            read_pieces = []

            def mm(out, lhsT, rhs, start, stop):
                ins = pe.matmul(out, lhsT, rhs, start=start, stop=stop, skip_group_check=True)
                if read_pieces and start and not stop:
                    ins.then_inc(used[read_pieces.pop()], 1)
                return ins

            n_ds = [0]

            def piece(l, g, j):
                gg = l * G_LAYER + g
                pe.wait_ge(landed[gg % G][j], 16 * (gg // G + 1))
                return ring[:, gg % G, j, :]

            def modulation(l):
                with pe.Fori(0, G_MOD // G) as i:
                    for u in range(G):
                        for j in range(3):
                            pe.wait_ge(landed[u][j], (i + (l * G_LAYER // G + 1)) * 16)
                            w = ring[:, u, j, :].rearrange("p (k n) -> p k n", k=KD)
                            for m in range(2):
                                col = (i * G + u) * 12 + j * 4 + m * 2
                                for k in range(KD):
                                    ins = mm(bank[7][:, bass.ds(col, 2)], w[:, k, m * P:(m + 1) * P], scT[:, k, :],
                                             k == 0, k == KD - 1)
                            ins.then_inc(used[j], 1)

            def project_qkv(l, h):
                g = G_MOD + h
                w = piece(l, g, 0).rearrange("p (k n) -> p k n", k=KD)
                for c in range(2):
                    b = pj()
                    for k in range(KD):
                        ins = mm(b[:, 0:N], w[:, k, c * P:(c + 1) * P], hT[:, k, :], k == 0, k == KD - 1)
                    ins.then_inc(S["pj_ready"], 1)
                read_pieces.append(0)
                w = piece(l, g, 1).rearrange("p (k n) -> p k n", k=KD)
                for t in range(NT):
                    b = pj()
                    for k in range(KD):
                        ins = mm(b[:, 0:DV], hT[:, k, t * P:(t + 1) * P], w[:, k, :], k == 0, k == KD - 1)
                    ins.then_inc(S["pj_ready"], 1)
                read_pieces.append(1)

            def project_r(l, h):
                g = G_MOD + h
                w = piece(l, g, 2).rearrange("p (k n) -> p k n", k=KD)
                for c in range(2):
                    b = pj()
                    for k in range(KD):
                        ins = mm(b[:, 0:N], w[:, k, c * P:(c + 1) * P], hT[:, k, :], k == 0, k == KD - 1)
                    ins.then_inc(S["pj_ready"], 1)
                read_pieces.append(2)

            n_mean = [0]

            def head_mean(l, h):
                n = l * H + h
                pe.wait_ge(S["num_sb"], n + 1)
                for m in range(MV):
                    ins = mm(bank[4][:, 0:N], ones_v[:, :], num[:, m, :], m == 0, m == MV - 1)
                ins.then_inc(S["mean_ready"], 1)

            def head_var(l, h):
                n = l * H + h
                pe.wait_ge(S["sq_ready"], n + 1)
                for m in range(MV):
                    ins = mm(bank[4][:, 0:N], ones_v[:, :], nsq[:, m, :], m == 0, m == MV - 1)
                ins.then_inc(S["var_ready"], 1)

            def attend_gla(h):
                b = h % 2
                places = state_places(0)
                if h >= 1:
                    pe.wait_ge(S["state_ready"], N_STATES * h)
                pe.wait_ge(S["heads_in"], h + 1)
                pe.wait_ge(S["scaled"], h + 1)
                for d in range(2):
                    if d + 2 * h >= 1:
                        pe.wait_ge(S["kt_sb"], 2 * h + d)
                    for t in range(NT):
                        ins = pe.transpose(bank[7][:, t * P:(t + 1) * P], eb[:, d * H + h, t * P:(t + 1) * P], ident[:, :])
                    ins.then_inc(S["kt_ready"], 1)
                for d in range(2):
                    if 2 * h + d >= 1:
                        pe.wait_ge(S["am_ready"], 2 * h + d)
                    for t in range(NT):
                        c = slice(t * P, (t + 1) * P)
                        ins = mm(bank[5][:, c], ec[:, d * H + h, c], ea[:, d * H + h, c], True, True)
                    ins.then_inc(S["sc_ready"], 1)
                if h >= 1:
                    pe.wait_ge(S["num_sb"], h)
                pe.wait_ge(S["am_ready"], 2 * h + 2)
                for m in range(MV):
                    for t in range(NT):
                        c = slice(t * P, (t + 1) * P)
                        for d in range(2):
                            mm(bank[2 + m][:, c], vt[:, b, t, m * P:(m + 1) * P], am[:, d, c], t == 0 and d == 0, False)
                pe.wait_ge(S["kt_sb"], 2 * h + 2)
                pe.wait_ge(S["state_in"], 16)
                made = {}
                steps = chain_steps((0, 1))
                for x, (lat, d, s, n, more) in enumerate(steps):
                    c = slice(n * CH, (n + 1) * CH)
                    if s > 0:
                        pe.wait_ge(S["state_ready"], made[lat, d, s - 1])
                    if s > 0 or lat:
                        src = st0[:, d * H + h, :] if s == 0 else st[:, 2 * lat + d, s % 2, :]
                        for m in range(MV):
                            ins = mm(bank[2 + m][:, c], src[:, m * P:(m + 1) * P], ed[:, d * H + h, c], False, x == len(steps) - 1)
                    if more:
                        bk, taken_by = places[n_ds[0] - N_STATES * h]
                        if taken_by is not None:
                            pe.wait_ge(S["state_ready"], N_STATES * h + taken_by + 1)
                        q = slice((n % 2) * CH, (n % 2 + 1) * CH)
                        mm(bank[bk][:, 0:DV], ktok[q, d, n // 2, :], vt[q, b, n // 2, :],
                           True, True).then_inc(S["ds_ready"], 1)
                        n_ds[0] += 1
                        made[lat, d, s] = n_ds[0]
                    if x == len(steps) - 1:
                        ins.then_inc(S["num_ready"], 1)

            def attend_mlstm(h):
                b = h % 2
                places = state_places(1)
                pe.wait_ge(S["state_ready"], N_STATES * (H + h))
                pe.wait_ge(S["heads_in"], H + h + 1)
                if h >= 1:
                    pe.wait_ge(S["kt_sb"], 2 * H + h)
                    pe.wait_ge(S["am_ready"], 2 * H + 2 * h)
                for t in range(NT):
                    ins = pe.transpose(bank[7][:, t * P:(t + 1) * P], kT[:, b, t * P:(t + 1) * P], ident[:, :])
                ins.then_inc(S["kt_ready"], 1)
                for t in range(NT):
                    c = slice(t * P, (t + 1) * P)
                    ins = mm(bank[5][:, c], kT[:, b, c], qT[:, b, c], True, True)
                ins.then_inc(S["sc_ready"], 1)
                for d in range(2):
                    for r in (wrow, einr, mir):
                        o = pj()
                        mm(o[:, 0:N], rowsel[:, h, :], r[0:H, d, :], True, True).then_inc(S["pj_ready"], 1)
                pe.wait_ge(S["kt_sb"], 2 * H + h + 1)
                pe.wait_ge(S["state_in"], 32)
                for d in range(2):
                    e = 2 * h + d
                    pe.wait_ge(S["am_ready"], 2 * H + e + 1)
                    if e >= 1:
                        pe.wait_ge(S["den_free"], e)
                    for m in range(MV):
                        for t in range(NT):
                            c = slice(t * P, (t + 1) * P)
                            mm(bank[2 + m][:, c], vt[:, b, t, m * P:(m + 1) * P], am[:, d, c], t == 0, False)
                    mm(bank[4][:, 0:N], ones[:, :], am[:, d, :], True, False)
                    steps = chain_steps((d,))
                    made = {}
                    for x, (lat, d, s, n, more) in enumerate(steps):
                        c = slice(n * CH, (n + 1) * CH)
                        if s > 0:
                            pe.wait_ge(S["state_ready"], made[lat, d, s - 1])
                        if s > 0 or lat:
                            src = st0[:, d * H + h, :] if s == 0 else st[:, 2 * lat + d, s % 2, :]
                            nsrc = nb0 if s == 0 else nb[:, lat, s % 2, :]
                            for m in range(MV):
                                mm(bank[2 + m][:, c], src[:, m * P:(m + 1) * P], qe[:, d, c], False, x == len(steps) - 1)
                            ins = mm(bank[4][:, c], nsrc, qe[:, d, c], False, x == len(steps) - 1)
                        if more:
                            bk, taken_by = places[n_ds[0] - N_STATES * (H + h)]
                            if taken_by is not None:
                                pe.wait_ge(S["state_ready"], N_STATES * (H + h) + taken_by + 1)
                            q = slice((n % 2) * CH, (n % 2 + 1) * CH)
                            kw = ktok[q, d, n // 2, :]
                            mm(bank[bk][:, DV:DV + 1], kw, ones[q, 0:1], True, True)
                            mm(bank[bk][:, 0:DV], kw, vt[q, b, n // 2, :],
                               True, True).then_inc(S["ds_ready"], 1)
                            n_ds[0] += 1
                            made[lat, d, s] = n_ds[0]
                        if x == len(steps) - 1:
                            ins.then_inc(S["num_ready"], 1)

            def out_projection(l):
                pe.wait_ge(S["o_ready"], (l + 1) * H)
                for q in range(G_OUT):
                    for j in range(3):
                        w = piece(l, G_MOD + G_HEAD + q, j)[:, 0:OUT_W[j] * KD].rearrange("p (k n) -> p k n", k=KD)
                        for c in range(OUT_W[j] // P):
                            b = pj()
                            for k in range(KD):
                                ins = mm(b[:, 0:N], w[:, k, c * P:(c + 1) * P], oT[:, k, :], k == 0, k == KD - 1)
                            ins.then_inc(S["pj_ready"], 1)
                        read_pieces.append(j)

            def layer_norm(x):
                for k in range(KD):
                    pe.wait_ge(S["z_ready"], x * KD + k + 1)
                    ins = mm(bank[4][:, 0:N], ones_d[:, :], zT[:, k, :], k == 0, k == KD - 1)
                ins.then_inc(S["lmean"], 1)
                for k in range(KD):
                    pe.wait_ge(S["lsq"], x * KD + k + 1)
                    ins = mm(bank[5][:, 0:N], ones_d[:, :], hT[:, k, :], k == 0, k == KD - 1)
                ins.then_inc(S["lvar"], 1)

            def route(l):
                pe.wait_ge(S["h_ready"], 2 * l + 2)
                w = NGRP + NE
                for t in range(NT):
                    c = slice(t * w, (t + 1) * w)
                    mm(bank[4][:, c], ones[0:1, :], brt[0:1, l, :], True, False)
                    for k in range(KD):
                        ins = mm(bank[4][:, c], hT[:, k, t * P:(t + 1) * P], wrt[:, l, k, :], False, k == KD - 1)
                ins.then_inc(S["rt_ready"], 1)
                for t in range(NT):
                    for q in range(2):
                        b = pj()
                        for k in range(4):
                            ins = pe.transpose(b[:, k * P:(k + 1) * P], hT[:, 4 * q + k, t * P:(t + 1) * P], ident[:, :])
                        ins.then_inc(S["pj_ready"], 1)
                pe.wait_ge(S["assign"], l + 1)
                for t in range(NT):
                    for s in range(t + 1):
                        mm(bank[5][:, t * NE:(t + 1) * NE], (trib if s == t else onesb)[:, :], mb[:, s, :], s == 0, s == t)
                for s in range(NT):
                    ins = mm(bank[5][:, NT * NE:(NT + 1) * NE], onesb[:, :], mb[:, s, :], s == 0, s == NT - 1)
                ins.then_inc(S["ranks"], 1)

            def gather(l):
                pe.wait_ge(S["slots"], l + 1)
                for k in range(KD):
                    for q in range(2):
                        b = pj()
                        for t in range(NT):
                            ins = mm(b[:, 0:N], htok[:, t, k * P:(k + 1) * P], sel[:, t, q * N:(q + 1) * N], t == 0, t == NT - 1)
                        ins.then_inc(S["pj_ready"], 1)
                pe.wait_ge(S["pw_ready"], l + 1)
                for c in range(SC):
                    b = pj()
                    for t in range(NT):
                        ins = pe.transpose(b[:, t * P:(t + 1) * P], pw[:, t, c * P:(c + 1) * P], ident[:, :])
                    ins.then_inc(S["pj_ready"], 1)

            def gate_up(l, u, off, out, sig):
                for j in range(2):
                    w = ring[:, u, j, :].rearrange("p (k n) -> p k n", k=KD)
                    for f in range(FE):
                        for k in range(KD):
                            ins = mm(out[:, (j * FE + f) * CAP:(j * FE + f + 1) * CAP], w[:, k, f * P:(f + 1) * P],
                                     xg[:, k, bass.ds(off, CAP)], k == 0, k == KD - 1)
                    if j == 0 and sig is None:
                        ins.then_inc(used[0], 1)
                return ins

            def down(u, hb, b0, b1):
                w = ring[:, u, 2, :].rearrange("p (k n) -> p k n", k=FE)
                for k in range(KD):
                    o = (b0 if k < 4 else b1)[:, (k % 4) * CAP:(k % 4 + 1) * CAP]
                    for f in range(FE):
                        ins = mm(o, w[:, f, k * P:(k + 1) * P], hid[:, hb, f, :], f == 0, f == FE - 1)
                return ins

            def experts(l):
                g0 = l * G_LAYER + G_MOD + G_HEAD + G_OUT
                e0 = l * NE

                def up_step(e, u, turn):
                    off = pe.value_load(offi[0:1, bass.ds(e, 1)], min_val=0, max_val=NS)
                    for j in range(2):
                        pe.wait_ge(landed[u][j], turn * 16 + 16 * (g0 // G + 1))
                    if not (isinstance(e, int) and e0 + e < 2):
                        pe.wait_ge(S["hid_ready"], e + (e0 - 1))
                    ins = gate_up(l, u, off, bank[2 + u], None)
                    ins.then_inc(S["gu_ready"], 1)
                    return ins

                def down_step(e, u, turn):
                    pe.wait_ge(landed[u][2], turn * 16 + 16 * (g0 // G + 1))
                    pe.wait_ge(S["hid_ready"], e + (e0 + 1))
                    pe.sem_inc(used[1], 1)
                    if not (isinstance(e, int) and e0 + e < 2):
                        pe.wait_ge(S["ya_done"], e + (e0 - 1))
                        pe.wait_ge(S["yd_done"], e + (e0 - 1))
                    down(u, u, bank[4 + 2 * u], bank[5 + 2 * u]).then_inc(S["dn_ready"], 1)
                    read_pieces.append(2)

                pe.wait_ge(S["xg_ready"], l + 1)
                up_step(0, 0, 0)
                up_step(1, 1, 0)
                down_step(0, 0, 0)
                with pe.Fori(1, NE // G) as i:
                    up_step(i * 2, 0, i)
                    down_step(i * 2 - 1, 1, i - 1)
                    up_step(i * 2 + 1, 1, i)
                    down_step(i * 2, 0, i)
                down_step(NE - 1, 1, NE // G - 1)
                pe.wait_ge(S["dn_ready"], (l + 1) * NE)
                pe.sem_inc(used[read_pieces.pop()], 1)
                pe.wait_ge(S["lists"], l + 1)

                n_ext = pe.value_load(xlisti[0:1, 2 * MAXJ:2 * MAXJ + 1], min_val=0, max_val=MAXJ)
                with pe.If(n_ext > 0):
                    with pe.Fori(0, n_ext) as i:
                        off = pe.value_load(xlisti[0:1, bass.ds(i + MAXJ, 1)], min_val=0, max_val=NS)
                        pe.wait_ge(X[l]["land"], i * 48 + 48)
                        gate_up(l, 0, off, bank[2], X[l]["gu"]).then_inc(X[l]["gu"], 1)
                        pe.wait_ge(X[l]["hid"], i + 1)
                        down(0, 0, bank[4], bank[5]).then_inc(X[l]["dn"], 1)
                        pe.wait_ge(X[l]["ya"], i + 1)
                        pe.wait_ge(X[l]["yd"], i + 1)

            def combine(l):
                pe.wait_ge(S["ya_done"], (l + 1) * NE)
                pe.wait_ge(S["yd_done"], (l + 1) * NE)
                pe.wait_ge(S["cw_ready"], l + 1)
                for c in range(SC):
                    for q in range(2):
                        b = pj()
                        for k in range(4):
                            ins = pe.transpose(b[:, k * P:(k + 1) * P], yg[:, 4 * q + k, c * P:(c + 1) * P], ident[:, :])
                        ins.then_inc(S["pj_ready"], 1)
                pe.wait_ge(S["ysl_ready"], l + 1)
                for k in range(KD):
                    b = pj()
                    for c in range(SC):
                        ins = mm(b[:, 0:N], ysl[:, c, k * P:(k + 1) * P], cw[:, c, :], c == 0, c == SC - 1)
                    ins.then_inc(S["pj_ready"], 1)

            pe.wait_ge(S["consts"], N_CONST)
            pe.wait_ge(S["small_in"], N_SMALL)
            pe.wait_ge(S["silu_c"], 1)
            for l in range(DEPTH):
                modulation(l)
                pe.wait_ge(S["h_ready"], 2 * l + 1)
                if l == 0:
                    b = pj()
                    for k in range(KD):
                        ins = mm(b[0:2 * RANK, 0:N], wglr[:, k, :], hT[:, k, :], k == 0, k == KD - 1)
                    ins.then_inc(S["pj_ready"], 1)
                    pe.wait_ge(S["gates_in"], 1)
                    pe.wait_ge(S["wgate_in"], 32)
                    for d in range(2):
                        for h in range(H):
                            b = pj()
                            mm(b[:, 0:N], wgate[:, d, h * DK:(h + 1) * DK], num[0:2 * RANK, 0, :], True, True)\
                                .then_inc(S["pj_ready"], 1)
                else:
                    pe.wait_ge(S["wgt_in"], 64)
                    b = pj()
                    for k in range(KD):
                        ins = mm(b[:, 0:N], wgt[:, k, :], hT[:, k, :], k == 0, k == KD - 1)
                    ins.then_inc(S["pj_ready"], 1)
                project_qkv(l, 0)
                project_r(l, 0)
                if l == 1:
                    pe.wait_ge(S["rows_ready"], 1)
                    for y, r in enumerate((urow, ulr)):
                        for d in range(2):
                            for t in range(NT):
                                i = (y * 2 + d) * NT + t
                                pe.transpose(bank[7][:, i * H:(i + 1) * H], r[0:H, d, t * P:(t + 1) * P], ident[0:H, 0:H])
                    for h in range(H):
                        ins = mm(bank[7][:, 64 + h * 2 * NCH:64 + (h + 1) * 2 * NCH], rowsel[:, h, :],
                                 decr[:, :, :].rearrange("p a b -> p (a b)"), True, True)
                    ins.then_inc(S["colps"], 1)
                    pe.wait_ge(S["colsb"], 1)
                for h in range(H):
                    if h + 1 < H:
                        project_qkv(l, h + 1)
                    if h >= 1:
                        head_var(l, h - 1)
                    if h + 1 < H:
                        project_r(l, h + 1)
                    if h >= 1:
                        pe.wait_ge(S["std_ready"], l * H + h)
                    (attend_gla if l == 0 else attend_mlstm)(h)
                    head_mean(l, h)
                head_var(l, H - 1)
                pe.wait_ge(S["num_ready"], H if l == 0 else 3 * H)
                pe.sem_inc(S["heads_done"], 1)
                out_projection(l)
                layer_norm(2 * l)
                route(l)
                gather(l)
                experts(l)
                combine(l)
                layer_norm(2 * l + 1)

        @block.scalar
        def _(act):
            for dst, src in SMALL:
                act.dma_start(dst, src).then_inc(S["small_in"], 16)
            steps = [0]
            n_pj = [0]

            def own(ins):
                steps[0] += 1
                ins.then_inc(S["act_step"], 1)
                act.wait_ge(S["act_step"], steps[0])

            def f(out, in_, func, **kw):
                return act.activation(out, in_, func, **kw)

            def pj():
                n_pj[0] += 1
                act.wait_ge(S["pj_ready"], n_pj[0])
                return bank[(n_pj[0] - 1) % 2]

            def free(ins):
                ins.then_inc(S["pj_free"], 1)

            def project_qkv(l, h):
                b = h % 2
                if h >= 2:
                    act.wait_ge(S["num_sb"], l * H + h - 1)
                free(f(qT[:, b, :], pj()[:, 0:N], ACT.Copy, scale=float(DK) ** -0.5))
                free(f(kT[:, b, :], pj()[:, 0:N], ACT.Copy))
                for t in range(NT):
                    free(f(vt[:, b, t, :], pj()[:, 0:DV], ACT.Copy))
                act.wait_ge(S["pj_free"], n_pj[0])
                act.sem_inc(S["heads_in"], 1)

            def project_r(l, h):
                if h >= 2:
                    act.wait_ge(S["o_ready"], l * H + h - 1)
                for m in range(MV):
                    free(f(rT[:, h % 2, m, :], pj()[:, 0:N], ACT.Silu if l == 0 else ACT.Sigmoid))

            def head_square(l, h):
                act.wait_ge(S["cent"], l * H + h + 1)
                f(nsq[:, :, :], num[:, :, :], ACT.Square).then_inc(S["sq_ready"], 1)

            def head_std(l, h):
                act.wait_ge(S["var_ready"], l * H + h + 1)
                if l * H + h >= 1:
                    act.wait_ge(S["o_ready"], l * H + h)
                f(rs, bank[4][:, 0:N], ACT.Sqrt, bias=epst[:, 0:1]).then_inc(S["std_ready"], 1)

            def attend_gla(h):
                for d in range(2):
                    act.wait_ge(S["kt_ready"], 2 * h + d + 1)
                    if h >= 1:
                        act.wait_ge(S["ds_ready"], N_STATES * h)
                    f(ktok[:, d, :, :], bank[7][:, 0:N], ACT.Copy).then_inc(S["kt_sb"], 1)
                act.wait_ge(S["num_ready"], h + 1)
                if h >= 1:
                    act.wait_ge(S["o_ready"], h)
                for m in range(MV):
                    ins = f(num[:, m, :], bank[2 + m][:, 0:N], ACT.Copy)
                ins.then_inc(S["num_sb"], 1)

            def attend_mlstm(h):
                b = h % 2
                act.wait_ge(S["kt_ready"], 2 * H + h + 1)
                if h >= 1:
                    act.wait_ge(S["ds_ready"], N_STATES * (H + h))
                for d in range(2):
                    for t in range(NT):
                        ins = f(ktok[:, d, t, :], bank[7][:, t * P:(t + 1) * P], ACT.Copy,
                                scale=cols[:, (2 + d) * NT + t, h:h + 1])
                ins.then_inc(S["kt_sb"], 1)
                for d in range(2):
                    e = 2 * h + d
                    if e >= 1:
                        act.wait_ge(S["am_ready"], 2 * H + e)
                    o = pj()
                    for t in range(NT):
                        ins = f(expd[:, t * P:(t + 1) * P], o[:, t * P:(t + 1) * P], ACT.Exp, scale=-1.0,
                                bias=cols[:, d * NT + t, h:h + 1])
                    free(ins)
                    if e >= 2:
                        act.wait_ge(S["ext_used"], e - 1)
                    free(f(einb[:, d, :], pj()[:, 0:N], ACT.Copy))
                    if e >= 1:
                        act.wait_ge(S["den_free"], e)
                    free(f(emt, pj()[:, 0:N], ACT.Copy))

            def normalise(x):
                for k in range(KD):
                    act.wait_ge(S["lcent"], x * KD + k + 1)
                    f(hT[:, k, :], zT[:, k, :], ACT.Square).then_inc(S["lsq"], 1)
                act.wait_ge(S["lvar"], x + 1)
                f(rs, bank[5][:, 0:N], ACT.Sqrt, bias=epst[:, 0:1]).then_inc(S["lstd"], 1)

            def scaled_by_gate(l, x, p):
                act.wait_ge(S["mod_ready"], l + 1)
                for k in range(KD):
                    b = pj()
                    for s, a, z in STREAMS:
                        ins = f(zT[:, k, a:z], b[:, a:z], ACT.Copy, scale=mod[:, l, p * KD + k, s:s + 1])
                    ins.then_inc(S["pj_free"], 1)
                    act.wait_ge(S["pj_free"], n_pj[0])
                    act.sem_inc(S["yscaled"], 1)

            act.wait_ge(S["small_in"], N_SMALL)
            act.wait_ge(S["consts"], N_CONST)
            f(scT[:, :, :], cT[:, :, :], ACT.Silu).then_inc(S["silu_c"], 1)
            for l in range(DEPTH):
                if l == 0:
                    free(f(num[0:2 * RANK, 0, :], pj()[0:2 * RANK, 0:N], ACT.Copy))
                    act.wait_ge(S["pj_free"], n_pj[0])
                    act.sem_inc(S["gates_in"], 1)
                    for i in range(2 * H):
                        free(f(ea[:, i, :], pj()[:, 0:N], ACT.Identity, bias=bgate[:, i:i + 1]))
                    act.wait_ge(S["pj_free"], n_pj[0])
                    act.sem_inc(S["logit_sb"], 1)
                    own(f(eb, ea, ACT.Abs))
                    own(f(eb, eb, ACT.Exp, scale=-1.0))
                    f(eb, eb, ACT.Ln, bias=onet[:, 0:1]).then_inc(S["gate_sp"], 1)
                    project_qkv(l, 0)
                    project_r(l, 0)
                    act.wait_ge(S["gate_d"], 1)
                    f(ec[:, :, :], ea, ACT.Exp, scale=-1.0 / TAU).then_inc(S["e_ready"], 1)
                    f(eb, eb, ACT.Exp, scale=-1.0 / TAU).then_inc(S["e_ready"], 1)
                    f(ed, ed, ACT.Exp, scale=1.0 / TAU).then_inc(S["e_ready"], 1)
                    act.wait_ge(S["e_ready"], 1)
                    f(ea, ea, ACT.Exp, scale=1.0 / TAU).then_inc(S["e_ready"], 1)
                else:
                    o = pj()
                    for y in range(4):
                        ins = f(graw[0:H, y, :], o[32 * y:32 * y + H, 0:N], ACT.Copy)
                    free(ins)
                    act.wait_ge(S["exp_in"], 1)
                    for d in range(2):
                        own(f(mir[0:H, d, :], graw[0:H, 1 + 2 * d, :], ACT.Abs))
                    own(f(mir[0:H], mir[0:H], ACT.Exp, scale=-1.0))
                    f(mir[0:H], mir[0:H], ACT.Ln, bias=onet[0:H, 0:1]).then_inc(S["exp_out"], 1)
                    project_qkv(l, 0)
                    project_r(l, 0)
                    act.wait_ge(S["exp_in"], 2)
                    for r in (einr[0:H], ulr[0:H], decr[:, :, :]):
                        ins = f(r, r, ACT.Exp)
                    ins = f(mir[0:H], mir[0:H], ACT.Exp, scale=-1.0)
                    ins.then_inc(S["rows_ready"], 1)
                    act.wait_ge(S["colps"], 1)
                    f(cols[:, :, :], bank[7][:, 0:12 * H], ACT.Copy)
                    f(dec[:, :, :], bank[7][:, 64:64 + 2 * H * NCH], ACT.Copy).then_inc(S["colsb"], 1)
                    act.wait_ge(S["colsb"], 1)
                for h in range(H):
                    if h >= 1:
                        head_square(l, h - 1)
                    if h + 1 < H:
                        project_qkv(l, h + 1)
                    if h >= 1:
                        head_std(l, h - 1)
                    if h + 1 < H:
                        project_r(l, h + 1)
                    (attend_gla if l == 0 else attend_mlstm)(h)
                head_square(l, H - 1)
                head_std(l, H - 1)
                scaled_by_gate(l, 2 * l, 2)
                normalise(2 * l)
                for t in range(NT):
                    for q in range(2):
                        free(f(htok[:, t, q * 512:(q + 1) * 512], pj()[:, :], ACT.Copy))
                act.wait_ge(S["gexp_in"], 2 * l + 1)
                f(gsc[:, :, :], gsc[:, :, :], ACT.Exp).then_inc(S["gexp"], 1)
                act.wait_ge(S["gexp_in"], 2 * l + 2)
                f(R["dd"][:, :], R["dd"][:, :], ACT.Exp).then_inc(S["gexp"], 1)
                act.wait_ge(S["slots"], l + 1)
                for k in range(KD):
                    for q in range(2):
                        free(f(xg[:, k, q * N:(q + 1) * N], pj()[:, 0:N], ACT.Copy))
                act.wait_ge(S["pj_free"], n_pj[0])
                act.sem_inc(S["xg_ready"], 1)
                for c in range(SC):
                    free(f(cw[:, c, :], pj()[:, 0:N], ACT.Copy))
                act.wait_ge(S["pj_free"], n_pj[0])
                act.sem_inc(S["cw_ready"], 1)

                e0 = l * NE

                def gate(e, u):
                    act.wait_ge(S["gu_ready"], e + (e0 + 1))
                    if not (isinstance(e, int) and e0 + e < 2):
                        act.wait_ge(S["hid_ready"], e + (e0 - 1))
                    f(sg[:, u, :, :], bank[2 + u][:, 0:FE * CAP], ACT.Silu).then_inc(S["sg_ready"], 1)

                def keep_y(e, u):
                    off = act.value_load(offi[0:1, bass.ds(e, 1)], min_val=0, max_val=NS)
                    act.wait_ge(S["dn_ready"], e + (e0 + 1))
                    if not (isinstance(e, int) and e0 + e < 1):
                        act.wait_ge(S["ya_done"], e + e0)
                    f(yg[:, 0:4, bass.ds(off, CAP)], bank[4 + 2 * u][:, 0:4 * CAP].rearrange("p (k n) -> p k n", k=4),
                      ACT.Copy).then_inc(S["ya_done"], 1)

                gate(0, 0)
                gate(1, 1)
                keep_y(0, 0)
                with act.Fori(1, NE // G) as i:
                    gate(i * 2, 0)
                    keep_y(i * 2 - 1, 1)
                    gate(i * 2 + 1, 1)
                    keep_y(i * 2, 0)
                keep_y(NE - 1, 1)
                act.wait_ge(S["lists"], l + 1)
                n_ext = act.value_load(xlisti[0:1, 2 * MAXJ:2 * MAXJ + 1], min_val=0, max_val=MAXJ)
                with act.If(n_ext > 0):
                    act.wait_ge(S["ya_done"], e0 + NE)
                    with act.Fori(0, n_ext) as i:
                        off = act.value_load(xlisti[0:1, bass.ds(i + MAXJ, 1)], min_val=0, max_val=NS)
                        act.wait_ge(X[l]["gu"], i + 1)
                        f(sg[:, 0, :, :], bank[2][:, 0:FE * CAP], ACT.Silu).then_inc(X[l]["sg"], 1)
                        act.wait_ge(X[l]["dn"], i + 1)
                        f(yg[:, 0:4, bass.ds(off, CAP)], bank[4][:, 0:4 * CAP].rearrange("p (k n) -> p k n", k=4),
                          ACT.Copy).then_inc(X[l]["ya"], 1)
                        act.wait_ge(X[l]["ya"], i + 1)
                for c in range(SC):
                    for q in range(2):
                        free(f(ysl[:, c, q * 512:(q + 1) * 512], pj()[:, :], ACT.Copy))
                act.wait_ge(S["pj_free"], n_pj[0])
                act.sem_inc(S["ysl_ready"], 1)
                scaled_by_gate(l, 2 * l + 1, 5)
                normalise(2 * l + 1)

        @block.vector
        def _(dve):
            steps = [0]

            def own(ins):
                steps[0] += 1
                ins.then_inc(S["dve_step"], 1)
                dve.wait_ge(S["dve_step"], steps[0])

            def behind(ins):
                steps[0] += 1
                return ins.then_inc(S["dve_step"], 1)

            def catch_up():
                dve.wait_ge(S["dve_step"], steps[0])

            def modulate(l, p):
                for k in range(KD):
                    for s, a, z in STREAMS:
                        ins = dve.tensor_scalar(hT[:, k, a:z], xT[:, k, a:z], mod[:, l, (p + 1) * KD + k, s:s + 1],
                                                mod[:, l, p * KD + k, s:s + 1], ALU.mult, ALU.add)
                ins.then_inc(S["h_ready"], 1)

            def residual(x):
                for k in range(KD):
                    dve.wait_ge(S["yscaled"], x * KD + k + 1)
                    dve.scalar_tensor_tensor(out=zT[:, k, :], in0=xT[:, k, :], scalar=ALPHA, in1=zT[:, k, :],
                                             op0=ALU.mult, op1=ALU.add).then_inc(S["z_ready"], 1)

            def normalise(x):
                dve.wait_ge(S["lmean"], x + 1)
                for k in range(KD):
                    dve.tensor_tensor(zT[:, k, :], zT[:, k, :], bank[4][:, 0:N], ALU.subtract).then_inc(S["lcent"], 1)
                dve.wait_ge(S["lstd"], x + 1)
                own(dve.reciprocal(rs, rs))
                for k in range(KD):
                    behind(dve.tensor_tensor(zT[:, k, :], zT[:, k, :], rs, ALU.mult))
                catch_up()
                for k in range(KD):
                    ins = behind(dve.tensor_scalar(xT[:, k, :], zT[:, k, :], lng[:, x, k:k + 1], lnb[:, x, k:k + 1], ALU.mult, ALU.add))
                catch_up()

            def states(l, h, dirs, n_ds):
                for lat, d, s, n, more in chain_steps(dirs):
                    if not more:
                        continue
                    i = n_ds[0]
                    n_ds[0] += 1
                    dve.wait_ge(S["ds_ready"], i + 1)
                    last = not lat and s == 1
                    new = sfin[:, h % 2, d, :] if last else st[:, 2 * lat + d, (s + 1) % 2, :]
                    old = (st0[:, d * H + h, :] if lat else None) if s == 0 else st[:, 2 * lat + d, s % 2, :]
                    bk, _ = state_places(l)[i - N_STATES * (l * H + h)]
                    up = bank[bk][:, 0:DV]
                    dc = dec[:, d * H + h, n:n + 1] if l == 0 else \
                        dec[:, :, :].rearrange("p a b -> p (a b)")[:, (h * 2 + d) * NCH + n:(h * 2 + d) * NCH + n + 1]
                    if last and l * H + h >= 2:
                        dve.wait_ge(out_state[h % 2], 32 * ((l * H + h) // 2))
                    if l == 1:
                        un = bank[bk][:, DV:DV + 1]
                        nnew = nfin[:, d * H + h:d * H + h + 1] if last else nb[:, lat, (s + 1) % 2, :]
                        nold = (nb0 if lat else None) if s == 0 else nb[:, lat, s % 2, :]
                        if nold is None:
                            behind(dve.tensor_copy(nnew, un.broadcast_to([P, P])))
                        elif last:
                            behind(dve.scalar_tensor_tensor(out=nnew, in0=nold[:, 0:1], scalar=dc, in1=un, op0=ALU.mult, op1=ALU.add))
                        else:
                            behind(dve.scalar_tensor_tensor(out=nnew, in0=nold, scalar=dc, in1=un.broadcast_to([P, P]),
                                                            op0=ALU.mult, op1=ALU.add))
                    if old is None:
                        ins = dve.tensor_copy(new, up)
                    else:
                        ins = dve.scalar_tensor_tensor(out=new, in0=old, scalar=dc, in1=up, op0=ALU.mult, op1=ALU.add)
                    ins.then_inc(S["state_ready"], 1)
                    dve.wait_ge(S["state_ready"], n_ds[0])

            def head_norm(l, h):
                b = h % 2
                if l == 0:
                    dve.wait_ge(S["num_sb"], h + 1)
                dve.wait_ge(S["mean_ready"], l * H + h + 1)
                for m in range(MV):
                    ins = dve.tensor_tensor(num[:, m, :], num[:, m, :], bank[4][:, 0:N], ALU.subtract)
                ins.then_inc(S["cent"], 1)

            def head_scale(l, h):
                b = h % 2
                dve.wait_ge(S["cent"], l * H + h + 1)
                dve.wait_ge(S["std_ready"], l * H + h + 1)
                own(dve.reciprocal(rs, rs))
                for m in range(MV):
                    behind(dve.scalar_tensor_tensor(out=num[:, m, :], in0=num[:, m, :], scalar=hng[:, l, 2 * h + m:2 * h + m + 1],
                                                    in1=rs, op0=ALU.mult, op1=ALU.mult))
                catch_up()
                for m in range(MV):
                    ins = dve.tensor_tensor(oT[:, 2 * h + m, :], num[:, m, :], rT[:, b, m, :], ALU.mult)
                ins.then_inc(S["o_ready"], 1)

            n_ds = [0]
            dve.wait_ge(S["small_in"], N_SMALL)
            dve.wait_ge(S["consts"], N_CONST)
            dve.wait_ge(S["x_in"], 16)
            q = KD // 2
            for k in range(q):
                v = xT[:, k, N_CTX:N].rearrange("p (r c) -> p r c", c=GRID_W)
                behind(dve.tensor_tensor(v, v, posr[:, k, :].unsqueeze(2).broadcast_to([P, N_LAT // GRID_W, GRID_W]), ALU.add))
                v = xT[:, q + k, N_CTX:N].rearrange("p (r c) -> p r c", c=GRID_W)
                behind(dve.tensor_tensor(v, v, posc[:, k:k + 1, :].broadcast_to([P, N_LAT // GRID_W, GRID_W]), ALU.add))
            catch_up()
            for l in range(DEPTH):
                dve.wait_ge(used[2], l * G_LAYER + G_MOD)
                own(dve.tensor_tensor(mod[:, l, :, :], bank[7][:, 0:12 * KD].rearrange("p (a b) -> p a b", b=2),
                                      modb[:, l, :].unsqueeze(2).broadcast_to([P, 6 * KD, 2]), ALU.add))
                behind(dve.tensor_scalar(mod[:, l, KD:2 * KD, :], mod[:, l, KD:2 * KD, :], 1.0, None, ALU.add))
                own(dve.tensor_scalar(mod[:, l, 4 * KD:5 * KD, :], mod[:, l, 4 * KD:5 * KD, :], 1.0, None, ALU.add))
                dve.sem_inc(S["mod_ready"], 1)
                modulate(l, 0)
                if l == 0:
                    dve.wait_ge(S["gate_sp"], 1)
                    own(dve.scalar_tensor_tensor(out=ea, in0=ea, scalar=0.0, in1=eb, op0=ALU.min, op1=ALU.subtract))
                    for d in range(2):
                        for h in range(H):
                            r = slice(None) if d == 0 else slice(None, None, -1)
                            behind(dve.tensor_tensor_scan(ed[:, d * H + h, r], keep[:, :], ea[:, d * H + h, r], 0.0,
                                                          ALU.mult, ALU.add))
                    catch_up()
                    for d in range(2):
                        v = [e[:, d * H:(d + 1) * H, :].rearrange("p a (n c) -> p (a n) c", c=CH) for e in (ea, eb, ed)]
                        ref, last = (CH // 2, CH - 1) if d == 0 else (CH - 1 - CH // 2, 0)
                        for dst, at in ((v[0], ref), (v[1], last)):
                            ins = behind(dve.tensor_tensor(dst, v[2], v[2][:, :, at:at + 1].broadcast_to([P, H * NCH, CH]), ALU.subtract))
                    catch_up()
                    dve.sem_inc(S["gate_d"], 1)
                    dve.wait_ge(S["e_ready"], 4)
                    for d in range(2):
                        last = CH - 1 if d == 0 else 0
                        v = ed[:, d * H:(d + 1) * H, :].rearrange("p a (n c) -> p a n c", c=CH)
                        behind(dve.tensor_copy(dec[:, d * H:(d + 1) * H, :], v[:, :, :, last]))
                    catch_up()
                else:
                    dve.wait_ge(S["pj_free"], N_PJ_L0 + 1)
                    own(dve.tensor_tensor(graw[0:H], graw[0:H], bgt[:, :].unsqueeze(2).broadcast_to([H, 4, N]), ALU.add))
                    dve.sem_inc(S["exp_in"], 1)
                    dve.wait_ge(S["exp_out"], 1)
                    g2 = graw[0:H].rearrange("p (d y) n -> p d y n", y=2)
                    own(dve.scalar_tensor_tensor(out=lf[0:H], in0=g2[:, :, 1, :], scalar=0.0, in1=mir[0:H], op0=ALU.min, op1=ALU.subtract))
                    for d in range(2):
                        r = slice(None) if d == 0 else slice(None, None, -1)
                        behind(dve.tensor_tensor_scan(bcum[0:H, d, r], keep[0:H, :], lf[0:H, d, r], 0.0, ALU.mult, ALU.add))
                    catch_up()
                    own(dve.tensor_tensor(urow[0:H], g2[:, :, 0, :], bcum[0:H], ALU.subtract))
                    for d in range(2):
                        r = slice(None) if d == 0 else slice(None, None, -1)
                        behind(dve.tensor_tensor_scan(wrow[0:H, d, r], fresh[:, :], urow[0:H, d, r], -BIG, ALU.add, ALU.max))
                    behind(dve.memset(mst[:, 0, :, 0], 0.0))
                    behind(dve.tensor_copy(mst[:, 1, :, 0], m0[:, :]))
                    catch_up()
                    for lat, d, s, n, more in chain_steps((0, 1)):
                        c = slice(n * CH, (n + 1) * CH)
                        last = n * CH + (CH - 1 if d == 0 else 0)
                        m = mst[:, lat, d, s:s + 1]
                        own(dve.tensor_scalar(wrow[0:H, d, c], wrow[0:H, d, c], m, None, ALU.max))
                        behind(dve.tensor_tensor(mst[:, lat, d, s + 1:s + 2], wrow[0:H, d, last:last + 1], bcum[0:H, d, last:last + 1], ALU.add))
                        behind(dve.tensor_scalar(einr[0:H, d, c], wrow[0:H, d, c], m, -1.0, ALU.subtract, ALU.mult))
                        behind(dve.tensor_scalar(ulr[0:H, d, c], urow[0:H, d, c], wrow[0:H, d, last:last + 1], None, ALU.subtract))
                        behind(dve.tensor_scalar(decr[:, d, n:n + 1], wrow[0:H, d, last:last + 1], m, -1.0, ALU.subtract, ALU.mult))
                        catch_up()
                    behind(dve.tensor_copy(mfin[:, :], mst[:, 0, :, 2]))
                    own(dve.tensor_tensor(mir[0:H], bcum[0:H], wrow[0:H], ALU.add))
                    dve.sem_inc(S["exp_in"], 1)
                    dve.wait_ge(S["colsb"], 1)

                def scale_gla(h):
                    b = h % 2
                    dve.wait_ge(S["heads_in"], h + 1)
                    for d in range(2):
                        for e, src in ((eb, kT), (ec, kT), (ea, qT), (ed, qT)):
                            ins = dve.tensor_tensor(e[:, d * H + h, :], e[:, d * H + h, :], src[:, b, :], ALU.mult)
                    ins.then_inc(S["scaled"], 1)

                if l == 0:
                    scale_gla(0)
                for h in range(H):
                    b = h % 2
                    if h >= 1:
                        head_norm(l, h - 1)
                    if l == 0:
                        if h >= 1:
                            head_scale(l, h - 1)
                        if h + 1 < H:
                            scale_gla(h + 1)
                        for d in range(2):
                            dve.wait_ge(S["sc_ready"], 2 * h + d + 1)
                            if h >= 1:
                                dve.wait_ge(S["num_ready"], h)
                            dve.copy_predicated(am[:, d, :], causal[:, d, :, :].rearrange("p a b -> p (a b)").bitcast(I32),
                                                bank[5][:, 0:N]).then_inc(S["am_ready"], 1)
                        states(l, h, (0, 1), n_ds)
                        dve.sem_inc(S["fin_state"], 1)
                    else:
                        if h >= 1:
                            head_scale(l, h - 1)
                        dve.wait_ge(S["heads_in"], H + h + 1)
                        dve.wait_ge(S["sc_ready"], 2 * H + h + 1)
                        for d in range(2):
                            e = 2 * h + d
                            base = N_PJ_L1[h] + 3 * d
                            dve.wait_ge(S["pj_free"], base + 1)
                            if e >= 1:
                                dve.wait_ge(S["num_ready"], H + e)
                            own(dve.tensor_tensor(dtmp, expd, bank[5][:, 0:N], ALU.mult))
                            behind(dve.tensor_copy(nb0, n0[:, d * H + h:d * H + h + 1].broadcast_to([P, P])))
                            dve.wait_ge(S["pj_free"], base + 2)
                            dve.tensor_tensor(qe[:, d, :], qT[:, b, :], einb[:, d, :], ALU.mult).then_inc(S["ext_used"], 1)
                            dve.copy_predicated(am[:, d, :], causal[:, d, :, :].rearrange("p a b -> p (a b)").bitcast(I32),
                                                dtmp).then_inc(S["am_ready"], 1)
                            states(l, h, (d,), n_ds)
                            dve.wait_ge(S["num_ready"], H + e + 1)
                            dve.wait_ge(S["pj_free"], base + 3)
                            own(dve.scalar_tensor_tensor(out=rden, in0=bank[4][:, 0:N], scalar=-1.0, in1=emt, op0=ALU.mult, op1=ALU.max))
                            own(dve.tensor_tensor(rden, rden, bank[4][:, 0:N], ALU.max))
                            own(dve.reciprocal(rden, rden))
                            for m in range(MV):
                                dst = num if d == 0 else nsq
                                ins = behind(dve.tensor_tensor(dst[:, m, :], rden, bank[2 + m][:, 0:N], ALU.mult))
                            catch_up()
                            dve.sem_inc(S["den_free"], 1)
                            if d == 1:
                                for m in range(MV):
                                    ins = behind(dve.tensor_tensor(num[:, m, :], num[:, m, :], nsq[:, m, :], ALU.add))
                                catch_up()
                                dve.sem_inc(S["num_sb"], 1)
                        dve.sem_inc(S["fin_state"], 1)
                head_norm(l, H - 1)
                head_scale(l, H - 1)
                if l == 1:
                    dve.sem_inc(S["fin_m"], 1)
                residual(2 * l)
                normalise(2 * l)
                modulate(l, 3)

                def first(onehot, scores, top, pm, w):
                    behind(dve.tensor_reduce(top, scores, AX, ALU.max))
                    catch_up()
                    own(dve.tensor_tensor(onehot, scores, top.unsqueeze(2).broadcast_to([P, NT, w]), ALU.is_equal))
                    own(dve.tensor_tensor(onehot, onehot, ramp[:, EPG - w:EPG].unsqueeze(1).broadcast_to([P, NT, w]), ALU.mult))
                    own(dve.tensor_reduce(pm, onehot, AX, ALU.max))
                    own(dve.tensor_tensor(onehot, onehot, pm.unsqueeze(2).broadcast_to([P, NT, w]), ALU.is_equal))

                for b in range(2):
                    dve.wait_ge(out_state[b], 16 * H * (l + 1))
                dve.wait_ge(S["rt_ready"], l + 1)
                own(dve.tensor_copy(lgt[:, :, :], bank[4][:, 0:NT * (NGRP + NE)].rearrange("p (a b) -> p a b", a=NT)))
                gl = lgt[:, :, 0:NGRP]
                first(goh[:, :, :], gl, R["gmax"][:, :], R["gpm"][:, :], NGRP)
                own(dve.tensor_tensor(gsc[:, :, :], gl, R["gmax"][:, :].unsqueeze(2).broadcast_to([P, NT, NGRP]), ALU.subtract))
                dve.sem_inc(S["gexp_in"], 1)
                for t in range(NT):
                    behind(dve.tensor_tensor(e4[:, t], lgt[:, t, NGRP:].rearrange("p (g e) -> p g e", g=NGRP),
                                             goh[:, t, :].unsqueeze(2).broadcast_to([P, NGRP, EPG]), ALU.mult))
                catch_up()
                own(dve.tensor_reduce(es[:, :, :], e4[:, :, :, :].rearrange("p t g e -> p t e g"), AX, ALU.add))
                first(eoh[:, 0], es[:, :, :], R["m1"][:, :], R["pm"][:, :], EPG)
                own(dve.scalar_tensor_tensor(out=esc[:, :, :], in0=eoh[:, 0], scalar=-BIG, in1=es[:, :, :], op0=ALU.mult, op1=ALU.add))
                first(eoh[:, 1], esc[:, :, :], R["m2"][:, :], R["pm"][:, :], EPG)
                own(dve.tensor_tensor(R["dd"][:, :], R["m2"][:, :], R["m1"][:, :], ALU.subtract))
                dve.sem_inc(S["gexp_in"], 1)
                for y in range(2):
                    for t in range(NT):
                        behind(dve.tensor_tensor(o12[:, y, t, :].rearrange("p (g e) -> p g e", g=NGRP),
                                                 goh[:, t, :].unsqueeze(2).broadcast_to([P, NGRP, EPG]),
                                                 eoh[:, y, t, :].unsqueeze(1).broadcast_to([P, NGRP, EPG]), ALU.mult))
                catch_up()
                dve.tensor_tensor(mb[:, :, :], o12[:, 0], o12[:, 1], ALU.add).then_inc(S["assign"], 1)
                dve.wait_ge(S["gexp"], 2 * l + 2)
                own(dve.tensor_reduce(R["gsum"][:, :], gsc[:, :, :], AX, ALU.add))
                own(dve.reciprocal(R["gw"][:, :], R["gsum"][:, :]))
                own(dve.tensor_scalar(R["den"][:, :], R["dd"][:, :], 1.0, None, ALU.add))
                own(dve.reciprocal(R["den"][:, :], R["den"][:, :]))
                own(dve.tensor_tensor(R["w1"][:, :], R["gw"][:, :], R["den"][:, :], ALU.mult))
                own(dve.tensor_tensor(R["w2"][:, :], R["w1"][:, :], R["dd"][:, :], ALU.mult))
                dve.wait_ge(S["ranks"], l + 1)
                own(dve.tensor_copy(cnt[:, :], bank[5][:, NT * NE:(NT + 1) * NE]))
                own(dve.tensor_tensor_scan(cums[:, :], ones[:, 0:NE], cnt[:, :], 0.0, ALU.mult, ALU.add))
                own(dve.tensor_tensor(offs[:, :], cums[:, :], cnt[:, :], ALU.subtract))
                behind(dve.tensor_copy(offi[:, :], offs[0:1, :]))
                own(dve.tensor_tensor(slt[:, :, :], offs[:, :].unsqueeze(1).broadcast_to([P, NT, NE]),
                                      bank[5][:, 0:NT * NE].rearrange("p (a b) -> p a b", a=NT), ALU.add))
                for y in range(2):
                    own(dve.tensor_tensor(o12[:, y], o12[:, y], slt[:, :, :], ALU.mult))
                    own(dve.tensor_reduce(R[f"s{y + 1}"][:, :], o12[:, y], AX, ALU.add))
                for t in range(NT):
                    own(dve.tensor_scalar(sel[:, t, :], slot_f[:, :], R["s1"][:, t:t + 1], None, ALU.is_equal))
                    own(dve.scalar_tensor_tensor(out=sel[:, t, :], in0=slot_f[:, :], scalar=R["s2"][:, t:t + 1], in1=sel[:, t, :],
                                                 op0=ALU.is_equal, op1=ALU.add))
                own(dve.memset(xg[:, :, NS:NSP], 0.0))
                dve.sem_inc(S["slots"], 1)
                for t in range(NT):
                    own(dve.tensor_scalar(pw[:, t, :], slot_f[:, :], R["s1"][:, t:t + 1], R["w1"][:, t:t + 1], ALU.is_equal, ALU.mult))
                    own(dve.tensor_scalar(htw, slot_f[:, :], R["s2"][:, t:t + 1], R["w2"][:, t:t + 1], ALU.is_equal, ALU.mult))
                    own(dve.tensor_tensor(pw[:, t, :], pw[:, t, :], htw, ALU.add))
                dve.sem_inc(S["pw_ready"], 1)
                ob = lambda a: a[0:1, :].unsqueeze(1).broadcast_to([1, MAXJ, NE])
                more, pos, start, key = xrow
                own(dve.tensor_tensor(more, ob(cnt), jcap[:, :, :], ALU.is_gt))
                flat = lambda a: a.rearrange("p a b -> p (a b)")
                behind(dve.memset(xone, 1.0))
                catch_up()
                own(dve.tensor_tensor_scan(flat(pos), xone, flat(more), 0.0, ALU.mult, ALU.add))
                own(dve.tensor_copy(xlist[:, 2 * MAXJ:2 * MAXJ + 1], flat(pos)[:, MAXJ * NE - 1:MAXJ * NE]))
                own(dve.tensor_tensor(key, pos, more, ALU.mult))
                own(dve.tensor_tensor(start, ob(offs), jcap[:, :, :], ALU.add))
                own(dve.tensor_scalar(xone[:, 0:NE], cums[0:1, :], float(-CAP), None, ALU.add))
                own(dve.tensor_tensor(start, start, ob(xone[:, 0:NE]), ALU.min))
                for i in range(MAXJ):
                    own(dve.scalar_tensor_tensor(out=pos, in0=key, scalar=float(i + 1), in1=eidx[:, :, :], op0=ALU.is_equal, op1=ALU.mult))
                    own(dve.tensor_reduce(xlist[:, i:i + 1], flat(pos), AX, ALU.add))
                    own(dve.scalar_tensor_tensor(out=pos, in0=key, scalar=float(i + 1), in1=start, op0=ALU.is_equal, op1=ALU.mult))
                    own(dve.tensor_reduce(xlist[:, MAXJ + i:MAXJ + i + 1], flat(pos), AX, ALU.add))
                own(dve.tensor_copy(xlisti[:, :], xlist[:, :]))
                dve.sem_inc(S["lists"], 1)

                e0 = l * NE

                def hidden(e, u):
                    dve.wait_ge(S["sg_ready"], e + (e0 + 1))
                    if not (isinstance(e, int) and e0 + e < 2):
                        dve.wait_ge(S["dn_ready"], e + (e0 - 1))
                    dve.tensor_tensor(hid[:, u, :, :].rearrange("p a b -> p (a b)"), sg[:, u, :, :].rearrange("p a b -> p (a b)"),
                                      bank[2 + u][:, FE * CAP:2 * FE * CAP], ALU.mult).then_inc(S["hid_ready"], 1)

                def keep_y(e, u):
                    off = dve.value_load(offi[0:1, bass.ds(e, 1)], min_val=0, max_val=NS)
                    dve.wait_ge(S["dn_ready"], e + (e0 + 1))
                    if not (isinstance(e, int) and e0 + e < 1):
                        dve.wait_ge(S["yd_done"], e + e0)
                    dve.tensor_copy(yg[:, 4:8, bass.ds(off, CAP)], bank[5 + 2 * u][:, 0:4 * CAP].rearrange("p (k n) -> p k n", k=4))\
                       .then_inc(S["yd_done"], 1)

                hidden(0, 0)
                hidden(1, 1)
                keep_y(0, 0)
                with dve.Fori(1, NE // G) as i:
                    hidden(i * 2, 0)
                    keep_y(i * 2 - 1, 1)
                    hidden(i * 2 + 1, 1)
                    keep_y(i * 2, 0)
                keep_y(NE - 1, 1)
                n_ext = dve.value_load(xlisti[0:1, 2 * MAXJ:2 * MAXJ + 1], min_val=0, max_val=MAXJ)
                with dve.If(n_ext > 0):
                    dve.wait_ge(S["yd_done"], e0 + NE)
                    with dve.Fori(0, n_ext) as i:
                        off = dve.value_load(xlisti[0:1, bass.ds(i + MAXJ, 1)], min_val=0, max_val=NS)
                        dve.wait_ge(X[l]["sg"], i + 1)
                        dve.tensor_tensor(hid[:, 0, :, :].rearrange("p a b -> p (a b)"), sg[:, 0, :, :].rearrange("p a b -> p (a b)"),
                                          bank[2][:, FE * CAP:2 * FE * CAP], ALU.mult).then_inc(X[l]["hid"], 1)
                        dve.wait_ge(X[l]["dn"], i + 1)
                        dve.tensor_copy(yg[:, 4:8, bass.ds(off, CAP)], bank[5][:, 0:4 * CAP].rearrange("p (k n) -> p k n", k=4))\
                           .then_inc(X[l]["yd"], 1)
                        dve.wait_ge(X[l]["yd"], i + 1)
                residual(2 * l + 1)
                normalise(2 * l + 1)
                dve.sem_inc(S["layer_done"], 1)


def kernel(x_prompt, x_sample, state_gla_S, state_mlstm_C, state_mlstm_n, state_mlstm_m, c, c_ctx,
           gla_w_in, gla_w_gate, gla_b_gate, gla_norm_g, gla_w_out,
           mlstm_w_in, mlstm_b_gates, mlstm_norm_g, mlstm_w_out,
           adaln_w, adaln_b, ln_g, ln_b,
           moe_w_group, moe_b_group, moe_w_expert, moe_b_expert, moe_w_gate, moe_w_up, moe_w_down):
    import concourse.bacc as bacc
    from concourse.bass_utils import run_bass_kernel_spmd

    def feat(a):
        a = np.asarray(a)
        a = a.reshape(a.shape[:-1] + (a.shape[-1] // P, P))
        return np.moveaxis(a, -1, 0)

    def rows(a, cols):
        a = np.asarray(a)[:, cols]
        return a.reshape(-1, P, a.shape[1]).transpose(1, 0, 2).reshape(P, -1)

    def tokens(a):
        return np.asarray(a).reshape(-1, KD, P).transpose(2, 1, 0)

    r_ = np.r_
    w_mod = np.asarray(adaln_w).reshape(DEPTH, KD, P, 3 * G_MOD, 256).transpose(0, 3, 2, 1, 4).reshape(DEPTH * 3 * G_MOD, P, PIECE)
    w_in, w_out = [], []
    qk, vo = H * DK, 2 * H * DK
    ro = vo + H * DV
    for w in (gla_w_in, mlstm_w_in):
        for h in range(H):
            w_in.append(rows(w[0], r_[h * DK:(h + 1) * DK, qk + h * DK:qk + (h + 1) * DK]))
            w_in.append(rows(w[0], r_[vo + h * DV:vo + (h + 1) * DV]))
            w_in.append(rows(w[0], r_[ro + h * DV:ro + (h + 1) * DV]))
    go = ro + H * DV
    for w in (gla_w_out, mlstm_w_out):
        for q in range(G_OUT):
            a = q * D // G_OUT
            w_out.append(np.concatenate([rows(w[0], r_[a + sum(OUT_W[:j]):a + sum(OUT_W[:j + 1])]) for j in range(3)], 1))
    w_moe = np.stack([
        np.asarray(moe_w_gate).reshape(DEPTH, NE, KD, P, DE).transpose(0, 1, 3, 2, 4).reshape(DEPTH, NE, P, PIECE),
        np.asarray(moe_w_up).reshape(DEPTH, NE, KD, P, DE).transpose(0, 1, 3, 2, 4).reshape(DEPTH, NE, P, PIECE),
        np.asarray(moe_w_down).reshape(DEPTH, NE, FE, P, D).transpose(0, 1, 3, 2, 4).reshape(DEPTH, NE, P, PIECE)], 2)

    nf = D // 4
    freqs = np.exp(-np.log(10000.0) * np.arange(nf) / nf).astype(np.float32)

    def emb(n):
        a = np.arange(n, dtype=np.float32)[:, None] * freqs
        return np.concatenate([np.sin(a), np.cos(a)], -1).reshape(n, KD // 2, P).transpose(2, 1, 0)

    ins = {
        "xT": np.concatenate([tokens(x_prompt[0]), tokens(x_sample[0])], 2),
        "cT": tokens(np.stack([np.asarray(c_ctx), np.asarray(c[0])])),
        "modb": feat(adaln_b),
        "lng": feat(np.asarray(ln_g).reshape(2 * DEPTH, D)),
        "lnb": feat(np.asarray(ln_b).reshape(2 * DEPTH, D)),
        "hng": feat(np.stack([np.asarray(gla_norm_g[0]), np.asarray(mlstm_norm_g[0])])),
        "posr": emb(N_LAT // GRID_W), "posc": emb(GRID_W),
        "wglr": rows(gla_w_in[0], r_[go:go + 2 * RANK]).reshape(P, KD, 2 * RANK),
        "wgate": np.asarray(gla_w_gate[0]),
        "bgate": feat(np.asarray(gla_b_gate[0]).reshape(-1)),
        "wgt": np.stack([rows(mlstm_w_in[0], r_[go + H * y:go + H * (y + 1)]).reshape(P, KD, H) for y in range(4)]),
        "bgt": np.asarray(mlstm_b_gates[0]).T,
        "wrt": np.concatenate([np.asarray(moe_w_group), np.asarray(moe_w_expert)], 2)
                 .reshape(DEPTH, KD, P, NGRP + NE).transpose(2, 0, 1, 3),
        "brt": np.concatenate([np.asarray(moe_b_group), np.asarray(moe_b_expert)], 1)[None],
        "st_gla": np.asarray(state_gla_S[0, 0]).reshape(2 * H, DK, DV).transpose(1, 0, 2),
        "st_ml": np.asarray(state_mlstm_C[0, 0]).reshape(2 * H, DK, DV).transpose(1, 0, 2),
        "n0": np.asarray(state_mlstm_n[0, 0]).reshape(2 * H, DK).T,
        "m0": np.asarray(state_mlstm_m[0, 0]).T,
        "w_mod": w_mod, "w_in": np.stack(w_in), "w_out": np.stack(w_out), "w_moe": w_moe.reshape(DEPTH * NE * 3, P, PIECE),
    }
    outs = {"y": (P, KD, N), "new_S": (2, H, DK, DV), "new_C": (2, H, DK, DV), "new_n": (DK, 2 * H), "new_m": (H, 2)}

    nc = bacc.Bacc("TRN2", target_bir_lowering=False, num_devices=1)
    ins = {n: np.ascontiguousarray(a) for n, a in ins.items()}
    A = {n: nc.dram_tensor("in_" + n, a.shape, mybir.dt.from_np(a.dtype), kind="ExternalInput").ap() for n, a in ins.items()}
    O = {n: nc.dram_tensor("out_" + n, s, F32, kind="ExternalOutput").ap() for n, s in outs.items()}
    backbone_step(nc, A, O)
    got = run_bass_kernel_spmd(nc, [{"in_" + n: a for n, a in ins.items()}], core_ids=[0]).results[0]
    y = got["out_y"].transpose(2, 1, 0).reshape(N, D)
    return (y[None, :N_CTX], y[None, N_CTX:], got["out_new_S"][None, None], got["out_new_C"][None, None],
            got["out_new_n"].T.reshape(1, 1, 2, H, DK), got["out_new_m"].T.reshape(1, 1, 2, H))
```

```python
from contextlib import ExitStack

import numpy as np
import concourse.bass as bass
from concourse import mybir

F32 = mybir.dt.float32
BF16 = mybir.dt.bfloat16
I32 = mybir.dt.int32
ALU = mybir.AluOpType
ACT = mybir.ActivationFunctionType
AX = mybir.AxisListType.X

P = 128
D = 1024
KD = D // P
DEPTH = 2
N_CTX, N_LAT = 128, 256
N = N_CTX + N_LAT
NT = N // P
GRID_W = 64
H = 4
DK, DV = 128, 256
MV = DV // P
RANK = 16
TAU = 16.0
CH = 64
NCH = N // CH
NGRP, EPG = 4, 8
NE = NGRP * EPG
DE = 256
FE = DE // P
EPS = 1e-5
ALPHA = (2.0 * DEPTH) ** 0.25
CAP = 96
NS = 2 * N
NSP = NS + CAP
MAXJ = (NS - 1) // CAP
SC = NS // P
G = 2
PIECE = 2048
MODW = PIECE // KD
BIG = 3.0e38
STREAMS = ((0, 0, N_CTX), (1, N_CTX, N))

G_MOD, G_HEAD, G_OUT, G_EXP = 8, H, 2, NE
G_LAYER = G_MOD + G_HEAD + G_OUT + G_EXP
OUT_W = (256, 128, 128)

N_STATES = 10
CHAIN = {(1, 0): (2, 3, 4, 5), (1, 1): (5, 4, 3, 2), (0, 0): (0, 1), (0, 1): (1, 0)}


def chain_steps(dirs):
    out = []
    for s in range(4):
        for lat, d in CHAIN:
            if d in dirs and s < len(CHAIN[lat, d]):
                out.append((lat, d, s, CHAIN[lat, d][s], (not lat) or s < 3))
    return out


def state_places(l):
    past, out = {}, []
    for dirs in (((0, 1),) if l == 0 else ((0,), (1,))):
        for lat, d, s, n, more in chain_steps(dirs):
            if more:
                out.append((6 + n % 2, past.get(n % 2)))
                past[n % 2] = len(out) - 1
    return out


def is_neg(v):
    return isinstance(v, int) and v < 0


def backbone_step(nc, A, O):
    ctx = ExitStack()
    with ctx:
        def sb(name, shape, dt=F32):
            return ctx.enter_context(nc.sbuf_tensor(name, shape, dt))

        def sem(name):
            return ctx.enter_context(nc.semaphore(name))

        bank = [ctx.enter_context(nc.psum_tensor(f"bank{i}", [P, 512], F32)) for i in range(8)]

        ring = sb("ring", [P, G, 3, PIECE])
        xT = sb("xT", [P, KD, N])
        hT = sb("hT", [P, KD, N])
        modrow = hT[0:2, 0:4, :].rearrange("p a b -> p (a b)").rearrange("p (a b) -> p a b", a=G)
        mod_banks = ((bank[2], bank[3]), (bank[5], bank[6]))
        zT = sb("zT", [P, KD, N])
        st0 = sb("st0", [P, 2 * H, DV])
        n0 = sb("n0", [P, 2 * H])
        m0 = sb("m0", [H, 2])
        cT = sb("cT", [P, KD, 2])
        scT = sb("scT", [P, KD, 2])
        mod = sb("mod", [P, DEPTH, 6 * KD, 2])
        modb = sb("modb", [P, DEPTH, 6 * KD])
        lng = sb("lng", [P, 2 * DEPTH, KD])
        lnb = sb("lnb", [P, 2 * DEPTH, KD])
        hng = sb("hng", [P, 2, KD])
        wglr = sb("wglr", [P, KD, 2 * RANK])
        bgate = sb("bgate", [P, 2 * H])
        wgt = zT[:, :, 0:P]
        bgt = sb("bgt", [H, 4])
        wrt = sb("wrt", [P, DEPTH, KD, NGRP + NE])
        brt = sb("brt", [1, DEPTH, NGRP + NE])
        ident = sb("ident", [P, P])
        ones_d = sb("ones_d", [P, P])
        ones_v = sb("ones_v", [P, P])
        ones = sb("ones", [P, P])
        onesb = sb("onesb", [P, P], BF16)
        trib = sb("trib", [P, P], BF16)
        rowsel = sb("rowsel", [H, H, P])
        causal = sb("causal", [P, 2, NT, P])
        keep = sb("keep", [P, N])
        fresh = sb("fresh", [H, N])
        slot_f = sb("slot_f", [P, NS])
        ramp = sb("ramp", [P, EPG])
        epst = sb("epst", [P, 1])
        onet = sb("onet", [P, 1])
        jcap = sb("jcap", [1, MAXJ, NE])
        eidx = sb("eidx", [1, MAXJ, NE])
        REGION = 22656
        region = sb("region", [P, REGION])
        taken = {"mix": 0, "moe": 0}

        def part(stage, *dims):
            size = int(np.prod(dims))
            a = taken[stage]
            taken[stage] += size
            assert taken[stage] <= REGION, (stage, taken)
            v = region[:, a:a + size]
            if len(dims) == 2:
                v = v.rearrange("p (a b) -> p a b", a=dims[0])
            if len(dims) == 3:
                v = v.rearrange("p (a b c) -> p a b c", a=dims[0], b=dims[1])
            if len(dims) == 4:
                v = v.rearrange("p (a b c d) -> p a b c d", a=dims[0], b=dims[1], c=dims[2])
            return v

        oT = part("mix", KD, N)
        early = oT.rearrange("p a b -> p (a b)")
        slot_i = early[:, 0:NS].bitcast(I32)
        posc = early[:, NS:NS + KD // 2 * GRID_W].rearrange("p (a b) -> p a b", b=GRID_W)
        posr = early[:, NS + KD // 2 * GRID_W:NS + KD // 2 * (GRID_W + N_LAT // GRID_W)].rearrange("p (a b) -> p a b", a=KD // 2)
        qT = part("mix", 2, N)
        kT = part("mix", 2, N)
        vt = part("mix", 2, NT, DV)
        rT = part("mix", 2, MV, N)
        ktok = part("mix", 2, NT, P)
        am = sb("am", [P, 2, N])
        st = part("mix", 4, 2, DV)
        wgate = st.rearrange("p a b c -> p (a b c)")[0:2 * RANK, 0:2 * H * DK].rearrange("p (a b) -> p a b", a=2)
        sfin = part("mix", 2, 2, DV)
        num = part("mix", MV, N)
        nsq = part("mix", MV, N)
        rs = part("mix", N)
        base_e = taken["mix"]
        ea = part("mix", 2 * H, N)
        eb = part("mix", 2 * H, N)
        ed = part("mix", 2 * H, N)
        ec = zT
        dec = sb("dec", [P, 2 * H, NCH])
        taken["mix"] = base_e
        graw = part("mix", 4, N)
        rows = [part("mix", 2, N) for _ in range(7)]
        lf, bcum, urow, wrow, einr, mir, ulr = rows
        dtmp, rden = graw[:, 0, :], graw[:, 1, :]
        expd, emt = graw[:, 2:4, :], bcum
        einb = lf
        qe = part("mix", 2, N)
        nb = part("mix", 2, 2, P)
        nb0 = part("mix", P)
        mst = sb("mst", [H, 2, 2, 5])
        decr = sb("decr", [H, 2, NCH])
        cols = sb("cols", [P, 12, H])
        nfin = sb("nfin", [P, 2 * H])
        mfin = sb("mfin", [H, 2])
        xg = part("moe", KD, NSP)
        yg = part("moe", KD, NSP)
        htok = part("moe", NT, D)
        cw = part("moe", SC, N)
        ysl = region[:, 0:SC * D].rearrange("p (a b) -> p a b", a=SC)
        sel = region[:, KD * NSP:KD * NSP + NT * NS].rearrange("p (a b) -> p a b", a=NT)
        pw = zT[:, 0:6, :].rearrange("p a b -> p (a b)").rearrange("p (a b) -> p a b", a=NT)
        htw = hT[:, 0:2, :].rearrange("p a b -> p (a b)")
        sg = part("moe", 2, FE, CAP)
        hid = part("moe", 2, FE, CAP)
        lgt = part("moe", NT, NGRP + NE)
        R = {n: sb("r_" + n, [P, NT]) for n in ("gmax", "gpm", "gsum", "gw", "m1", "m2", "pm", "dd", "den", "w1", "w2", "s1", "s2")}
        gsc = sb("gsc", [P, NT, NGRP])
        goh = sb("goh", [P, NT, NGRP])
        e4 = part("moe", NT, NGRP, EPG)
        es = part("moe", NT, EPG)
        esc = part("moe", NT, EPG)
        eoh = part("moe", 2, NT, EPG)
        o12 = part("moe", 2, NT, NE)
        mb = sb("mb", [P, NT, NE], BF16)
        cnt = sb("cnt", [P, NE])
        cums = sb("cums", [P, NE])
        offs = sb("offs", [P, NE])
        slt = part("moe", NT, NE)
        offi = sb("offi", [1, NE], I32)
        xrow = [hT[0:1, 2 + i, 0:MAXJ * NE].rearrange("p (a b) -> p a b", a=MAXJ) for i in range(4)]
        xone = hT[0:1, 6, 0:MAXJ * NE]
        xlist = sb("xlist", [1, 2 * MAXJ + 1])
        xlisti = sb("xlisti", [1, 2 * MAXJ + 1], I32)

        S = {n: sem(n) for n in (
            "small_in", "x_in", "state_in", "consts", "silu_c", "mod_cols", "mod_sb", "mod_ready", "h_ready",
            "pj_ready", "pj_free", "gates_in", "logit_sb", "gate_sp", "gate_d", "e_ready", 
            "scaled", "kt_ready", "kt_sb", "sc_ready", "am_ready", "num_ready", "num_sb", "ds_ready",
            "state_ready", "mean_ready", "cent", "sq_ready", "var_ready", "std_ready", "o_ready", "den_free", "num_cp",
            "fin_state", "yscaled", "z_ready", "lmean", "lcent", "lsq", "lvar", "lstd",
            "rt_ready", "rt_done", "gexp_in", "gexp", "assign", "ranks", "slots", "lists", "pw_ready", "xg_ready",
            "cw_ready", "gu_ready", "sg_ready", "hid_ready", "dn_ready", "ya_done", "yd_done", "ysl_ready",
            "rows_ready", "rows_sb", "exp_in", "exp_out", "colps", "colsb", "y_out", "m_out", "fin_m", 
            "dve_step", "act_step", "pool_step", "heads_done", "layer_done", "wgt_in", "wgate_in", "ring_back")}
        out_state = [sem(f"out_state{b}") for b in range(2)]
        used = [sem(f"used{j}") for j in range(3)]
        landed = [[sem(f"landed{u}_{j}") for j in range(3)] for u in range(G)]
        X = [{n: sem(f"x{n}{l}") for n in ("land", "gu", "sg", "hid", "dn", "ya", "yd")} for l in range(DEPTH)]

        SMALL = [(cT[:, :, :], A["cT"]), (modb[:, :, :], A["modb"]), (lng[:, :, :], A["lng"]), (lnb[:, :, :], A["lnb"]),
                 (hng[:, :, :], A["hng"]), (posr[:, :, :], A["posr"]), (posc[:, :, :], A["posc"]),
                 (wglr[:, :, :], A["wglr"]), (bgate[:, :], A["bgate"]), (wrt[:, :, :, :], A["wrt"]), (brt[:, :, :], A["brt"]),
                 (n0[:, :], A["n0"]), (m0[:, :], A["m0"]), (bgt[:, :], A["bgt"])]
        N_SMALL = 16 * len(SMALL)
        N_CONST = 18

        PJ_HEAD = 2 + NT + MV
        N_PJ_L0 = 1 + 2 * H + H * PJ_HEAD + KD + 2 * NT + 2 * KD + SC + 2 * SC + KD
        PJ_END = [[1 + 2 * H + PJ_HEAD * (h + 1) for h in range(H)],
                  [N_PJ_L0 + 1 + PJ_HEAD * (h + 1) + 6 * h for h in range(H)]]
        block = ctx.enter_context(nc.Block())

        @block.sync
        def _(sp):
            sp.dma_start(xT[:, :, :], A["xT"]).then_inc(S["x_in"], 16)
            sp.dma_start(st0[:, :, :], A["st_gla"]).then_inc(S["state_in"], 16)

            def load(g, src, widths=(PIECE,) * 3):
                u = g[1]
                for j in range(3):
                    if not is_neg(g[0] - G):
                        sp.wait_ge(used[j], g[0] - G + 1)
                    sp.dma_start(ring[:, u, j, 0:widths[j]], src(j)).then_inc(landed[u][j], 16)

            for l in range(DEPTH):
                g0 = l * G_LAYER

                def mod_group(i, u):
                    g = g0 + G * i + u
                    load((g, u), lambda j: A["w_mod"][bass.ds((l * G_MOD + G * i + u) * 3 + j, 1)].rearrange("a p n -> p (a n)"))

                for u in range(G):
                    mod_group(0, u)
                with sp.Fori(1, G_MOD // G) as i:
                    for u in range(G):
                        mod_group(i, u)
                g0 += G_MOD
                for h in range(H):
                    load((g0 + h, h % G), lambda j: A["w_in"][(l * H + h) * 3 + j])
                g0 += G_HEAD
                for q in range(G_OUT):
                    at = (0, OUT_W[0] * KD, (OUT_W[0] + OUT_W[1]) * KD)
                    load((g0 + q, q % G), lambda j: A["w_out"][l * G_OUT + q, :, at[j]:at[j] + OUT_W[j] * KD],
                         [w * KD for w in OUT_W])
                g0 += G_OUT
                if l == 0:
                    sp.wait_ge(S["heads_done"], 1)
                    sp.dma_start(st0[:, :, :], A["st_ml"]).then_inc(S["state_in"], 16)
                with sp.Fori(0, NE // G) as i:
                    for u in range(G):
                        load((g0 + G * i + u, u),
                             lambda j: A["w_moe"][bass.ds((l * NE + G * i + u) * 3 + j, 1)].rearrange("a p n -> p (a n)"))
                sp.wait_ge(S["lists"], l + 1)
                n_ext = sp.value_load(xlisti[0:1, 2 * MAXJ:2 * MAXJ + 1], min_val=0, max_val=MAXJ)
                with sp.If(n_ext > 0):
                    for j in range(3):
                        sp.wait_ge(used[j], (l + 1) * G_LAYER)
                    with sp.Fori(0, n_ext) as i:
                        e = sp.value_load(xlisti[0:1, bass.ds(i, 1)], min_val=0, max_val=NE - 1)
                        for j in range(3):
                            sp.dma_start(ring[:, 0, j, :],
                                         A["w_moe"][bass.ds((e + l * NE) * 3 + j, 1)].rearrange("a p n -> p (a n)"))\
                              .then_inc(X[l]["land"], 16)
                        sp.wait_ge(X[l]["dn"], i + 1)
                        sp.sem_inc(S["ring_back"], 1)
            sp.wait_ge(S["layer_done"], DEPTH)
            sp.dma_start(O["y"], xT[:, :, :]).then_inc(S["y_out"], 16)
            sp.wait_ge(S["y_out"], 16)

        @block.gpsimd
        def _(pool):
            steps = [0]

            def own(ins):
                steps[0] += 1
                ins.then_inc(S["pool_step"], 1)
                pool.wait_ge(S["pool_step"], steps[0])

            ready = lambda ins: ins.then_inc(S["consts"], 1)
            ready(pool.memset(ones_d[:, :], 1.0 / D))
            ready(pool.memset(ones_v[:, :], 1.0 / DV))
            ready(pool.memset(ones[:, :], 1.0))
            ready(pool.memset(onesb[:, :], 1.0))
            ready(pool.memset(epst[:, :], EPS))
            ready(pool.memset(onet[:, :], 1.0))
            own(pool.memset(wgate[:, :, :], 0.0))
            pool.dma_start(wgate[0:RANK, 0, :], A["wgate"][0]).then_inc(S["wgate_in"], 16)
            pool.dma_start(wgate[RANK:2 * RANK, 1, :], A["wgate"][1]).then_inc(S["wgate_in"], 16)
            own(pool.memset(ident[:, :], 0.0))
            ready(pool.affine_select(out=ident[:, :], in_=ident[:, :], compare_op=ALU.not_equal, fill=1.0,
                                     base=0, pattern=[[-1, P]], channel_multiplier=1))
            own(pool.memset(trib[:, :], 1.0))
            ready(pool.affine_select(out=trib[:, :], in_=trib[:, :], compare_op=ALU.is_gt, fill=0.0,
                                     base=0, pattern=[[1, P]], channel_multiplier=-1))
            own(pool.memset(rowsel[:, :, :], 0.0))
            ready(pool.affine_select(out=rowsel[:, :, :], in_=rowsel[:, :, :], compare_op=ALU.not_equal, fill=1.0,
                                     base=0, pattern=[[-1, H], [0, P]], channel_multiplier=1))
            own(pool.memset(causal[:, :, :, :], 1.0))
            own(pool.affine_select(out=causal[:, 0], in_=causal[:, 0], compare_op=ALU.is_ge, fill=0.0,
                                   base=0, pattern=[[0, NT], [1, P]], channel_multiplier=-1))
            own(pool.affine_select(out=causal[:, 1], in_=causal[:, 1], compare_op=ALU.is_ge, fill=0.0,
                                   base=0, pattern=[[0, NT], [-1, P]], channel_multiplier=1))
            ready(pool.affine_select(out=causal[:, 0, :, CH:P], in_=causal[:, 0, :, CH:P], compare_op=ALU.is_ge, fill=0.0,
                                     base=-CH, pattern=[[0, NT], [0, CH]], channel_multiplier=1))
            ready(pool.affine_select(out=causal[:, 1, :, 0:CH], in_=causal[:, 1, :, 0:CH], compare_op=ALU.is_ge, fill=0.0,
                                     base=CH - 1, pattern=[[0, NT], [0, CH]], channel_multiplier=-1))
            own(pool.memset(keep[:, :], 1.0))
            ready(pool.memset(keep[:, 0:N:CH], 0.0))
            own(pool.memset(fresh[:, :], 0.0))
            ready(pool.memset(fresh[:, 0:N:CH], -BIG))
            own(pool.iota(slot_i[:, :], pattern=[[1, NS]], base=0, channel_multiplier=0))
            ready(pool.tensor_copy(slot_f[:, :], slot_i[:, :]))
            for k in range(EPG):
                ins = pool.memset(ramp[:, k:k + 1], float(EPG - k))
            ready(ins)
            for j in range(MAXJ):
                ins = pool.memset(jcap[:, j, :], float(CAP * (j + 1)))
            ready(ins)
            for e in range(NE):
                ins = pool.memset(eidx[:, :, e:e + 1], float(e))
            ready(ins)
            ready(pool.memset(am[:, :, :], 0.0))

            for l in range(DEPTH):
                for h in range(H):
                    pool.wait_ge(S["fin_state"], l * H + h + 1)
                    for d in range(2):
                        dst = (O["new_S"] if l == 0 else O["new_C"])[d, h]
                        pool.dma_start(dst, sfin[:, h % 2, d, :]).then_inc(out_state[h % 2], 16)
                if l == 0:
                    pool.wait_ge(S["layer_done"], 1)
                    own(pool.memset(wgt, 0.0))
                    for y in range(4):
                        pool.dma_start(wgt[:, :, 32 * y:32 * y + H], A["wgt"][y]).then_inc(S["wgt_in"], 16)
            pool.wait_ge(S["fin_m"], 1)
            pool.dma_start(O["new_n"], nfin[:, :]).then_inc(S["m_out"], 16)
            pool.dma_start(O["new_m"], mfin[:, :]).then_inc(S["m_out"], 16)
            pool.wait_ge(S["m_out"], 32)
            for b in range(2):
                pool.wait_ge(out_state[b], 16 * DEPTH * H)

        @block.tensor
        def _(pe):
            n_pj = [0]

            def pj():
                n = n_pj[0]
                n_pj[0] += 1
                if n >= 2:
                    pe.wait_ge(S["pj_free"], n - 1)
                return bank[n % 2]

            read_pieces = []

            def mm(out, lhsT, rhs, start, stop):
                ins = pe.matmul(out, lhsT, rhs, start=start, stop=stop, skip_group_check=True)
                if read_pieces and start and not stop:
                    ins.then_inc(used[read_pieces.pop()], 1)
                return ins

            n_ds = [0]

            def piece(l, g, j):
                gg = l * G_LAYER + g
                pe.wait_ge(landed[gg % G][j], 16 * (gg // G + 1))
                return ring[:, gg % G, j, :]

            def modulation(l):
                def rows(i, u):
                    at = mod_banks[u]
                    for j in range(3):
                        pe.wait_ge(landed[u][j], (i + (l * G_LAYER // G + 1)) * 16)
                        if j == 1:
                            for k in range(KD):
                                ins = mm(at[0][0:2, :].rearrange("p (a b) -> p a b", a=2), scT[:, k, :],
                                         ring[:, u, 0:2, k * MODW:(k + 1) * MODW], k == 0, k == KD - 1)
                            ins.then_inc(used[0], 1)
                    for k in range(KD):
                        ins = mm(at[1][0:2, 0:MODW], scT[:, k, :], ring[:, u, 2, k * MODW:(k + 1) * MODW], k == 0, k == KD - 1)
                        if k == 0:
                            ins.then_inc(used[1], 1)
                    ins.then_inc(used[2], 1)

                def columns(i, u):
                    pe.wait_ge(S["mod_sb"], i * G + (l * G_MOD + u + 1))
                    for c in range(3 * MODW // P):
                        ins = mm(bank[7][:, bass.ds((i * G + u) * 12 + c * 2, 2)], modrow[:, u, c * P:(c + 1) * P],
                                 ident[0:2, 0:2], True, True)
                    return ins

                assert not read_pieces
                if l >= 1:
                    pe.wait_ge(S["lstd"], 2 * l)
                rows(0, 0)
                with pe.Fori(0, G_MOD // G - 1) as i:
                    rows(i, 1)
                    columns(i, 0)
                    rows(i + 1, 0)
                    columns(i, 1)
                rows(G_MOD // G - 1, 1)
                columns(G_MOD // G - 1, 0)
                columns(G_MOD // G - 1, 1).then_inc(S["mod_cols"], 1)

            open_bank = [None]

            def project_half(l, h, i):
                if h >= H:
                    return
                n = i // 2
                j = (0, 0, 1, 1, 1, 2, 2)[n]
                if i % 2 == 0:
                    piece(l, G_MOD + h, j)
                    open_bank[0] = pj()
                w = ring[:, h % G, j, :].rearrange("p (k n) -> p k n", k=KD)
                b = open_bank[0]
                for k in range(i % 2 * KD // 2, (i % 2 + 1) * KD // 2):
                    if j == 1:
                        t = n - 2
                        ins = mm(b[:, 0:DV], hT[:, k, t * P:(t + 1) * P], w[:, k, :], k == 0, k == KD - 1)
                    else:
                        c = n if n < 2 else n - 5
                        ins = mm(b[:, 0:N], w[:, k, c * P:(c + 1) * P], hT[:, k, :], k == 0, k == KD - 1)
                if i % 2 == 1:
                    ins.then_inc(S["pj_ready"], 1)
                    if n in (1, 4, 6):
                        read_pieces.append(j)

            def project(l, h, n):
                project_half(l, h, 2 * n)
                project_half(l, h, 2 * n + 1)

            def head_mean(l, h):
                n = l * H + h
                pe.wait_ge(S["num_sb"], n + 1)
                for m in range(MV):
                    ins = mm(bank[4][:, 0:N], ones_v[:, :], num[:, m, :], m == 0, m == MV - 1)
                ins.then_inc(S["mean_ready"], 1)

            def head_var(l, h):
                n = l * H + h
                pe.wait_ge(S["sq_ready"], n + 1)
                if n >= 1:
                    pe.wait_ge(S["std_ready"], n)
                for m in range(MV):
                    ins = mm(bank[4][:, 0:N], ones_v[:, :], nsq[:, m, :], m == 0, m == MV - 1)
                ins.then_inc(S["var_ready"], 1)

            def attend_gla(h):
                b = h % 2
                places = state_places(0)
                if h >= 1:
                    pe.wait_ge(S["state_ready"], N_STATES * h)
                pe.wait_ge(S["pj_free"], PJ_END[0][h])
                pe.wait_ge(S["scaled"], h + 1)
                for d in range(2):
                    if d + 2 * h >= 1:
                        pe.wait_ge(S["kt_sb"], 2 * h + d)
                    for t in range(NT):
                        ins = pe.transpose(bank[7][:, t * P:(t + 1) * P], eb[:, d * H + h, t * P:(t + 1) * P], ident[:, :])
                    ins.then_inc(S["kt_ready"], 1)
                for d in range(2):
                    if 2 * h + d >= 1:
                        pe.wait_ge(S["am_ready"], 2 * h + d)
                    for t in range(NT):
                        c = slice(t * P, (t + 1) * P)
                        ins = mm(bank[5][:, c], ec[:, d * H + h, c], ea[:, d * H + h, c], True, True)
                    ins.then_inc(S["sc_ready"], 1)
                if h >= 1:
                    head_mean(0, h - 1)
                project(0, h + 1, 0)
                if h >= 1:
                    head_var(0, h - 1)
                pe.wait_ge(S["am_ready"], 2 * h + 2)
                for m in range(MV):
                    for t in range(NT):
                        c = slice(t * P, (t + 1) * P)
                        for d in range(2):
                            mm(bank[2 + m][:, c], vt[:, b, t, m * P:(m + 1) * P], am[:, d, c], t == 0 and d == 0, False)
                pe.wait_ge(S["kt_sb"], 2 * h + 2)
                pe.wait_ge(S["state_in"], 16)
                made = {}
                steps = chain_steps((0, 1))
                for x, (lat, d, s, n, more) in enumerate(steps):
                    c = slice(n * CH, (n + 1) * CH)
                    if x == 2:
                        project(0, h + 1, 1)
                    if s > 0 and s != steps[x - 1][2]:
                        if s > 1:
                            project(0, h + 1, 2 * s - 1)
                        project(0, h + 1, 2 * s)
                    if s > 0:
                        pe.wait_ge(S["state_ready"], made[lat, d, s - 1])
                    if s > 0 or lat:
                        src = st0[:, d * H + h, :] if s == 0 else st[:, 2 * lat + d, s % 2, :]
                        for m in range(MV):
                            ins = mm(bank[2 + m][:, c], src[:, m * P:(m + 1) * P], ed[:, d * H + h, c], False, x == len(steps) - 1)
                    if more:
                        bk, taken_by = places[n_ds[0] - N_STATES * h]
                        if taken_by is not None:
                            pe.wait_ge(S["state_ready"], N_STATES * h + taken_by + 1)
                        q = slice((n % 2) * CH, (n % 2 + 1) * CH)
                        mm(bank[bk][:, 0:DV], ktok[q, d, n // 2, :], vt[q, b, n // 2, :],
                           True, True).then_inc(S["ds_ready"], 1)
                        n_ds[0] += 1
                        made[lat, d, s] = n_ds[0]
                    if x == len(steps) - 1:
                        ins.then_inc(S["num_ready"], 1)

            def attend_mlstm(h):
                b = h % 2
                places = state_places(1)
                pe.wait_ge(S["state_ready"], N_STATES * (H + h))
                pe.wait_ge(S["pj_free"], PJ_END[1][h])
                if h >= 1:
                    pe.wait_ge(S["kt_sb"], 2 * H + h)
                    pe.wait_ge(S["am_ready"], 2 * H + 2 * h)
                for t in range(NT):
                    ins = pe.transpose(bank[7][:, t * P:(t + 1) * P], kT[:, b, t * P:(t + 1) * P], ident[:, :])
                ins.then_inc(S["kt_ready"], 1)
                for t in range(NT):
                    c = slice(t * P, (t + 1) * P)
                    ins = mm(bank[5][:, c], kT[:, b, c], qT[:, b, c], True, True)
                ins.then_inc(S["sc_ready"], 1)
                for d in range(2):
                    for r in (wrow, einr, mir):
                        o = pj()
                        mm(o[:, 0:N], rowsel[:, h, :], r[0:H, d, :], True, True).then_inc(S["pj_ready"], 1)
                if h >= 1:
                    head_mean(1, h - 1)
                project(1, h + 1, 0)
                if h >= 1:
                    head_var(1, h - 1)
                pe.wait_ge(S["kt_sb"], 2 * H + h + 1)
                pe.wait_ge(S["state_in"], 32)
                for d in range(2):
                    e = 2 * h + d
                    pe.wait_ge(S["am_ready"], 2 * H + e + 1)
                    if d == 1:
                        project_half(1, h + 1, 7)
                        project_half(1, h + 1, 8)
                    if e >= 1:
                        pe.wait_ge(S["num_cp"], e)
                    for m in range(MV):
                        for t in range(NT):
                            c = slice(t * P, (t + 1) * P)
                            mm(bank[2 + m][:, c], vt[:, b, t, m * P:(m + 1) * P], am[:, d, c], t == 0, False)
                    if e >= 1:
                        pe.wait_ge(S["den_free"], e)
                    if d == 0 and h >= 1:
                        pe.wait_ge(S["std_ready"], H + h)
                    mm(bank[4][:, 0:N], ones[:, :], am[:, d, :], True, False)
                    steps = chain_steps((d,))
                    made = {}
                    for x, (lat, d, s, n, more) in enumerate(steps):
                        c = slice(n * CH, (n + 1) * CH)
                        if x >= 1:
                            project_half(1, h + 1, 7 * d + 1 + x)
                        if s > 0:
                            pe.wait_ge(S["state_ready"], made[lat, d, s - 1])
                        if s > 0 or lat:
                            src = st0[:, d * H + h, :] if s == 0 else st[:, 2 * lat + d, s % 2, :]
                            nsrc = nb0 if s == 0 else nb[:, lat, s % 2, :]
                            for m in range(MV):
                                mm(bank[2 + m][:, c], src[:, m * P:(m + 1) * P], qe[:, d, c], False, x == len(steps) - 1)
                            ins = mm(bank[4][:, c], nsrc, qe[:, d, c], False, x == len(steps) - 1)
                        if more:
                            bk, taken_by = places[n_ds[0] - N_STATES * (H + h)]
                            if taken_by is not None:
                                pe.wait_ge(S["state_ready"], N_STATES * (H + h) + taken_by + 1)
                            q = slice((n % 2) * CH, (n % 2 + 1) * CH)
                            kw = ktok[q, d, n // 2, :]
                            mm(bank[bk][:, DV:DV + 1], kw, ones[q, 0:1], True, True)
                            mm(bank[bk][:, 0:DV], kw, vt[q, b, n // 2, :],
                               True, True).then_inc(S["ds_ready"], 1)
                            n_ds[0] += 1
                            made[lat, d, s] = n_ds[0]
                        if x == len(steps) - 1:
                            ins.then_inc(S["num_ready"], 1)

            def out_projection(l):
                pe.wait_ge(S["o_ready"], (l + 1) * H)
                for q in range(G_OUT):
                    for j in range(3):
                        w = piece(l, G_MOD + G_HEAD + q, j)[:, 0:OUT_W[j] * KD].rearrange("p (k n) -> p k n", k=KD)
                        for c in range(OUT_W[j] // P):
                            b = pj()
                            for k in range(KD):
                                ins = mm(b[:, 0:N], w[:, k, c * P:(c + 1) * P], oT[:, k, :], k == 0, k == KD - 1)
                            ins.then_inc(S["pj_ready"], 1)
                        read_pieces.append(j)

            def layer_norm(x):
                for k in range(KD):
                    pe.wait_ge(S["z_ready"], x * KD + k + 1)
                    ins = mm(bank[4][:, 0:N], ones_d[:, :], zT[:, k, :], k == 0, k == KD - 1)
                ins.then_inc(S["lmean"], 1)
                for k in range(KD):
                    pe.wait_ge(S["lsq"], x * KD + k + 1)
                    ins = mm(bank[5][:, 0:N], ones_d[:, :], hT[:, k, :], k == 0, k == KD - 1)
                ins.then_inc(S["lvar"], 1)

            def route(l):
                pe.wait_ge(S["h_ready"], 2 * l + 2)
                w = NGRP + NE
                for t in range(NT):
                    c = slice(t * w, (t + 1) * w)
                    mm(bank[4][:, c], ones[0:1, :], brt[0:1, l, :], True, False)
                    for k in range(KD):
                        ins = mm(bank[4][:, c], hT[:, k, t * P:(t + 1) * P], wrt[:, l, k, :], False, k == KD - 1)
                ins.then_inc(S["rt_ready"], 1)
                for t in range(NT):
                    for q in range(2):
                        b = pj()
                        for k in range(4):
                            ins = pe.transpose(b[:, k * P:(k + 1) * P], hT[:, 4 * q + k, t * P:(t + 1) * P], ident[:, :])
                        ins.then_inc(S["pj_ready"], 1)
                pe.wait_ge(S["assign"], l + 1)
                for t in range(NT):
                    for s in range(t + 1):
                        mm(bank[5][:, t * NE:(t + 1) * NE], (trib if s == t else onesb)[:, :], mb[:, s, :], s == 0, s == t)
                for s in range(NT):
                    ins = mm(bank[5][:, NT * NE:(NT + 1) * NE], onesb[:, :], mb[:, s, :], s == 0, s == NT - 1)
                ins.then_inc(S["ranks"], 1)

            def gather(l):
                pe.wait_ge(S["slots"], l + 1)
                for k in range(KD):
                    for q in range(2):
                        b = pj()
                        for t in range(NT):
                            ins = mm(b[:, 0:N], htok[:, t, k * P:(k + 1) * P], sel[:, t, q * N:(q + 1) * N], t == 0, t == NT - 1)
                        ins.then_inc(S["pj_ready"], 1)
                pe.wait_ge(S["pw_ready"], l + 1)
                for c in range(SC):
                    b = pj()
                    for t in range(NT):
                        ins = pe.transpose(b[:, t * P:(t + 1) * P], pw[:, t, c * P:(c + 1) * P], ident[:, :])
                    ins.then_inc(S["pj_ready"], 1)

            def gate_up(l, u, off, out, sig):
                for j in range(2):
                    w = ring[:, u, j, :].rearrange("p (k n) -> p k n", k=KD)
                    for f in range(FE):
                        for k in range(KD):
                            ins = mm(out[:, (j * FE + f) * CAP:(j * FE + f + 1) * CAP], w[:, k, f * P:(f + 1) * P],
                                     xg[:, k, bass.ds(off, CAP)], k == 0, k == KD - 1)
                    if j == 0 and sig is None:
                        ins.then_inc(used[0], 1)
                return ins

            def down(u, hb, b0, b1):
                w = ring[:, u, 2, :].rearrange("p (k n) -> p k n", k=FE)
                for k in range(KD):
                    o = (b0 if k < 4 else b1)[:, (k % 4) * CAP:(k % 4 + 1) * CAP]
                    for f in range(FE):
                        ins = mm(o, w[:, f, k * P:(k + 1) * P], hid[:, hb, f, :], f == 0, f == FE - 1)
                return ins

            def experts(l):
                g0 = l * G_LAYER + G_MOD + G_HEAD + G_OUT
                e0 = l * NE

                def up_step(e, u, turn):
                    off = pe.value_load(offi[0:1, bass.ds(e, 1)], min_val=0, max_val=NS)
                    for j in range(2):
                        pe.wait_ge(landed[u][j], turn * 16 + 16 * (g0 // G + 1))
                    if not (isinstance(e, int) and e0 + e < 2):
                        pe.wait_ge(S["hid_ready"], e + (e0 - 1))
                    ins = gate_up(l, u, off, bank[2 + u], None)
                    ins.then_inc(S["gu_ready"], 1)
                    return ins

                def down_step(e, u, turn):
                    pe.wait_ge(landed[u][2], turn * 16 + 16 * (g0 // G + 1))
                    pe.wait_ge(S["hid_ready"], e + (e0 + 1))
                    pe.sem_inc(used[1], 1)
                    if not (isinstance(e, int) and e0 + e < 2):
                        pe.wait_ge(S["ya_done"], e + (e0 - 1))
                        pe.wait_ge(S["yd_done"], e + (e0 - 1))
                    down(u, u, bank[4 + 2 * u], bank[5 + 2 * u]).then_inc(S["dn_ready"], 1)
                    read_pieces.append(2)

                pe.wait_ge(S["xg_ready"], l + 1)
                up_step(0, 0, 0)
                up_step(1, 1, 0)
                down_step(0, 0, 0)
                with pe.Fori(1, NE // G) as i:
                    up_step(i * 2, 0, i)
                    down_step(i * 2 - 1, 1, i - 1)
                    up_step(i * 2 + 1, 1, i)
                    down_step(i * 2, 0, i)
                down_step(NE - 1, 1, NE // G - 1)
                pe.wait_ge(S["dn_ready"], (l + 1) * NE)
                pe.sem_inc(used[read_pieces.pop()], 1)
                pe.wait_ge(S["lists"], l + 1)

                n_ext = pe.value_load(xlisti[0:1, 2 * MAXJ:2 * MAXJ + 1], min_val=0, max_val=MAXJ)
                with pe.If(n_ext > 0):
                    with pe.Fori(0, n_ext) as i:
                        off = pe.value_load(xlisti[0:1, bass.ds(i + MAXJ, 1)], min_val=0, max_val=NS)
                        pe.wait_ge(X[l]["land"], i * 48 + 48)
                        gate_up(l, 0, off, bank[2], X[l]["gu"]).then_inc(X[l]["gu"], 1)
                        pe.wait_ge(X[l]["hid"], i + 1)
                        down(0, 0, bank[4], bank[5]).then_inc(X[l]["dn"], 1)
                        pe.wait_ge(X[l]["ya"], i + 1)
                        pe.wait_ge(X[l]["yd"], i + 1)

            def combine(l):
                pe.wait_ge(S["ya_done"], (l + 1) * NE)
                pe.wait_ge(S["yd_done"], (l + 1) * NE)
                pe.wait_ge(S["cw_ready"], l + 1)
                for c in range(SC):
                    for q in range(2):
                        b = pj()
                        for k in range(4):
                            ins = pe.transpose(b[:, k * P:(k + 1) * P], yg[:, 4 * q + k, c * P:(c + 1) * P], ident[:, :])
                        ins.then_inc(S["pj_ready"], 1)
                pe.wait_ge(S["ysl_ready"], l + 1)
                for k in range(KD):
                    b = pj()
                    for c in range(SC):
                        ins = mm(b[:, 0:N], ysl[:, c, k * P:(k + 1) * P], cw[:, c, :], c == 0, c == SC - 1)
                    ins.then_inc(S["pj_ready"], 1)

            pe.wait_ge(S["consts"], N_CONST)
            pe.wait_ge(S["small_in"], N_SMALL)
            pe.wait_ge(S["silu_c"], 1)
            for l in range(DEPTH):
                modulation(l)
                pe.wait_ge(S["h_ready"], 2 * l + 1)
                if l == 0:
                    b = pj()
                    for k in range(KD):
                        ins = mm(b[0:2 * RANK, 0:N], wglr[:, k, :], hT[:, k, :], k == 0, k == KD - 1)
                    ins.then_inc(S["pj_ready"], 1)
                    pe.wait_ge(S["gates_in"], 1)
                    pe.wait_ge(S["wgate_in"], 32)
                    for d in range(2):
                        for h in range(H):
                            b = pj()
                            mm(b[:, 0:N], wgate[:, d, h * DK:(h + 1) * DK], num[0:2 * RANK, 0, :], True, True)\
                                .then_inc(S["pj_ready"], 1)
                else:
                    pe.wait_ge(S["wgt_in"], 64)
                    b = pj()
                    for k in range(KD):
                        ins = mm(b[:, 0:N], wgt[:, k, :], hT[:, k, :], k == 0, k == KD - 1)
                    ins.then_inc(S["pj_ready"], 1)
                for n in range(PJ_HEAD):
                    project(l, 0, n)
                if l == 1:
                    pe.wait_ge(S["rows_ready"], 1)
                    for y, r in enumerate((urow, ulr)):
                        for d in range(2):
                            for t in range(NT):
                                i = (y * 2 + d) * NT + t
                                pe.transpose(bank[7][:, i * H:(i + 1) * H], r[0:H, d, t * P:(t + 1) * P], ident[0:H, 0:H])
                    for h in range(H):
                        ins = mm(bank[7][:, 64 + h * 2 * NCH:64 + (h + 1) * 2 * NCH], rowsel[:, h, :],
                                 decr[:, :, :].rearrange("p a b -> p (a b)"), True, True)
                    ins.then_inc(S["colps"], 1)
                    pe.wait_ge(S["colsb"], 1)
                for h in range(H):
                    (attend_gla if l == 0 else attend_mlstm)(h)
                head_mean(l, H - 1)
                head_var(l, H - 1)
                pe.wait_ge(S["num_ready"], H if l == 0 else 3 * H)
                pe.sem_inc(S["heads_done"], 1)
                out_projection(l)
                layer_norm(2 * l)
                route(l)
                gather(l)
                experts(l)
                combine(l)
                layer_norm(2 * l + 1)

        @block.scalar
        def _(act):
            for dst, src in SMALL:
                act.dma_start(dst, src).then_inc(S["small_in"], 16)
            steps = [0]
            n_pj = [0]

            def own(ins):
                steps[0] += 1
                ins.then_inc(S["act_step"], 1)
                act.wait_ge(S["act_step"], steps[0])

            def f(out, in_, func, **kw):
                return act.activation(out, in_, func, **kw)

            def pj():
                n_pj[0] += 1
                act.wait_ge(S["pj_ready"], n_pj[0])
                return bank[(n_pj[0] - 1) % 2]

            def free(ins):
                ins.then_inc(S["pj_free"], 1)

            def project(l, h, n):
                if h >= H:
                    return
                b = h % 2
                if h >= 2 and n == 0:
                    act.wait_ge(S["num_sb"], l * H + h - 1)
                if h >= 2 and n == 5:
                    act.wait_ge(S["o_ready"], l * H + h - 1)
                o = pj()
                if n < 2:
                    ins = f((qT, kT)[n][:, b, :], o[:, 0:N], ACT.Copy, scale=float(DK) ** -0.5 if n == 0 else 1.0)
                elif n < 5:
                    ins = f(vt[:, b, n - 2, :], o[:, 0:DV], ACT.Copy)
                else:
                    ins = f(rT[:, b, n - 5, :], o[:, 0:N], ACT.Silu if l == 0 else ACT.Sigmoid)
                free(ins)

            def head_square(l, h):
                act.wait_ge(S["cent"], l * H + h + 1)
                f(nsq[:, :, :], num[:, :, :], ACT.Square).then_inc(S["sq_ready"], 1)

            def head_std(l, h):
                act.wait_ge(S["var_ready"], l * H + h + 1)
                if l * H + h >= 1:
                    act.wait_ge(S["o_ready"], l * H + h)
                f(rs, bank[4][:, 0:N], ACT.Sqrt, bias=epst[:, 0:1]).then_inc(S["std_ready"], 1)

            def attend_gla(h):
                for d in range(2):
                    act.wait_ge(S["kt_ready"], 2 * h + d + 1)
                    if h >= 1:
                        act.wait_ge(S["ds_ready"], N_STATES * h)
                    f(ktok[:, d, :, :], bank[7][:, 0:N], ACT.Copy).then_inc(S["kt_sb"], 1)
                if h >= 1:
                    head_square(0, h - 1)
                project(0, h + 1, 0)
                if h >= 1:
                    head_std(0, h - 1)
                for n in range(1, PJ_HEAD):
                    project(0, h + 1, n)
                act.wait_ge(S["num_ready"], h + 1)
                if h >= 1:
                    act.wait_ge(S["o_ready"], h)
                for m in range(MV):
                    ins = f(num[:, m, :], bank[2 + m][:, 0:N], ACT.Copy)
                ins.then_inc(S["num_sb"], 1)

            def take_sums(h, d):
                act.wait_ge(S["num_ready"], H + 2 * h + d + 1)
                if h >= 1:
                    act.wait_ge(S["o_ready"], H + h)
                for m in range(MV):
                    ins = f((num, nsq)[d][:, m, :], bank[2 + m][:, 0:N], ACT.Copy)
                ins.then_inc(S["num_cp"], 1)

            def attend_mlstm(h):
                b = h % 2
                act.wait_ge(S["kt_ready"], 2 * H + h + 1)
                if h >= 1:
                    act.wait_ge(S["ds_ready"], N_STATES * (H + h))
                for d in range(2):
                    for t in range(NT):
                        ins = f(ktok[:, d, t, :], bank[7][:, t * P:(t + 1) * P], ACT.Copy,
                                scale=cols[:, (2 + d) * NT + t, h:h + 1])
                ins.then_inc(S["kt_sb"], 1)
                for d in range(2):
                    e = 2 * h + d
                    if e >= 2:
                        act.wait_ge(S["am_ready"], 2 * H + e - 1)
                    o = pj()
                    for t in range(NT):
                        ins = f(expd[:, d, t * P:(t + 1) * P], o[:, t * P:(t + 1) * P], ACT.Exp, scale=-1.0,
                                bias=cols[:, d * NT + t, h:h + 1])
                    free(ins)
                    if e >= 2:
                        act.wait_ge(S["am_ready"], 2 * H + e - 1)
                    free(f(einb[:, d, :], pj()[:, 0:N], ACT.Copy))
                    if e >= 2:
                        act.wait_ge(S["den_free"], e - 1)
                    free(f(emt[:, d, :], pj()[:, 0:N], ACT.Copy))
                project(1, h + 1, 0)
                if h >= 1:
                    head_square(1, h - 1)
                    head_std(1, h - 1)
                for n in range(1, PJ_HEAD):
                    if n == 3:
                        take_sums(h, 0)
                    project(1, h + 1, n)
                take_sums(h, 1)

            def normalise(x):
                for k in range(KD):
                    act.wait_ge(S["lcent"], x * KD + k + 1)
                    f(hT[:, k, :], zT[:, k, :], ACT.Square).then_inc(S["lsq"], 1)
                act.wait_ge(S["lvar"], x + 1)
                f(rs, bank[5][:, 0:N], ACT.Sqrt, bias=epst[:, 0:1]).then_inc(S["lstd"], 1)

            def scaled_by_gate(l, x, p):
                act.wait_ge(S["mod_ready"], l + 1)
                for k in range(KD):
                    b = pj()
                    for s, a, z in STREAMS:
                        ins = f(zT[:, k, a:z], b[:, a:z], ACT.Copy, scale=mod[:, l, p * KD + k, s:s + 1])
                    ins.then_inc(S["pj_free"], 1)
                    act.wait_ge(S["pj_free"], n_pj[0])
                    act.sem_inc(S["yscaled"], 1)

            act.wait_ge(S["small_in"], N_SMALL)
            act.wait_ge(S["consts"], N_CONST)
            f(scT[:, :, :], cT[:, :, :], ACT.Silu).then_inc(S["silu_c"], 1)
            for l in range(DEPTH):
                with act.Fori(0, G_MOD // G) as i:
                    for u in range(G):
                        act.wait_ge(used[2], i * G + (l * G_LAYER + u + 1))
                        f(modrow[:, u, 0:2 * MODW], mod_banks[u][0][0:2, :], ACT.Copy)
                        f(modrow[:, u, 2 * MODW:], mod_banks[u][1][0:2, 0:MODW], ACT.Copy).then_inc(S["mod_sb"], 1)
                if l == 0:
                    free(f(num[0:2 * RANK, 0, :], pj()[0:2 * RANK, 0:N], ACT.Copy))
                    act.wait_ge(S["pj_free"], n_pj[0])
                    act.sem_inc(S["gates_in"], 1)
                    for i in range(2 * H):
                        free(f(ea[:, i, :], pj()[:, 0:N], ACT.Identity, bias=bgate[:, i:i + 1]))
                    act.wait_ge(S["pj_free"], n_pj[0])
                    act.sem_inc(S["logit_sb"], 1)
                    own(f(eb, ea, ACT.Abs))
                    own(f(eb, eb, ACT.Exp, scale=-1.0))
                    f(eb, eb, ACT.Ln, bias=onet[:, 0:1]).then_inc(S["gate_sp"], 1)
                    for n in range(PJ_HEAD):
                        project(l, 0, n)
                    act.wait_ge(S["gate_d"], 1)
                    f(ec[:, :, :], ea, ACT.Exp, scale=-1.0 / TAU).then_inc(S["e_ready"], 1)
                    f(eb, eb, ACT.Exp, scale=-1.0 / TAU).then_inc(S["e_ready"], 1)
                    f(ed, ed, ACT.Exp, scale=1.0 / TAU).then_inc(S["e_ready"], 1)
                    act.wait_ge(S["e_ready"], 1)
                    f(ea, ea, ACT.Exp, scale=1.0 / TAU).then_inc(S["e_ready"], 1)
                else:
                    o = pj()
                    for y in range(4):
                        ins = f(graw[0:H, y, :], o[32 * y:32 * y + H, 0:N], ACT.Copy)
                    free(ins)
                    act.wait_ge(S["exp_in"], 1)
                    for d in range(2):
                        own(f(mir[0:H, d, :], graw[0:H, 1 + 2 * d, :], ACT.Abs))
                    own(f(mir[0:H], mir[0:H], ACT.Exp, scale=-1.0))
                    f(mir[0:H], mir[0:H], ACT.Ln, bias=onet[0:H, 0:1]).then_inc(S["exp_out"], 1)
                    for n in range(PJ_HEAD):
                        project(l, 0, n)
                    act.wait_ge(S["exp_in"], 2)
                    for r in (einr[0:H], ulr[0:H], decr[:, :, :]):
                        ins = f(r, r, ACT.Exp)
                    ins = f(mir[0:H], mir[0:H], ACT.Exp, scale=-1.0)
                    ins.then_inc(S["rows_ready"], 1)
                    act.wait_ge(S["colps"], 1)
                    f(cols[:, :, :], bank[7][:, 0:12 * H], ACT.Copy)
                    f(dec[:, :, :], bank[7][:, 64:64 + 2 * H * NCH], ACT.Copy).then_inc(S["colsb"], 1)
                    act.wait_ge(S["colsb"], 1)
                for h in range(H):
                    (attend_gla if l == 0 else attend_mlstm)(h)
                head_square(l, H - 1)
                head_std(l, H - 1)
                scaled_by_gate(l, 2 * l, 2)
                normalise(2 * l)
                for t in range(NT):
                    for q in range(2):
                        free(f(htok[:, t, q * 512:(q + 1) * 512], pj()[:, :], ACT.Copy))
                act.wait_ge(S["gexp_in"], 2 * l + 1)
                f(gsc[:, :, :], gsc[:, :, :], ACT.Exp).then_inc(S["gexp"], 1)
                act.wait_ge(S["gexp_in"], 2 * l + 2)
                f(R["dd"][:, :], R["dd"][:, :], ACT.Exp).then_inc(S["gexp"], 1)
                act.wait_ge(S["slots"], l + 1)
                for k in range(KD):
                    for q in range(2):
                        free(f(xg[:, k, q * N:(q + 1) * N], pj()[:, 0:N], ACT.Copy))
                act.wait_ge(S["pj_free"], n_pj[0])
                act.sem_inc(S["xg_ready"], 1)
                for c in range(SC):
                    free(f(cw[:, c, :], pj()[:, 0:N], ACT.Copy))
                act.wait_ge(S["pj_free"], n_pj[0])
                act.sem_inc(S["cw_ready"], 1)

                e0 = l * NE

                def gate(e, u):
                    act.wait_ge(S["gu_ready"], e + (e0 + 1))
                    if not (isinstance(e, int) and e0 + e < 2):
                        act.wait_ge(S["hid_ready"], e + (e0 - 1))
                    f(sg[:, u, :, :], bank[2 + u][:, 0:FE * CAP], ACT.Silu).then_inc(S["sg_ready"], 1)

                def keep_y(e, u):
                    off = act.value_load(offi[0:1, bass.ds(e, 1)], min_val=0, max_val=NS)
                    act.wait_ge(S["dn_ready"], e + (e0 + 1))
                    if not (isinstance(e, int) and e0 + e < 1):
                        act.wait_ge(S["ya_done"], e + e0)
                    f(yg[:, 0:4, bass.ds(off, CAP)], bank[4 + 2 * u][:, 0:4 * CAP].rearrange("p (k n) -> p k n", k=4),
                      ACT.Copy).then_inc(S["ya_done"], 1)

                gate(0, 0)
                gate(1, 1)
                keep_y(0, 0)
                with act.Fori(1, NE // G) as i:
                    gate(i * 2, 0)
                    keep_y(i * 2 - 1, 1)
                    gate(i * 2 + 1, 1)
                    keep_y(i * 2, 0)
                keep_y(NE - 1, 1)
                act.wait_ge(S["lists"], l + 1)
                n_ext = act.value_load(xlisti[0:1, 2 * MAXJ:2 * MAXJ + 1], min_val=0, max_val=MAXJ)
                with act.If(n_ext > 0):
                    act.wait_ge(S["ya_done"], e0 + NE)
                    with act.Fori(0, n_ext) as i:
                        off = act.value_load(xlisti[0:1, bass.ds(i + MAXJ, 1)], min_val=0, max_val=NS)
                        act.wait_ge(X[l]["gu"], i + 1)
                        f(sg[:, 0, :, :], bank[2][:, 0:FE * CAP], ACT.Silu).then_inc(X[l]["sg"], 1)
                        act.wait_ge(X[l]["dn"], i + 1)
                        f(yg[:, 0:4, bass.ds(off, CAP)], bank[4][:, 0:4 * CAP].rearrange("p (k n) -> p k n", k=4),
                          ACT.Copy).then_inc(X[l]["ya"], 1)
                        act.wait_ge(X[l]["ya"], i + 1)
                for c in range(SC):
                    for q in range(2):
                        free(f(ysl[:, c, q * 512:(q + 1) * 512], pj()[:, :], ACT.Copy))
                act.wait_ge(S["pj_free"], n_pj[0])
                act.sem_inc(S["ysl_ready"], 1)
                scaled_by_gate(l, 2 * l + 1, 5)
                normalise(2 * l + 1)

        @block.vector
        def _(dve):
            steps = [0]

            def own(ins):
                steps[0] += 1
                ins.then_inc(S["dve_step"], 1)
                dve.wait_ge(S["dve_step"], steps[0])

            def behind(ins):
                steps[0] += 1
                return ins.then_inc(S["dve_step"], 1)

            def catch_up():
                dve.wait_ge(S["dve_step"], steps[0])

            def modulate(l, p):
                for k in range(KD):
                    for s, a, z in STREAMS:
                        ins = dve.tensor_scalar(hT[:, k, a:z], xT[:, k, a:z], mod[:, l, (p + 1) * KD + k, s:s + 1],
                                                mod[:, l, p * KD + k, s:s + 1], ALU.mult, ALU.add)
                ins.then_inc(S["h_ready"], 1)

            def residual(x):
                for k in range(KD):
                    dve.wait_ge(S["yscaled"], x * KD + k + 1)
                    dve.scalar_tensor_tensor(out=zT[:, k, :], in0=xT[:, k, :], scalar=ALPHA, in1=zT[:, k, :],
                                             op0=ALU.mult, op1=ALU.add).then_inc(S["z_ready"], 1)

            def normalise(x):
                dve.wait_ge(S["lmean"], x + 1)
                for k in range(KD):
                    dve.tensor_tensor(zT[:, k, :], zT[:, k, :], bank[4][:, 0:N], ALU.subtract).then_inc(S["lcent"], 1)
                dve.wait_ge(S["lstd"], x + 1)
                own(dve.reciprocal(rs, rs))
                for k in range(KD):
                    behind(dve.tensor_tensor(zT[:, k, :], zT[:, k, :], rs, ALU.mult))
                catch_up()
                for k in range(KD):
                    ins = behind(dve.tensor_scalar(xT[:, k, :], zT[:, k, :], lng[:, x, k:k + 1], lnb[:, x, k:k + 1], ALU.mult, ALU.add))
                catch_up()

            def states(l, h, dirs, n_ds, between):
                step = 0
                for lat, d, s, n, more in chain_steps(dirs):
                    if not more:
                        continue
                    if s != step:
                        between(step)
                        step = s
                    i = n_ds[0]
                    n_ds[0] += 1
                    dve.wait_ge(S["ds_ready"], i + 1)
                    last = not lat and s == 1
                    new = sfin[:, h % 2, d, :] if last else st[:, 2 * lat + d, (s + 1) % 2, :]
                    old = (st0[:, d * H + h, :] if lat else None) if s == 0 else st[:, 2 * lat + d, s % 2, :]
                    bk, _ = state_places(l)[i - N_STATES * (l * H + h)]
                    up = bank[bk][:, 0:DV]
                    dc = dec[:, d * H + h, n:n + 1] if l == 0 else \
                        dec[:, :, :].rearrange("p a b -> p (a b)")[:, (h * 2 + d) * NCH + n:(h * 2 + d) * NCH + n + 1]
                    if last and l * H + h >= 2:
                        dve.wait_ge(out_state[h % 2], 32 * ((l * H + h) // 2))
                    if l == 1:
                        un = bank[bk][:, DV:DV + 1]
                        nnew = nfin[:, d * H + h:d * H + h + 1] if last else nb[:, lat, (s + 1) % 2, :]
                        nold = (nb0 if lat else None) if s == 0 else nb[:, lat, s % 2, :]
                        if nold is None:
                            behind(dve.tensor_copy(nnew, un.broadcast_to([P, P])))
                        elif last:
                            behind(dve.scalar_tensor_tensor(out=nnew, in0=nold[:, 0:1], scalar=dc, in1=un, op0=ALU.mult, op1=ALU.add))
                        else:
                            behind(dve.scalar_tensor_tensor(out=nnew, in0=nold, scalar=dc, in1=un.broadcast_to([P, P]),
                                                            op0=ALU.mult, op1=ALU.add))
                    if old is None:
                        ins = dve.tensor_copy(new, up)
                    else:
                        ins = dve.scalar_tensor_tensor(out=new, in0=old, scalar=dc, in1=up, op0=ALU.mult, op1=ALU.add)
                    ins.then_inc(S["state_ready"], 1)
                    dve.wait_ge(S["state_ready"], n_ds[0])

            def head_norm(l, h):
                b = h % 2
                if l == 0:
                    dve.wait_ge(S["num_sb"], h + 1)
                dve.wait_ge(S["mean_ready"], l * H + h + 1)
                for m in range(MV):
                    ins = dve.tensor_tensor(num[:, m, :], num[:, m, :], bank[4][:, 0:N], ALU.subtract)
                ins.then_inc(S["cent"], 1)

            def head_scale(l, h):
                b = h % 2
                dve.wait_ge(S["cent"], l * H + h + 1)
                dve.wait_ge(S["std_ready"], l * H + h + 1)
                own(dve.reciprocal(rs, rs))
                for m in range(MV):
                    behind(dve.scalar_tensor_tensor(out=num[:, m, :], in0=num[:, m, :], scalar=hng[:, l, 2 * h + m:2 * h + m + 1],
                                                    in1=rs, op0=ALU.mult, op1=ALU.mult))
                catch_up()
                for m in range(MV):
                    ins = dve.tensor_tensor(oT[:, 2 * h + m, :], num[:, m, :], rT[:, b, m, :], ALU.mult)
                ins.then_inc(S["o_ready"], 1)

            n_ds = [0]
            dve.wait_ge(S["small_in"], N_SMALL)
            dve.wait_ge(S["consts"], N_CONST)
            dve.wait_ge(S["x_in"], 16)
            q = KD // 2
            for k in range(q):
                v = xT[:, k, N_CTX:N].rearrange("p (r c) -> p r c", c=GRID_W)
                behind(dve.tensor_tensor(v, v, posr[:, k, :].unsqueeze(2).broadcast_to([P, N_LAT // GRID_W, GRID_W]), ALU.add))
                v = xT[:, q + k, N_CTX:N].rearrange("p (r c) -> p r c", c=GRID_W)
                behind(dve.tensor_tensor(v, v, posc[:, k:k + 1, :].broadcast_to([P, N_LAT // GRID_W, GRID_W]), ALU.add))
            catch_up()
            for l in range(DEPTH):
                dve.wait_ge(S["mod_cols"], l + 1)
                own(dve.tensor_tensor(mod[:, l, :, :], bank[7][:, 0:12 * KD].rearrange("p (a b) -> p a b", b=2),
                                      modb[:, l, :].unsqueeze(2).broadcast_to([P, 6 * KD, 2]), ALU.add))
                behind(dve.tensor_scalar(mod[:, l, KD:2 * KD, :], mod[:, l, KD:2 * KD, :], 1.0, None, ALU.add))
                own(dve.tensor_scalar(mod[:, l, 4 * KD:5 * KD, :], mod[:, l, 4 * KD:5 * KD, :], 1.0, None, ALU.add))
                dve.sem_inc(S["mod_ready"], 1)
                modulate(l, 0)
                if l == 0:
                    dve.wait_ge(S["gate_sp"], 1)
                    own(dve.scalar_tensor_tensor(out=ea, in0=ea, scalar=0.0, in1=eb, op0=ALU.min, op1=ALU.subtract))
                    for d in range(2):
                        for h in range(H):
                            r = slice(None) if d == 0 else slice(None, None, -1)
                            behind(dve.tensor_tensor_scan(ed[:, d * H + h, r], keep[:, :], ea[:, d * H + h, r], 0.0,
                                                          ALU.mult, ALU.add))
                    catch_up()
                    for d in range(2):
                        v = [e[:, d * H:(d + 1) * H, :].rearrange("p a (n c) -> p (a n) c", c=CH) for e in (ea, eb, ed)]
                        ref, last = (CH // 2, CH - 1) if d == 0 else (CH - 1 - CH // 2, 0)
                        for dst, at in ((v[0], ref), (v[1], last)):
                            ins = behind(dve.tensor_tensor(dst, v[2], v[2][:, :, at:at + 1].broadcast_to([P, H * NCH, CH]), ALU.subtract))
                    catch_up()
                    dve.sem_inc(S["gate_d"], 1)
                    dve.wait_ge(S["e_ready"], 4)
                    for d in range(2):
                        last = CH - 1 if d == 0 else 0
                        v = ed[:, d * H:(d + 1) * H, :].rearrange("p a (n c) -> p a n c", c=CH)
                        behind(dve.tensor_copy(dec[:, d * H:(d + 1) * H, :], v[:, :, :, last]))
                    catch_up()
                else:
                    dve.wait_ge(S["pj_free"], N_PJ_L0 + 1)
                    own(dve.tensor_tensor(graw[0:H], graw[0:H], bgt[:, :].unsqueeze(2).broadcast_to([H, 4, N]), ALU.add))
                    dve.sem_inc(S["exp_in"], 1)
                    dve.wait_ge(S["exp_out"], 1)
                    g2 = graw[0:H].rearrange("p (d y) n -> p d y n", y=2)
                    own(dve.scalar_tensor_tensor(out=lf[0:H], in0=g2[:, :, 1, :], scalar=0.0, in1=mir[0:H], op0=ALU.min, op1=ALU.subtract))
                    for d in range(2):
                        r = slice(None) if d == 0 else slice(None, None, -1)
                        behind(dve.tensor_tensor_scan(bcum[0:H, d, r], keep[0:H, :], lf[0:H, d, r], 0.0, ALU.mult, ALU.add))
                    catch_up()
                    own(dve.tensor_tensor(urow[0:H], g2[:, :, 0, :], bcum[0:H], ALU.subtract))
                    for d in range(2):
                        r = slice(None) if d == 0 else slice(None, None, -1)
                        behind(dve.tensor_tensor_scan(wrow[0:H, d, r], fresh[:, :], urow[0:H, d, r], -BIG, ALU.add, ALU.max))
                    behind(dve.memset(mst[:, 0, :, 0], 0.0))
                    behind(dve.tensor_copy(mst[:, 1, :, 0], m0[:, :]))
                    catch_up()
                    for lat, d, s, n, more in chain_steps((0, 1)):
                        c = slice(n * CH, (n + 1) * CH)
                        last = n * CH + (CH - 1 if d == 0 else 0)
                        m = mst[:, lat, d, s:s + 1]
                        own(dve.tensor_scalar(wrow[0:H, d, c], wrow[0:H, d, c], m, None, ALU.max))
                        behind(dve.tensor_tensor(mst[:, lat, d, s + 1:s + 2], wrow[0:H, d, last:last + 1], bcum[0:H, d, last:last + 1], ALU.add))
                        behind(dve.tensor_scalar(einr[0:H, d, c], wrow[0:H, d, c], m, -1.0, ALU.subtract, ALU.mult))
                        behind(dve.tensor_scalar(ulr[0:H, d, c], urow[0:H, d, c], wrow[0:H, d, last:last + 1], None, ALU.subtract))
                        behind(dve.tensor_scalar(decr[:, d, n:n + 1], wrow[0:H, d, last:last + 1], m, -1.0, ALU.subtract, ALU.mult))
                        catch_up()
                    behind(dve.tensor_copy(mfin[:, :], mst[:, 0, :, 2]))
                    own(dve.tensor_tensor(mir[0:H], bcum[0:H], wrow[0:H], ALU.add))
                    dve.sem_inc(S["exp_in"], 1)
                    dve.wait_ge(S["colsb"], 1)

                def scale_gla(h, parts):
                    b = h % 2
                    dve.wait_ge(S["pj_free"], PJ_END[0][h] - PJ_HEAD + 2)
                    for part in parts:
                        for d in range(2):
                            for e, src in (((eb, kT), (ec, kT)), ((ea, qT), (ed, qT)))[part]:
                                ins = dve.tensor_tensor(e[:, d * H + h, :], e[:, d * H + h, :], src[:, b, :], ALU.mult)
                    if 1 in parts:
                        ins.then_inc(S["scaled"], 1)

                if l == 0:
                    scale_gla(0, (0, 1))
                for h in range(H):
                    b = h % 2
                    if l == 0:
                        for d in range(2):
                            dve.wait_ge(S["sc_ready"], 2 * h + d + 1)
                            if h >= 1:
                                dve.wait_ge(S["num_ready"], h)
                            dve.copy_predicated(am[:, d, :], causal[:, d, :, :].rearrange("p a b -> p (a b)").bitcast(I32),
                                                bank[5][:, 0:N]).then_inc(S["am_ready"], 1)
                        if h >= 1:
                            head_norm(l, h - 1)

                        def between(s):
                            if s == 0 and h >= 1:
                                head_scale(0, h - 1)
                            if s == 1 and h + 1 < H:
                                scale_gla(h + 1, (0,))

                        states(l, h, (0, 1), n_ds, between)
                        dve.sem_inc(S["fin_state"], 1)
                        if h + 1 < H:
                            scale_gla(h + 1, (1,))
                    else:
                        dve.wait_ge(S["sc_ready"], 2 * H + h + 1)
                        for d in range(2):
                            base = PJ_END[1][h] + 3 * d
                            dve.wait_ge(S["pj_free"], base + 1)
                            if h >= 1:
                                dve.wait_ge(S["num_ready"], H + 2 * h)
                            own(dve.tensor_tensor(dtmp, expd[:, d, :], bank[5][:, 0:N], ALU.mult))
                            if d == 0:
                                behind(dve.tensor_copy(nb0, n0[:, h:h + 1].broadcast_to([P, P])))
                            own(dve.copy_predicated(am[:, d, :], causal[:, d, :, :].rearrange("p a b -> p (a b)").bitcast(I32), dtmp))
                            dve.wait_ge(S["pj_free"], base + 2)
                            dve.tensor_tensor(qe[:, d, :], qT[:, b, :], einb[:, d, :], ALU.mult).then_inc(S["am_ready"], 1)
                        if h >= 1:
                            head_norm(l, h - 1)
                        for d in range(2):
                            e = 2 * h + d

                            def between(s):
                                if s == 0 and d == 0 and h >= 1:
                                    head_scale(1, h - 1)

                            states(l, h, (d,), n_ds, between)
                            dve.wait_ge(S["num_ready"], H + e + 1)
                            dve.wait_ge(S["pj_free"], PJ_END[1][h] + 3 * d + 3)
                            own(dve.scalar_tensor_tensor(out=rden, in0=bank[4][:, 0:N], scalar=-1.0, in1=emt[:, d, :], op0=ALU.mult, op1=ALU.max))
                            own(dve.tensor_tensor(rden, rden, bank[4][:, 0:N], ALU.max))
                            if d == 0:
                                own(dve.tensor_copy(nb0, n0[:, H + h:H + h + 1].broadcast_to([P, P])))
                            dve.sem_inc(S["den_free"], 1)
                            own(dve.reciprocal(rden, rden))
                            dve.wait_ge(S["num_cp"], e + 1)
                            dst = (num, nsq)[d]
                            own(dve.tensor_tensor(dst[:, :, :], dst[:, :, :], rden.unsqueeze(1).broadcast_to([P, MV, N]), ALU.mult))
                            if d == 1:
                                own(dve.tensor_tensor(num[:, :, :], num[:, :, :], nsq[:, :, :], ALU.add))
                                dve.sem_inc(S["num_sb"], 1)
                        dve.sem_inc(S["fin_state"], 1)
                head_norm(l, H - 1)
                head_scale(l, H - 1)
                if l == 1:
                    dve.sem_inc(S["fin_m"], 1)
                residual(2 * l)
                normalise(2 * l)
                modulate(l, 3)

                def first(onehot, scores, top, pm, w):
                    behind(dve.tensor_reduce(top, scores, AX, ALU.max))
                    catch_up()
                    own(dve.tensor_tensor(onehot, scores, top.unsqueeze(2).broadcast_to([P, NT, w]), ALU.is_equal))
                    own(dve.tensor_tensor(onehot, onehot, ramp[:, EPG - w:EPG].unsqueeze(1).broadcast_to([P, NT, w]), ALU.mult))
                    own(dve.tensor_reduce(pm, onehot, AX, ALU.max))
                    own(dve.tensor_tensor(onehot, onehot, pm.unsqueeze(2).broadcast_to([P, NT, w]), ALU.is_equal))

                for b in range(2):
                    dve.wait_ge(out_state[b], 16 * H * (l + 1))
                dve.wait_ge(S["rt_ready"], l + 1)
                own(dve.tensor_copy(lgt[:, :, :], bank[4][:, 0:NT * (NGRP + NE)].rearrange("p (a b) -> p a b", a=NT)))
                gl = lgt[:, :, 0:NGRP]
                first(goh[:, :, :], gl, R["gmax"][:, :], R["gpm"][:, :], NGRP)
                own(dve.tensor_tensor(gsc[:, :, :], gl, R["gmax"][:, :].unsqueeze(2).broadcast_to([P, NT, NGRP]), ALU.subtract))
                dve.sem_inc(S["gexp_in"], 1)
                for t in range(NT):
                    behind(dve.tensor_tensor(e4[:, t], lgt[:, t, NGRP:].rearrange("p (g e) -> p g e", g=NGRP),
                                             goh[:, t, :].unsqueeze(2).broadcast_to([P, NGRP, EPG]), ALU.mult))
                catch_up()
                own(dve.tensor_reduce(es[:, :, :], e4[:, :, :, :].rearrange("p t g e -> p t e g"), AX, ALU.add))
                first(eoh[:, 0], es[:, :, :], R["m1"][:, :], R["pm"][:, :], EPG)
                own(dve.scalar_tensor_tensor(out=esc[:, :, :], in0=eoh[:, 0], scalar=-BIG, in1=es[:, :, :], op0=ALU.mult, op1=ALU.add))
                first(eoh[:, 1], esc[:, :, :], R["m2"][:, :], R["pm"][:, :], EPG)
                own(dve.tensor_tensor(R["dd"][:, :], R["m2"][:, :], R["m1"][:, :], ALU.subtract))
                dve.sem_inc(S["gexp_in"], 1)
                for y in range(2):
                    for t in range(NT):
                        behind(dve.tensor_tensor(o12[:, y, t, :].rearrange("p (g e) -> p g e", g=NGRP),
                                                 goh[:, t, :].unsqueeze(2).broadcast_to([P, NGRP, EPG]),
                                                 eoh[:, y, t, :].unsqueeze(1).broadcast_to([P, NGRP, EPG]), ALU.mult))
                catch_up()
                dve.tensor_tensor(mb[:, :, :], o12[:, 0], o12[:, 1], ALU.add).then_inc(S["assign"], 1)
                dve.wait_ge(S["gexp"], 2 * l + 2)
                own(dve.tensor_reduce(R["gsum"][:, :], gsc[:, :, :], AX, ALU.add))
                own(dve.reciprocal(R["gw"][:, :], R["gsum"][:, :]))
                own(dve.tensor_scalar(R["den"][:, :], R["dd"][:, :], 1.0, None, ALU.add))
                own(dve.reciprocal(R["den"][:, :], R["den"][:, :]))
                own(dve.tensor_tensor(R["w1"][:, :], R["gw"][:, :], R["den"][:, :], ALU.mult))
                own(dve.tensor_tensor(R["w2"][:, :], R["w1"][:, :], R["dd"][:, :], ALU.mult))
                dve.wait_ge(S["ranks"], l + 1)
                own(dve.tensor_copy(cnt[:, :], bank[5][:, NT * NE:(NT + 1) * NE]))
                own(dve.tensor_tensor_scan(cums[:, :], ones[:, 0:NE], cnt[:, :], 0.0, ALU.mult, ALU.add))
                own(dve.tensor_tensor(offs[:, :], cums[:, :], cnt[:, :], ALU.subtract))
                behind(dve.tensor_copy(offi[:, :], offs[0:1, :]))
                own(dve.tensor_tensor(slt[:, :, :], offs[:, :].unsqueeze(1).broadcast_to([P, NT, NE]),
                                      bank[5][:, 0:NT * NE].rearrange("p (a b) -> p a b", a=NT), ALU.add))
                for y in range(2):
                    own(dve.tensor_tensor(o12[:, y], o12[:, y], slt[:, :, :], ALU.mult))
                    own(dve.tensor_reduce(R[f"s{y + 1}"][:, :], o12[:, y], AX, ALU.add))
                for t in range(NT):
                    own(dve.tensor_scalar(sel[:, t, :], slot_f[:, :], R["s1"][:, t:t + 1], None, ALU.is_equal))
                    own(dve.scalar_tensor_tensor(out=sel[:, t, :], in0=slot_f[:, :], scalar=R["s2"][:, t:t + 1], in1=sel[:, t, :],
                                                 op0=ALU.is_equal, op1=ALU.add))
                own(dve.memset(xg[:, :, NS:NSP], 0.0))
                dve.sem_inc(S["slots"], 1)
                for t in range(NT):
                    own(dve.tensor_scalar(pw[:, t, :], slot_f[:, :], R["s1"][:, t:t + 1], R["w1"][:, t:t + 1], ALU.is_equal, ALU.mult))
                    own(dve.tensor_scalar(htw, slot_f[:, :], R["s2"][:, t:t + 1], R["w2"][:, t:t + 1], ALU.is_equal, ALU.mult))
                    own(dve.tensor_tensor(pw[:, t, :], pw[:, t, :], htw, ALU.add))
                dve.sem_inc(S["pw_ready"], 1)
                ob = lambda a: a[0:1, :].unsqueeze(1).broadcast_to([1, MAXJ, NE])
                more, pos, start, key = xrow
                own(dve.tensor_tensor(more, ob(cnt), jcap[:, :, :], ALU.is_gt))
                flat = lambda a: a.rearrange("p a b -> p (a b)")
                behind(dve.memset(xone, 1.0))
                catch_up()
                own(dve.tensor_tensor_scan(flat(pos), xone, flat(more), 0.0, ALU.mult, ALU.add))
                own(dve.tensor_copy(xlist[:, 2 * MAXJ:2 * MAXJ + 1], flat(pos)[:, MAXJ * NE - 1:MAXJ * NE]))
                own(dve.tensor_tensor(key, pos, more, ALU.mult))
                own(dve.tensor_tensor(start, ob(offs), jcap[:, :, :], ALU.add))
                own(dve.tensor_scalar(xone[:, 0:NE], cums[0:1, :], float(-CAP), None, ALU.add))
                own(dve.tensor_tensor(start, start, ob(xone[:, 0:NE]), ALU.min))
                for i in range(MAXJ):
                    own(dve.scalar_tensor_tensor(out=pos, in0=key, scalar=float(i + 1), in1=eidx[:, :, :], op0=ALU.is_equal, op1=ALU.mult))
                    own(dve.tensor_reduce(xlist[:, i:i + 1], flat(pos), AX, ALU.add))
                    own(dve.scalar_tensor_tensor(out=pos, in0=key, scalar=float(i + 1), in1=start, op0=ALU.is_equal, op1=ALU.mult))
                    own(dve.tensor_reduce(xlist[:, MAXJ + i:MAXJ + i + 1], flat(pos), AX, ALU.add))
                own(dve.tensor_copy(xlisti[:, :], xlist[:, :]))
                dve.sem_inc(S["lists"], 1)

                e0 = l * NE

                def hidden(e, u):
                    dve.wait_ge(S["sg_ready"], e + (e0 + 1))
                    if not (isinstance(e, int) and e0 + e < 2):
                        dve.wait_ge(S["dn_ready"], e + (e0 - 1))
                    dve.tensor_tensor(hid[:, u, :, :].rearrange("p a b -> p (a b)"), sg[:, u, :, :].rearrange("p a b -> p (a b)"),
                                      bank[2 + u][:, FE * CAP:2 * FE * CAP], ALU.mult).then_inc(S["hid_ready"], 1)

                def keep_y(e, u):
                    off = dve.value_load(offi[0:1, bass.ds(e, 1)], min_val=0, max_val=NS)
                    dve.wait_ge(S["dn_ready"], e + (e0 + 1))
                    if not (isinstance(e, int) and e0 + e < 1):
                        dve.wait_ge(S["yd_done"], e + e0)
                    dve.tensor_copy(yg[:, 4:8, bass.ds(off, CAP)], bank[5 + 2 * u][:, 0:4 * CAP].rearrange("p (k n) -> p k n", k=4))\
                       .then_inc(S["yd_done"], 1)

                hidden(0, 0)
                hidden(1, 1)
                keep_y(0, 0)
                with dve.Fori(1, NE // G) as i:
                    hidden(i * 2, 0)
                    keep_y(i * 2 - 1, 1)
                    hidden(i * 2 + 1, 1)
                    keep_y(i * 2, 0)
                keep_y(NE - 1, 1)
                n_ext = dve.value_load(xlisti[0:1, 2 * MAXJ:2 * MAXJ + 1], min_val=0, max_val=MAXJ)
                with dve.If(n_ext > 0):
                    dve.wait_ge(S["yd_done"], e0 + NE)
                    with dve.Fori(0, n_ext) as i:
                        off = dve.value_load(xlisti[0:1, bass.ds(i + MAXJ, 1)], min_val=0, max_val=NS)
                        dve.wait_ge(X[l]["sg"], i + 1)
                        dve.tensor_tensor(hid[:, 0, :, :].rearrange("p a b -> p (a b)"), sg[:, 0, :, :].rearrange("p a b -> p (a b)"),
                                          bank[2][:, FE * CAP:2 * FE * CAP], ALU.mult).then_inc(X[l]["hid"], 1)
                        dve.wait_ge(X[l]["dn"], i + 1)
                        dve.tensor_copy(yg[:, 4:8, bass.ds(off, CAP)], bank[5][:, 0:4 * CAP].rearrange("p (k n) -> p k n", k=4))\
                           .then_inc(X[l]["yd"], 1)
                        dve.wait_ge(X[l]["yd"], i + 1)
                residual(2 * l + 1)
                normalise(2 * l + 1)
                dve.sem_inc(S["layer_done"], 1)


def kernel(x_prompt, x_sample, state_gla_S, state_mlstm_C, state_mlstm_n, state_mlstm_m, c, c_ctx,
           gla_w_in, gla_w_gate, gla_b_gate, gla_norm_g, gla_w_out,
           mlstm_w_in, mlstm_b_gates, mlstm_norm_g, mlstm_w_out,
           adaln_w, adaln_b, ln_g, ln_b,
           moe_w_group, moe_b_group, moe_w_expert, moe_b_expert, moe_w_gate, moe_w_up, moe_w_down):
    import concourse.bacc as bacc
    from concourse.bass_utils import run_bass_kernel_spmd

    def feat(a):
        a = np.asarray(a)
        a = a.reshape(a.shape[:-1] + (a.shape[-1] // P, P))
        return np.moveaxis(a, -1, 0)

    def rows(a, cols):
        a = np.asarray(a)[:, cols]
        return a.reshape(-1, P, a.shape[1]).transpose(1, 0, 2).reshape(P, -1)

    def tokens(a):
        return np.asarray(a).reshape(-1, KD, P).transpose(2, 1, 0)

    r_ = np.r_
    w_mod = np.asarray(adaln_w).reshape(DEPTH, KD, P, 3 * G_MOD, 256).transpose(0, 3, 2, 1, 4).reshape(DEPTH * 3 * G_MOD, P, PIECE)
    w_in, w_out = [], []
    qk, vo = H * DK, 2 * H * DK
    ro = vo + H * DV
    for w in (gla_w_in, mlstm_w_in):
        for h in range(H):
            w_in.append(rows(w[0], r_[h * DK:(h + 1) * DK, qk + h * DK:qk + (h + 1) * DK]))
            w_in.append(rows(w[0], r_[vo + h * DV:vo + (h + 1) * DV]))
            w_in.append(rows(w[0], r_[ro + h * DV:ro + (h + 1) * DV]))
    go = ro + H * DV
    for w in (gla_w_out, mlstm_w_out):
        for q in range(G_OUT):
            a = q * D // G_OUT
            w_out.append(np.concatenate([rows(w[0], r_[a + sum(OUT_W[:j]):a + sum(OUT_W[:j + 1])]) for j in range(3)], 1))
    w_moe = np.stack([
        np.asarray(moe_w_gate).reshape(DEPTH, NE, KD, P, DE).transpose(0, 1, 3, 2, 4).reshape(DEPTH, NE, P, PIECE),
        np.asarray(moe_w_up).reshape(DEPTH, NE, KD, P, DE).transpose(0, 1, 3, 2, 4).reshape(DEPTH, NE, P, PIECE),
        np.asarray(moe_w_down).reshape(DEPTH, NE, FE, P, D).transpose(0, 1, 3, 2, 4).reshape(DEPTH, NE, P, PIECE)], 2)

    nf = D // 4
    freqs = np.exp(-np.log(10000.0) * np.arange(nf) / nf).astype(np.float32)

    def emb(n):
        a = np.arange(n, dtype=np.float32)[:, None] * freqs
        return np.concatenate([np.sin(a), np.cos(a)], -1).reshape(n, KD // 2, P).transpose(2, 1, 0)

    ins = {
        "xT": np.concatenate([tokens(x_prompt[0]), tokens(x_sample[0])], 2),
        "cT": tokens(np.stack([np.asarray(c_ctx), np.asarray(c[0])])),
        "modb": feat(adaln_b),
        "lng": feat(np.asarray(ln_g).reshape(2 * DEPTH, D)),
        "lnb": feat(np.asarray(ln_b).reshape(2 * DEPTH, D)),
        "hng": feat(np.stack([np.asarray(gla_norm_g[0]), np.asarray(mlstm_norm_g[0])])),
        "posr": emb(N_LAT // GRID_W), "posc": emb(GRID_W),
        "wglr": rows(gla_w_in[0], r_[go:go + 2 * RANK]).reshape(P, KD, 2 * RANK),
        "wgate": np.asarray(gla_w_gate[0]),
        "bgate": feat(np.asarray(gla_b_gate[0]).reshape(-1)),
        "wgt": np.stack([rows(mlstm_w_in[0], r_[go + H * y:go + H * (y + 1)]).reshape(P, KD, H) for y in range(4)]),
        "bgt": np.asarray(mlstm_b_gates[0]).T,
        "wrt": np.concatenate([np.asarray(moe_w_group), np.asarray(moe_w_expert)], 2)
                 .reshape(DEPTH, KD, P, NGRP + NE).transpose(2, 0, 1, 3),
        "brt": np.concatenate([np.asarray(moe_b_group), np.asarray(moe_b_expert)], 1)[None],
        "st_gla": np.asarray(state_gla_S[0, 0]).reshape(2 * H, DK, DV).transpose(1, 0, 2),
        "st_ml": np.asarray(state_mlstm_C[0, 0]).reshape(2 * H, DK, DV).transpose(1, 0, 2),
        "n0": np.asarray(state_mlstm_n[0, 0]).reshape(2 * H, DK).T,
        "m0": np.asarray(state_mlstm_m[0, 0]).T,
        "w_mod": w_mod, "w_in": np.stack(w_in), "w_out": np.stack(w_out), "w_moe": w_moe.reshape(DEPTH * NE * 3, P, PIECE),
    }
    outs = {"y": (P, KD, N), "new_S": (2, H, DK, DV), "new_C": (2, H, DK, DV), "new_n": (DK, 2 * H), "new_m": (H, 2)}

    nc = bacc.Bacc("TRN2", target_bir_lowering=False, num_devices=1)
    ins = {n: np.ascontiguousarray(a) for n, a in ins.items()}
    A = {n: nc.dram_tensor("in_" + n, a.shape, mybir.dt.from_np(a.dtype), kind="ExternalInput").ap() for n, a in ins.items()}
    O = {n: nc.dram_tensor("out_" + n, s, F32, kind="ExternalOutput").ap() for n, s in outs.items()}
    backbone_step(nc, A, O)
    got = run_bass_kernel_spmd(nc, [{"in_" + n: a for n, a in ins.items()}], core_ids=[0]).results[0]
    y = got["out_y"].transpose(2, 1, 0).reshape(N, D)
    return (y[None, :N_CTX], y[None, N_CTX:], got["out_new_S"][None, None], got["out_new_C"][None, None],
            got["out_new_n"].T.reshape(1, 1, 2, H, DK), got["out_new_m"].T.reshape(1, 1, 2, H))
```

```python
from contextlib import ExitStack

import numpy as np
import concourse.bass as bass
from concourse import mybir

F32 = mybir.dt.float32
BF16 = mybir.dt.bfloat16
I32 = mybir.dt.int32
ALU = mybir.AluOpType
ACT = mybir.ActivationFunctionType
AX = mybir.AxisListType.X

P = 128
D = 1024
KD = D // P
DEPTH = 2
N_CTX, N_LAT = 128, 256
N = N_CTX + N_LAT
NT = N // P
GRID_W = 64
H = 4
DK, DV = 128, 256
MV = DV // P
RANK = 16
TAU = 16.0
CH = 64
NCH = N // CH
NGRP, EPG = 4, 8
NE = NGRP * EPG
DE = 256
FE = DE // P
EPS = 1e-5
ALPHA = (2.0 * DEPTH) ** 0.25
CAP = 96
NS = 2 * N
NSP = NS + CAP
MAXJ = (NS - 1) // CAP
SC = NS // P
G = 2
PIECE = 2048
MODW = PIECE // KD
BIG = 3.0e38
STREAMS = ((0, 0, N_CTX), (1, N_CTX, N))

G_MOD, G_HEAD, G_OUT, G_EXP = (8, 0), H, 2, NE
LAYER_AT = (0, G_MOD[0] + G_HEAD + G_OUT + G_EXP)
N_GROUPS = (LAYER_AT[1], LAYER_AT[1] + G_HEAD + G_OUT + G_EXP)
HEAD_AT = (G_MOD[0], LAYER_AT[1])
M2 = 3
N_M2 = M2 * NE // 2
AFTER = ((0, 3), (1, 0), (1, 3))
OUT_W = (256, 128, 128)
OUT_CHUNKS = [(j, c) for j in range(3) for c in range(OUT_W[j] // P)]
OUT_BANK = {2: 6, 3: 7, 4: 2}

N_STATES = 10
CHAIN = {(1, 0): (2, 3, 4, 5), (1, 1): (5, 4, 3, 2), (0, 0): (0, 1), (0, 1): (1, 0)}


def chain_steps(dirs):
    out = []
    for s in range(4):
        for lat, d in CHAIN:
            if d in dirs and s < len(CHAIN[lat, d]):
                out.append((lat, d, s, CHAIN[lat, d][s], (not lat) or s < 3))
    return out


def state_places(l):
    past, out = {}, []
    for dirs in (((0, 1),) if l == 0 else ((0,), (1,))):
        for lat, d, s, n, more in chain_steps(dirs):
            if more:
                out.append((6 + n % 2, past.get(n % 2)))
                past[n % 2] = len(out) - 1
    return out


def is_neg(v):
    return isinstance(v, int) and v < 0


def backbone_step(nc, A, O):
    ctx = ExitStack()
    with ctx:
        def sb(name, shape, dt=F32):
            return ctx.enter_context(nc.sbuf_tensor(name, shape, dt))

        def sem(name):
            return ctx.enter_context(nc.semaphore(name))

        bank = [ctx.enter_context(nc.psum_tensor(f"bank{i}", [P, 512], F32)) for i in range(8)]

        ring = sb("ring", [P, G, 3, PIECE])
        xT = sb("xT", [P, KD, N])
        hT = sb("hT", [P, KD, N])
        modrow = hT[0:2, 0:4, :].rearrange("p a b -> p (a b)")[:, 0:G * 2 * MODW].rearrange("p (a b) -> p a b", a=G)
        m0acc = hT[:, 4:8, :].rearrange("p a b -> p (a b)")[:, 0:G * 2 * MODW].rearrange("p (a b c) -> p a b c", a=G, b=2)
        mod_banks = (bank[2], bank[5])
        zT = sb("zT", [P, KD, N])
        st0 = sb("st0", [P, 2 * H, DV])
        n0 = sb("n0", [P, 2 * H])
        m0 = sb("m0", [H, 2])
        cT = sb("cT", [P, KD, 2])
        scT = sb("scT", [P, KD, 2])
        mod = sb("mod", [P, DEPTH, 6 * KD, 2])
        modb = sb("modb", [P, DEPTH, 6 * KD])
        cg = sb("cg", [P, KD, 2])
        cb = sb("cb", [P, KD, 2])
        lng = sb("lng", [P, 2 * DEPTH, KD])
        lnb = sb("lnb", [P, 2 * DEPTH, KD])
        hng = sb("hng", [P, 2, KD])
        wglr = sb("wglr", [P, KD, 2 * RANK])
        bgate = sb("bgate", [P, 2 * H])
        bgt = sb("bgt", [H, 4])
        wrt = sb("wrt", [P, DEPTH, KD, NGRP + NE])
        brt = sb("brt", [1, DEPTH, NGRP + NE])
        ident = sb("ident", [P, P])
        ones_d = sb("ones_d", [P, P])
        ones_v = sb("ones_v", [P, P])
        ones = sb("ones", [P, P])
        onesb = sb("onesb", [P, P], BF16)
        trib = sb("trib", [P, P], BF16)
        rowsel = sb("rowsel", [H, H, P])
        causal = sb("causal", [P, 2, NT, P])
        keep = sb("keep", [P, N])
        fresh = sb("fresh", [H, N])
        slot_f = sb("slot_f", [P, NS])
        ramp = sb("ramp", [P, EPG])
        epst = sb("epst", [P, 1])
        onet = sb("onet", [P, 1])
        jcap = sb("jcap", [1, MAXJ, NE])
        eidx = sb("eidx", [1, MAXJ, NE])
        REGION = 22656
        region = sb("region", [P, REGION])
        taken = {"mix": 0, "moe": 0}

        def part(stage, *dims):
            size = int(np.prod(dims))
            a = taken[stage]
            taken[stage] += size
            assert taken[stage] <= REGION, (stage, taken)
            v = region[:, a:a + size]
            if len(dims) == 2:
                v = v.rearrange("p (a b) -> p a b", a=dims[0])
            if len(dims) == 3:
                v = v.rearrange("p (a b c) -> p a b c", a=dims[0], b=dims[1])
            if len(dims) == 4:
                v = v.rearrange("p (a b c d) -> p a b c d", a=dims[0], b=dims[1], c=dims[2])
            return v

        oT = part("mix", KD, N)
        wgt = oT[:, :, 0:P]
        early = oT.rearrange("p a b -> p (a b)")
        slot_i = early[:, 0:NS].bitcast(I32)
        posc = early[:, NS:NS + KD // 2 * GRID_W].rearrange("p (a b) -> p a b", b=GRID_W)
        posr = early[:, NS + KD // 2 * GRID_W:NS + KD // 2 * (GRID_W + N_LAT // GRID_W)].rearrange("p (a b) -> p a b", a=KD // 2)
        qT = part("mix", 2, N)
        kT = part("mix", 2, N)
        vt = part("mix", 2, NT, DV)
        rT = part("mix", 2, MV, N)
        ktok = part("mix", 2, NT, P)
        am = sb("am", [P, 2, N])
        st = part("mix", 4, 2, DV)
        wgate = st.rearrange("p a b c -> p (a b c)")[0:2 * RANK, 0:2 * H * DK].rearrange("p (a b) -> p a b", a=2)
        sfin = part("mix", 2, 2, DV)
        num = part("mix", MV, N)
        nsq = part("mix", MV, N)
        rs = part("mix", N)
        base_e = taken["mix"]
        ea = part("mix", 2 * H, N)
        eb = part("mix", 2 * H, N)
        ed = part("mix", 2 * H, N)
        ec = zT
        dec = sb("dec", [P, 2 * H, NCH])
        taken["mix"] = base_e
        graw = part("mix", 4, N)
        rows = [part("mix", 2, N) for _ in range(7)]
        lf, bcum, urow, wrow, einr, mir, ulr = rows
        dtmp, rden = graw[:, 0, :], graw[:, 1, :]
        expd, emt = graw[:, 2:4, :], bcum
        einb = lf
        qe = part("mix", 2, N)
        nb = part("mix", 2, 2, P)
        nb0 = part("mix", P)
        mst = sb("mst", [H, 2, 2, 5])
        decr = sb("decr", [H, 2, NCH])
        cols = sb("cols", [P, 12, H])
        nfin = sb("nfin", [P, 2 * H])
        mfin = sb("mfin", [H, 2])
        xg = part("moe", KD, NSP)
        yg = part("moe", KD, NSP)
        htok = part("moe", NT, D)
        cw = part("moe", SC, N)
        ysl = region[:, 0:SC * D].rearrange("p (a b) -> p a b", a=SC)
        sel = region[:, KD * NSP:KD * NSP + NT * NS].rearrange("p (a b) -> p a b", a=NT)
        pw = zT[:, 0:6, :].rearrange("p a b -> p (a b)").rearrange("p (a b) -> p a b", a=NT)
        htw = hT[:, 0:2, :].rearrange("p a b -> p (a b)")
        m2w = zT[:, :, :].rearrange("p a b -> p (a b)").rearrange("p (m k n) -> p m k n", m=M2, k=KD)
        m2acc = hT[:, 0:2, :].rearrange("p a b -> p (a b)").rearrange("p (m s n) -> p m s n", m=M2, s=2)
        sg = part("moe", 2, FE, CAP)
        hid = part("moe", 2, FE, CAP)
        lgt = part("moe", NT, NGRP + NE)
        R = {n: sb("r_" + n, [P, NT]) for n in ("gmax", "gpm", "gsum", "gw", "m1", "m2", "pm", "dd", "den", "w1", "w2", "s1", "s2")}
        gsc = sb("gsc", [P, NT, NGRP])
        goh = sb("goh", [P, NT, NGRP])
        e4 = part("moe", NT, NGRP, EPG)
        es = part("moe", NT, EPG)
        esc = part("moe", NT, EPG)
        eoh = part("moe", 2, NT, EPG)
        o12 = part("moe", 2, NT, NE)
        mb = sb("mb", [P, NT, NE], BF16)
        cnt = sb("cnt", [P, NE])
        cums = sb("cums", [P, NE])
        offs = sb("offs", [P, NE])
        slt = part("moe", NT, NE)
        offi = sb("offi", [1, NE], I32)
        xrow = [hT[0:1, 2 + i, 0:MAXJ * NE].rearrange("p (a b) -> p a b", a=MAXJ) for i in range(4)]
        xone = hT[0:1, 6, 0:MAXJ * NE]
        xlist = sb("xlist", [1, 2 * MAXJ + 1])
        xlisti = sb("xlisti", [1, 2 * MAXJ + 1], I32)

        S = {n: sem(n) for n in (
            "small_in", "c_in", "x_in", "state_in", "consts", "silu_c", "m0_acc", "m0_step", "m0_used", "mod_sb", "m2_acc", "m2_step", "m2_used", "z_norm", "y_ready", "mod_ready", "h_ready",
            "pj_ready", "pj_free", "gates_in", "logit_sb", "gate_sp", "gate_d", "e_ready", 
            "scaled", "kt_ready", "kt_sb", "sc_ready", "am_ready", "num_ready", "num_sb", "ds_ready",
            "state_ready", "mean_ready", "cent", "sq_ready", "var_ready", "std_ready", "o_ready", "den_free", "num_cp",
            "fin_state", "yscaled", "z_ready", "lmean", "lcent", "lsq", "lvar", "lstd",
            "rt_ready", "rt_done", "gexp_in", "gexp", "assign", "ranks", "slots", "lists", "pw_ready", "xg_ready",
            "cw_ready", "gu_ready", "sg_ready", "hid_ready", "dn_ready", "ya_done", "yd_done", "ysl_ready",
            "rows_ready", "rows_sb", "exp_in", "exp_out", "colps", "colsb", "y_out", "m_out", "fin_m", 
            "dve_step", "act_step", "pool_step", "heads_done", "wgt_in", "wgate_in", "ring_back")}
        out_state = [sem(f"out_state{b}") for b in range(2)]
        used = [sem(f"used{j}") for j in range(3)]
        m2_landed = [sem(f"m2_landed{m}") for m in range(M2)]
        landed = [[sem(f"landed{u}_{j}") for j in range(3)] for u in range(G)]
        X = [{n: sem(f"x{n}{l}") for n in ("land", "gu", "sg", "hid", "dn", "ya", "yd")} for l in range(DEPTH)]

        SMALL = [(modb[:, :, :], A["modb"]), (lng[:, :, :], A["lng"]), (lnb[:, :, :], A["lnb"]),
                 (hng[:, :, :], A["hng"]), (posr[:, :, :], A["posr"]), (posc[:, :, :], A["posc"]),
                 (wglr[:, :, :], A["wglr"]), (bgate[:, :], A["bgate"]), (wrt[:, :, :, :], A["wrt"]), (brt[:, :, :], A["brt"]),
                 (n0[:, :], A["n0"]), (m0[:, :], A["m0"]), (bgt[:, :], A["bgt"])]
        N_SMALL = 16 * len(SMALL)
        N_CONST = 18

        PJ_HEAD = 2 + NT + MV
        N_PJ_L0 = 1 + 2 * H + H * PJ_HEAD + KD + 2 * NT + 2 * KD + SC + 2 * SC + KD
        PJ_END = [[1 + 2 * H + PJ_HEAD * (h + 1) for h in range(H)],
                  [N_PJ_L0 + 1 + PJ_HEAD * (h + 1) + 6 * h for h in range(H)]]
        block = ctx.enter_context(nc.Block())

        @block.sync
        def _(sp):
            sp.dma_start(cT[:, :, :], A["cT"]).then_inc(S["c_in"], 16)

            def load(g, src, widths=(PIECE,) * 3):
                u = g[1]
                for j in range(3):
                    if not is_neg(g[0] - G):
                        sp.wait_ge(used[j], g[0] - G + 1)
                    sp.dma_start(ring[:, u, j, 0:widths[j]], src(j)).then_inc(landed[u][j], 16)

            def mod_group(i, u):
                for j, done in enumerate((used[0], used[0], S["m0_acc"])):
                    if not isinstance(i, int):
                        sp.wait_ge(done, i * G + (u + 1 - G))
                    sp.dma_start(ring[:, u, j, :], A["w_mod"][bass.ds((G * i + u) * 3 + j, 1)].rearrange("a p n -> p (a n)"))\
                        .then_inc(landed[u][j], 16)

            for u in range(G):
                mod_group(0, u)
            sp.dma_start(xT[:, :, :], A["xT"]).then_inc(S["x_in"], 16)
            with sp.Fori(1, G_MOD[0] // G) as i:
                for u in range(G):
                    mod_group(i, u)
            sp.dma_start(st0[:, :, :], A["st_gla"]).then_inc(S["state_in"], 16)
            for l in range(DEPTH):
                g0 = HEAD_AT[l]
                for h in range(H):
                    load((g0 + h, h % G), lambda j: A["w_in"][(l * H + h) * 3 + j])
                g0 += G_HEAD
                for q in range(G_OUT):
                    at = (0, OUT_W[0] * KD, (OUT_W[0] + OUT_W[1]) * KD)
                    load((g0 + q, q % G), lambda j: A["w_out"][l * G_OUT + q, :, at[j]:at[j] + OUT_W[j] * KD],
                         [w * KD for w in OUT_W])
                g0 += G_OUT
                if l == 0:
                    sp.wait_ge(S["heads_done"], 1)
                    sp.dma_start(st0[:, :, :], A["st_ml"]).then_inc(S["state_in"], 16)

                def expert_pair(i):
                    for u in range(G):
                        src = lambda j: A["w_moe"][bass.ds((l * NE + G * i + u) * 3 + j, 1)].rearrange("a p n -> p (a n)")
                        if isinstance(i, int):
                            load((g0 + G * i + u, u), src)
                            continue
                        e = G * i + (l * NE + u - G)
                        for j, (s, n) in enumerate(((used[0], G * i + (g0 + u - G)), (S["gu_ready"], e), (S["dn_ready"], e))):
                            sp.wait_ge(s, n + 1)
                            sp.dma_start(ring[:, u, j, :], src(j)).then_inc(landed[u][j], 16)

                expert_pair(0)
                with sp.Fori(1, NE // G) as i:
                    expert_pair(i)
                sp.wait_ge(S["lists"], l + 1)
                n_ext = sp.value_load(xlisti[0:1, 2 * MAXJ:2 * MAXJ + 1], min_val=0, max_val=MAXJ)
                with sp.If(n_ext > 0):
                    for j in range(3):
                        sp.wait_ge(used[j], N_GROUPS[l])
                    with sp.Fori(0, n_ext) as i:
                        e = sp.value_load(xlisti[0:1, bass.ds(i, 1)], min_val=0, max_val=NE - 1)
                        for j in range(3):
                            sp.dma_start(ring[:, 0, j, :],
                                         A["w_moe"][bass.ds((e + l * NE) * 3 + j, 1)].rearrange("a p n -> p (a n)"))\
                              .then_inc(X[l]["land"], 16)
                        sp.wait_ge(X[l]["dn"], i + 1)
                        sp.sem_inc(S["ring_back"], 1)
            for k in range(0, KD, 2):
                sp.wait_ge(S["y_ready"], k + 2)
                sp.dma_start(O["y"][:, k:k + 2], xT[:, k:k + 2, :]).then_inc(S["y_out"], 16)
            sp.wait_ge(S["y_out"], 16 * KD // 2)

        @block.gpsimd
        def _(pool):
            steps = [0]

            def own(ins):
                steps[0] += 1
                ins.then_inc(S["pool_step"], 1)
                pool.wait_ge(S["pool_step"], steps[0])

            ready = lambda ins: ins.then_inc(S["consts"], 1)
            ready(pool.memset(ones_d[:, :], 1.0 / D))
            ready(pool.memset(ones_v[:, :], 1.0 / DV))
            ready(pool.memset(ones[:, :], 1.0))
            ready(pool.memset(onesb[:, :], 1.0))
            ready(pool.memset(epst[:, :], EPS))
            ready(pool.memset(onet[:, :], 1.0))
            own(pool.memset(wgate[:, :, :], 0.0))
            pool.dma_start(wgate[0:RANK, 0, :], A["wgate"][0]).then_inc(S["wgate_in"], 16)
            pool.dma_start(wgate[RANK:2 * RANK, 1, :], A["wgate"][1]).then_inc(S["wgate_in"], 16)
            own(pool.memset(ident[:, :], 0.0))
            ready(pool.affine_select(out=ident[:, :], in_=ident[:, :], compare_op=ALU.not_equal, fill=1.0,
                                     base=0, pattern=[[-1, P]], channel_multiplier=1))
            own(pool.memset(trib[:, :], 1.0))
            ready(pool.affine_select(out=trib[:, :], in_=trib[:, :], compare_op=ALU.is_gt, fill=0.0,
                                     base=0, pattern=[[1, P]], channel_multiplier=-1))
            own(pool.memset(rowsel[:, :, :], 0.0))
            ready(pool.affine_select(out=rowsel[:, :, :], in_=rowsel[:, :, :], compare_op=ALU.not_equal, fill=1.0,
                                     base=0, pattern=[[-1, H], [0, P]], channel_multiplier=1))
            own(pool.memset(causal[:, :, :, :], 1.0))
            own(pool.affine_select(out=causal[:, 0], in_=causal[:, 0], compare_op=ALU.is_ge, fill=0.0,
                                   base=0, pattern=[[0, NT], [1, P]], channel_multiplier=-1))
            own(pool.affine_select(out=causal[:, 1], in_=causal[:, 1], compare_op=ALU.is_ge, fill=0.0,
                                   base=0, pattern=[[0, NT], [-1, P]], channel_multiplier=1))
            ready(pool.affine_select(out=causal[:, 0, :, CH:P], in_=causal[:, 0, :, CH:P], compare_op=ALU.is_ge, fill=0.0,
                                     base=-CH, pattern=[[0, NT], [0, CH]], channel_multiplier=1))
            ready(pool.affine_select(out=causal[:, 1, :, 0:CH], in_=causal[:, 1, :, 0:CH], compare_op=ALU.is_ge, fill=0.0,
                                     base=CH - 1, pattern=[[0, NT], [0, CH]], channel_multiplier=-1))
            own(pool.memset(keep[:, :], 1.0))
            ready(pool.memset(keep[:, 0:N:CH], 0.0))
            own(pool.memset(fresh[:, :], 0.0))
            ready(pool.memset(fresh[:, 0:N:CH], -BIG))
            own(pool.iota(slot_i[:, :], pattern=[[1, NS]], base=0, channel_multiplier=0))
            ready(pool.tensor_copy(slot_f[:, :], slot_i[:, :]))
            for k in range(EPG):
                ins = pool.memset(ramp[:, k:k + 1], float(EPG - k))
            ready(ins)
            for j in range(MAXJ):
                ins = pool.memset(jcap[:, j, :], float(CAP * (j + 1)))
            ready(ins)
            for e in range(NE):
                ins = pool.memset(eidx[:, :, e:e + 1], float(e))
            ready(ins)
            ready(pool.memset(am[:, :, :], 0.0))

            def mod_chunks(i):
                for m in range(M2):
                    if not isinstance(i, int):
                        pool.wait_ge(S["m2_acc"], i * M2 + (m + 1 - M2))
                    pool.dma_start(m2w[:, m].rearrange("p k n -> p (k n)"),
                                 A["w_mod1"][bass.ds(i * M2 + m, 1)].rearrange("a p n -> p (a n)")).then_inc(m2_landed[m], 16)

            for l in range(DEPTH):
                for h in range(H):
                    pool.wait_ge(S["fin_state"], l * H + h + 1)
                    for d in range(2):
                        dst = (O["new_S"] if l == 0 else O["new_C"])[d, h]
                        pool.dma_start(dst, sfin[:, h % 2, d, :]).then_inc(out_state[h % 2], 16)
                if l == 0:
                    pool.wait_ge(S["cw_ready"], 1)
                    mod_chunks(0)
                    with pool.Fori(1, NE // G) as i:
                        mod_chunks(i)
                    pool.wait_ge(S["z_ready"], 2 * KD)
                    own(pool.memset(wgt, 0.0))
                    for y in range(4):
                        pool.dma_start(wgt[:, :, 32 * y:32 * y + H], A["wgt"][y]).then_inc(S["wgt_in"], 16)
            pool.wait_ge(S["fin_m"], 1)
            pool.dma_start(O["new_n"], nfin[:, :]).then_inc(S["m_out"], 16)
            pool.dma_start(O["new_m"], mfin[:, :]).then_inc(S["m_out"], 16)
            pool.wait_ge(S["m_out"], 32)
            for b in range(2):
                pool.wait_ge(out_state[b], 16 * DEPTH * H)

        @block.tensor
        def _(pe):
            n_pj = [0]

            def pj():
                n = n_pj[0]
                n_pj[0] += 1
                if n >= 2:
                    pe.wait_ge(S["pj_free"], n - 1)
                return bank[n % 2]

            read_pieces = []

            def mm(out, lhsT, rhs, start, stop):
                ins = pe.matmul(out, lhsT, rhs, start=start, stop=stop, skip_group_check=True)
                if read_pieces and start and not stop:
                    ins.then_inc(used[read_pieces.pop()], 1)
                return ins

            n_ds = [0]

            def piece(l, g, j):
                gg = LAYER_AT[l] + g
                pe.wait_ge(landed[gg % G][j], 16 * (gg // G + 1))
                return ring[:, gg % G, j, :]

            def modulation():
                def rows(i, u):
                    for j in range(2):
                        pe.wait_ge(landed[u][j], (i + 1) * 16)
                    for k in range(KD):
                        ins = mm(mod_banks[u][0:2, :].rearrange("p (a b) -> p a b", a=2), scT[:, k, :],
                                 ring[:, u, 0:2, k * MODW:(k + 1) * MODW], k == 0, k == KD - 1)
                    ins.then_inc(used[0], 1)

                def columns(i, u):
                    pe.wait_ge(S["mod_sb"], i * G + (u + 1))
                    for c in range(2 * MODW // P):
                        mm(bank[7][:, bass.ds((i * G + u) * 12 + c * 2, 2)], modrow[:, u, c * P:(c + 1) * P],
                           ident[0:2, 0:2], True, True)
                    pe.wait_ge(S["m0_acc"], i * G + (u + 1))
                    for c in range(MODW // P):
                        for x in range(2):
                            ins = mm(bank[7][:, bass.ds((i * G + u) * 12 + (4 * MODW // P + 2 * c + x), 1)],
                                     m0acc[:, u, x, c * P:(c + 1) * P], ones[:, 0:1], True, True)
                    ins.then_inc(S["m0_used"], 1)
                    pe.sem_inc(used[1], 1)
                    pe.sem_inc(used[2], 1)

                assert not read_pieces
                rows(0, 0)
                pe.wait_ge(S["consts"], N_CONST)
                with pe.Fori(0, G_MOD[0] // G - 1) as i:
                    rows(i, 1)
                    columns(i, 0)
                    rows(i + 1, 0)
                    columns(i, 1)
                rows(G_MOD[0] // G - 1, 1)
                columns(G_MOD[0] // G - 1, 0)
                columns(G_MOD[0] // G - 1, 1)

            def mod_sums(i):
                for m in range(M2):
                    pe.wait_ge(S["m2_acc"], i * M2 + (m + 1))
                    for x in range(2):
                        ins = mm(bank[0][:, bass.ds(i * (2 * M2) + (2 * m + x), 1)], m2acc[:, m, x, :], ones[:, 0:1], True, True)
                    ins.then_inc(S["m2_used"], 1)

            open_bank = [None]

            def project_half(l, h, i):
                if h >= H:
                    return
                n = i // 2
                j = (0, 0, 1, 1, 1, 2, 2)[n]
                if i % 2 == 0:
                    piece(l, G_MOD[l] + h, j)
                    open_bank[0] = pj()
                w = ring[:, h % G, j, :].rearrange("p (k n) -> p k n", k=KD)
                b = open_bank[0]
                for k in range(i % 2 * KD // 2, (i % 2 + 1) * KD // 2):
                    if j == 1:
                        t = n - 2
                        ins = mm(b[:, 0:DV], hT[:, k, t * P:(t + 1) * P], w[:, k, :], k == 0, k == KD - 1)
                    else:
                        c = n if n < 2 else n - 5
                        ins = mm(b[:, 0:N], w[:, k, c * P:(c + 1) * P], hT[:, k, :], k == 0, k == KD - 1)
                if i % 2 == 1:
                    ins.then_inc(S["pj_ready"], 1)
                    if n in (1, 4, 6):
                        read_pieces.append(j)

            def project(l, h, n):
                project_half(l, h, 2 * n)
                project_half(l, h, 2 * n + 1)

            def head_mean(l, h):
                n = l * H + h
                pe.wait_ge(S["num_sb"], n + 1)
                for m in range(MV):
                    ins = mm(bank[4][:, 0:N], ones_v[:, :], num[:, m, :], m == 0, m == MV - 1)
                ins.then_inc(S["mean_ready"], 1)

            def head_var(l, h):
                n = l * H + h
                pe.wait_ge(S["sq_ready"], n + 1)
                if n >= 1:
                    pe.wait_ge(S["std_ready"], n)
                for m in range(MV):
                    ins = mm(bank[4][:, 0:N], ones_v[:, :], nsq[:, m, :], m == 0, m == MV - 1)
                ins.then_inc(S["var_ready"], 1)

            def attend_gla(h):
                b = h % 2
                places = state_places(0)
                if h >= 1:
                    pe.wait_ge(S["state_ready"], N_STATES * h)
                pe.wait_ge(S["pj_free"], PJ_END[0][h])
                pe.wait_ge(S["scaled"], h + 1)
                for d in range(2):
                    if d + 2 * h >= 1:
                        pe.wait_ge(S["kt_sb"], 2 * h + d)
                    for t in range(NT):
                        ins = pe.transpose(bank[7][:, t * P:(t + 1) * P], eb[:, d * H + h, t * P:(t + 1) * P], ident[:, :])
                    ins.then_inc(S["kt_ready"], 1)
                for d in range(2):
                    if 2 * h + d >= 1:
                        pe.wait_ge(S["am_ready"], 2 * h + d)
                    for t in range(NT):
                        c = slice(t * P, (t + 1) * P)
                        ins = mm(bank[5][:, c], ec[:, d * H + h, c], ea[:, d * H + h, c], True, True)
                    ins.then_inc(S["sc_ready"], 1)
                if h >= 1:
                    head_mean(0, h - 1)
                project(0, h + 1, 0)
                if h >= 1:
                    head_var(0, h - 1)
                pe.wait_ge(S["am_ready"], 2 * h + 2)
                for m in range(MV):
                    for t in range(NT):
                        c = slice(t * P, (t + 1) * P)
                        for d in range(2):
                            mm(bank[2 + m][:, c], vt[:, b, t, m * P:(m + 1) * P], am[:, d, c], t == 0 and d == 0, False)
                pe.wait_ge(S["kt_sb"], 2 * h + 2)
                pe.wait_ge(S["state_in"], 16)
                made = {}
                steps = chain_steps((0, 1))
                for x, (lat, d, s, n, more) in enumerate(steps):
                    c = slice(n * CH, (n + 1) * CH)
                    if x == 2:
                        project(0, h + 1, 1)
                    if s > 0 and s != steps[x - 1][2]:
                        if s > 1:
                            project(0, h + 1, 2 * s - 1)
                        project(0, h + 1, 2 * s)
                    if s > 0:
                        pe.wait_ge(S["state_ready"], made[lat, d, s - 1])
                    if s > 0 or lat:
                        src = st0[:, d * H + h, :] if s == 0 else st[:, 2 * lat + d, s % 2, :]
                        for m in range(MV):
                            ins = mm(bank[2 + m][:, c], src[:, m * P:(m + 1) * P], ed[:, d * H + h, c], False, x == len(steps) - 1)
                    if more:
                        bk, taken_by = places[n_ds[0] - N_STATES * h]
                        if taken_by is not None:
                            pe.wait_ge(S["state_ready"], N_STATES * h + taken_by + 1)
                        q = slice((n % 2) * CH, (n % 2 + 1) * CH)
                        mm(bank[bk][:, 0:DV], ktok[q, d, n // 2, :], vt[q, b, n // 2, :],
                           True, True).then_inc(S["ds_ready"], 1)
                        n_ds[0] += 1
                        made[lat, d, s] = n_ds[0]
                    if x == len(steps) - 1:
                        ins.then_inc(S["num_ready"], 1)

            def attend_mlstm(h):
                b = h % 2
                places = state_places(1)
                pe.wait_ge(S["state_ready"], N_STATES * (H + h))
                pe.wait_ge(S["pj_free"], PJ_END[1][h])
                if h >= 1:
                    pe.wait_ge(S["kt_sb"], 2 * H + h)
                    pe.wait_ge(S["am_ready"], 2 * H + 2 * h)
                for t in range(NT):
                    ins = pe.transpose(bank[7][:, t * P:(t + 1) * P], kT[:, b, t * P:(t + 1) * P], ident[:, :])
                ins.then_inc(S["kt_ready"], 1)
                for t in range(NT):
                    c = slice(t * P, (t + 1) * P)
                    ins = mm(bank[5][:, c], kT[:, b, c], qT[:, b, c], True, True)
                ins.then_inc(S["sc_ready"], 1)
                for d in range(2):
                    for r in (wrow, einr, mir):
                        o = pj()
                        mm(o[:, 0:N], rowsel[:, h, :], r[0:H, d, :], True, True).then_inc(S["pj_ready"], 1)
                if h >= 1:
                    head_mean(1, h - 1)
                project(1, h + 1, 0)
                if h >= 1:
                    head_var(1, h - 1)
                pe.wait_ge(S["kt_sb"], 2 * H + h + 1)
                pe.wait_ge(S["state_in"], 32)
                for d in range(2):
                    e = 2 * h + d
                    pe.wait_ge(S["am_ready"], 2 * H + e + 1)
                    if d == 1:
                        project_half(1, h + 1, 7)
                        project_half(1, h + 1, 8)
                    if e >= 1:
                        pe.wait_ge(S["num_cp"], e)
                    for m in range(MV):
                        for t in range(NT):
                            c = slice(t * P, (t + 1) * P)
                            mm(bank[2 + m][:, c], vt[:, b, t, m * P:(m + 1) * P], am[:, d, c], t == 0, False)
                    if e >= 1:
                        pe.wait_ge(S["den_free"], e)
                    if d == 0 and h >= 1:
                        pe.wait_ge(S["std_ready"], H + h)
                    mm(bank[4][:, 0:N], ones[:, :], am[:, d, :], True, False)
                    steps = chain_steps((d,))
                    made = {}
                    for x, (lat, d, s, n, more) in enumerate(steps):
                        c = slice(n * CH, (n + 1) * CH)
                        if x >= 1:
                            project_half(1, h + 1, 7 * d + 1 + x)
                        if s > 0:
                            pe.wait_ge(S["state_ready"], made[lat, d, s - 1])
                        if s > 0 or lat:
                            src = st0[:, d * H + h, :] if s == 0 else st[:, 2 * lat + d, s % 2, :]
                            nsrc = nb0 if s == 0 else nb[:, lat, s % 2, :]
                            for m in range(MV):
                                mm(bank[2 + m][:, c], src[:, m * P:(m + 1) * P], qe[:, d, c], False, x == len(steps) - 1)
                            ins = mm(bank[4][:, c], nsrc, qe[:, d, c], False, x == len(steps) - 1)
                        if more:
                            bk, taken_by = places[n_ds[0] - N_STATES * (H + h)]
                            if taken_by is not None:
                                pe.wait_ge(S["state_ready"], N_STATES * (H + h) + taken_by + 1)
                            q = slice((n % 2) * CH, (n % 2 + 1) * CH)
                            kw = ktok[q, d, n // 2, :]
                            mm(bank[bk][:, DV:DV + 1], kw, ones[q, 0:1], True, True)
                            mm(bank[bk][:, 0:DV], kw, vt[q, b, n // 2, :],
                               True, True).then_inc(S["ds_ready"], 1)
                            n_ds[0] += 1
                            made[lat, d, s] = n_ds[0]
                        if x == len(steps) - 1:
                            ins.then_inc(S["num_ready"], 1)

            out_banks = {}

            def out_products(l, c, heads):
                q, (j, at) = c // len(OUT_CHUNKS), OUT_CHUNKS[c % len(OUT_CHUNKS)]
                w = piece(l, G_MOD[l] + G_HEAD + q, j)[:, 0:OUT_W[j] * KD].rearrange("p (k n) -> p k n", k=KD)
                if 0 in heads:
                    if c in OUT_BANK:
                        n_pj[0] += 1
                        out_banks[c] = bank[OUT_BANK[c]]
                    else:
                        out_banks[c] = pj()
                for k in range(MV * heads[0], MV * heads[-1] + MV):
                    ins = mm(out_banks[c][:, 0:N], w[:, k, at * P:(at + 1) * P], oT[:, k, :], k == 0, k == KD - 1)
                return ins

            def finish_heads(l):
                begun = 0
                pe.wait_ge(S["o_ready"], (l + 1) * H - 1)
                pe.wait_ge(S["state_ready"], N_STATES * H * (l + 1))
                for step in ((head_mean, 1, head_var, 2) if l == 0 else (2, head_mean, 1, head_var, 2)):
                    if isinstance(step, int):
                        for _ in range(step):
                            out_products(l, begun, list(range(H - 1)))
                            begun += 1
                    else:
                        step(l, H - 1)
                return begun

            def out_projection(l, begun):
                pe.wait_ge(S["o_ready"], (l + 1) * H)
                for c in range(KD):
                    j, at = OUT_CHUNKS[c % len(OUT_CHUNKS)]
                    out_products(l, c, [H - 1] if c < begun else list(range(H))).then_inc(S["pj_ready"], 1)
                    if c >= 1:
                        norm_mean(2 * l, c - 1)
                    if at == OUT_W[j] // P - 1:
                        read_pieces.append(j)

            def norm_mean(x, k):
                pe.wait_ge(S["z_ready"], x * KD + k + 1)
                return mm(bank[4][:, 0:N], ones_d[:, :], zT[:, k, :], k == 0, k == KD - 1)

            def layer_norm(x):
                norm_mean(x, KD - 1).then_inc(S["lmean"], 1)
                for k in range(KD):
                    pe.wait_ge(S["lsq"], x * KD + k + 1)
                    ins = mm(bank[5][:, 0:N], ones_d[:, :], hT[:, k, :], k == 0, k == KD - 1)
                ins.then_inc(S["lvar"], 1)

            def route(l):
                w = NGRP + NE
                for t in range(NT):
                    c = slice(t * w, (t + 1) * w)
                    mm(bank[4][:, c], ones[0:1, :], brt[0:1, l, :], True, False)
                    for k in range(KD):
                        pe.wait_ge(S["h_ready"], (2 * l + 1) * KD + k + 1)
                        ins = mm(bank[4][:, c], hT[:, k, t * P:(t + 1) * P], wrt[:, l, k, :], False, k == KD - 1)
                ins.then_inc(S["rt_ready"], 1)
                for t in range(NT):
                    for q in range(2):
                        b = pj()
                        for k in range(4):
                            ins = pe.transpose(b[:, k * P:(k + 1) * P], hT[:, 4 * q + k, t * P:(t + 1) * P], ident[:, :])
                        ins.then_inc(S["pj_ready"], 1)
                pe.wait_ge(S["assign"], l + 1)
                for t in range(NT):
                    for s in range(t + 1):
                        mm(bank[5][:, t * NE:(t + 1) * NE], (trib if s == t else onesb)[:, :], mb[:, s, :], s == 0, s == t)
                for s in range(NT):
                    ins = mm(bank[5][:, NT * NE:(NT + 1) * NE], onesb[:, :], mb[:, s, :], s == 0, s == NT - 1)
                ins.then_inc(S["ranks"], 1)

            def gather(l):
                for q in range(2):
                    pe.wait_ge(S["slots"], 2 * l + q + 1)
                    for k in range(KD):
                        b = pj()
                        for t in range(NT):
                            ins = mm(b[:, 0:N], htok[:, t, k * P:(k + 1) * P], sel[:, t, q * N:(q + 1) * N], t == 0, t == NT - 1)
                        ins.then_inc(S["pj_ready"], 1)
                pe.wait_ge(S["pw_ready"], l + 1)
                for c in range(SC):
                    b = pj()
                    for t in range(NT):
                        ins = pe.transpose(b[:, t * P:(t + 1) * P], pw[:, t, c * P:(c + 1) * P], ident[:, :])
                    ins.then_inc(S["pj_ready"], 1)

            def gate_up(l, u, off, out, sig, turn=None):
                for j in range(2):
                    if turn is not None:
                        pe.wait_ge(landed[u][j], turn)
                    w = ring[:, u, j, :].rearrange("p (k n) -> p k n", k=KD)
                    for f in range(FE):
                        for k in range(KD):
                            ins = mm(out[:, (j * FE + f) * CAP:(j * FE + f + 1) * CAP], w[:, k, f * P:(f + 1) * P],
                                     xg[:, k, bass.ds(off, CAP)], k == 0, k == KD - 1)
                    if j == 0 and sig is None:
                        ins.then_inc(used[0], 1)
                return ins

            def down(u, hb, b0, b1):
                w = ring[:, u, 2, :].rearrange("p (k n) -> p k n", k=FE)
                for k in range(KD):
                    o = (b0 if k < 4 else b1)[:, (k % 4) * CAP:(k % 4 + 1) * CAP]
                    for f in range(FE):
                        ins = mm(o, w[:, f, k * P:(k + 1) * P], hid[:, hb, f, :], f == 0, f == FE - 1)
                return ins

            def experts(l):
                g0 = HEAD_AT[l] + G_HEAD + G_OUT
                e0 = l * NE

                def slots_of(e):
                    return [pe.value_load(offi[0:1, bass.ds(e + u, 1)], min_val=0, max_val=NS) for u in range(G)]

                def up_step(e, u, turn, off):
                    if not (isinstance(e, int) and e0 + e < 2):
                        pe.wait_ge(S["hid_ready"], e + (e0 - 1))
                    ins = gate_up(l, u, off, bank[2 + u], None, turn * 16 + 16 * (g0 // G + 1))
                    ins.then_inc(S["gu_ready"], 1)
                    return ins

                def down_step(e, u, turn):
                    pe.wait_ge(landed[u][2], turn * 16 + 16 * (g0 // G + 1))
                    pe.wait_ge(S["hid_ready"], e + (e0 + 1))
                    pe.sem_inc(used[1], 1)
                    if not (isinstance(e, int) and e0 + e < 2):
                        pe.wait_ge(S["ya_done"], e + (e0 - 1))
                        pe.wait_ge(S["yd_done"], e + (e0 - 1))
                    down(u, u, bank[4 + 2 * u], bank[5 + 2 * u]).then_inc(S["dn_ready"], 1)
                    read_pieces.append(2)

                pe.wait_ge(S["xg_ready"], l + 1)
                off = slots_of(0)
                up_step(0, 0, 0, off[0])
                up_step(1, 1, 0, off[1])
                down_step(0, 0, 0)
                with pe.Fori(1, NE // G) as i:
                    off = slots_of(i * 2)
                    up_step(i * 2, 0, i, off[0])
                    if l == 0:
                        mod_sums(i - 1)
                    down_step(i * 2 - 1, 1, i - 1)
                    up_step(i * 2 + 1, 1, i, off[1])
                    down_step(i * 2, 0, i)
                down_step(NE - 1, 1, NE // G - 1)
                if l == 0:
                    mod_sums(NE // G - 1)
                pe.wait_ge(S["dn_ready"], (l + 1) * NE)
                pe.sem_inc(used[read_pieces.pop()], 1)
                pe.wait_ge(S["lists"], l + 1)

                n_ext = pe.value_load(xlisti[0:1, 2 * MAXJ:2 * MAXJ + 1], min_val=0, max_val=MAXJ)
                with pe.If(n_ext > 0):
                    with pe.Fori(0, n_ext) as i:
                        off = pe.value_load(xlisti[0:1, bass.ds(i + MAXJ, 1)], min_val=0, max_val=NS)
                        pe.wait_ge(X[l]["land"], i * 48 + 48)
                        gate_up(l, 0, off, bank[2], X[l]["gu"]).then_inc(X[l]["gu"], 1)
                        pe.wait_ge(X[l]["hid"], i + 1)
                        down(0, 0, bank[4], bank[5]).then_inc(X[l]["dn"], 1)
                        pe.wait_ge(X[l]["ya"], i + 1)
                        pe.wait_ge(X[l]["yd"], i + 1)

            def combine(l):
                pe.wait_ge(S["ya_done"], (l + 1) * NE)
                pe.wait_ge(S["yd_done"], (l + 1) * NE)
                pe.wait_ge(S["cw_ready"], l + 1)
                if l == 0:
                    pe.wait_ge(S["mod_ready"], 2)
                for c in range(SC):
                    for q in range(2):
                        b = pj()
                        for k in range(4):
                            ins = pe.transpose(b[:, k * P:(k + 1) * P], yg[:, 4 * q + k, c * P:(c + 1) * P], ident[:, :])
                        ins.then_inc(S["pj_ready"], 1)
                pe.wait_ge(S["ysl_ready"], l + 1)
                for k in range(KD):
                    b = pj()
                    for c in range(SC):
                        ins = mm(b[:, 0:N], ysl[:, c, k * P:(k + 1) * P], cw[:, c, :], c == 0, c == SC - 1)
                    ins.then_inc(S["pj_ready"], 1)
                    if k >= 1:
                        norm_mean(2 * l + 1, k - 1)

            pe.wait_ge(S["silu_c"], 1)
            for l in range(DEPTH):
                if l == 0:
                    modulation()
                    pe.wait_ge(S["small_in"], N_SMALL)
                    b = pj()
                    for k in range(KD):
                        pe.wait_ge(S["h_ready"], k + 1)
                        ins = mm(b[0:2 * RANK, 0:N], wglr[:, k, :], hT[:, k, :], k == 0, k == KD - 1)
                    ins.then_inc(S["pj_ready"], 1)
                    pe.wait_ge(S["gates_in"], 1)
                    pe.wait_ge(S["wgate_in"], 32)
                    for d in range(2):
                        for h in range(H):
                            b = pj()
                            mm(b[:, 0:N], wgate[:, d, h * DK:(h + 1) * DK], num[0:2 * RANK, 0, :], True, True)\
                                .then_inc(S["pj_ready"], 1)
                else:
                    pe.wait_ge(S["wgt_in"], 64)
                    b = pj()
                    for k in range(KD):
                        pe.wait_ge(S["h_ready"], 2 * l * KD + k + 1)
                        ins = mm(b[:, 0:N], wgt[:, k, :], hT[:, k, :], k == 0, k == KD - 1)
                    ins.then_inc(S["pj_ready"], 1)
                for n in range(PJ_HEAD):
                    project(l, 0, n)
                if l == 1:
                    pe.wait_ge(S["rows_ready"], 1)
                    for y, r in enumerate((urow, ulr)):
                        for d in range(2):
                            for t in range(NT):
                                i = (y * 2 + d) * NT + t
                                pe.transpose(bank[7][:, i * H:(i + 1) * H], r[0:H, d, t * P:(t + 1) * P], ident[0:H, 0:H])
                    for h in range(H):
                        ins = mm(bank[7][:, 64 + h * 2 * NCH:64 + (h + 1) * 2 * NCH], rowsel[:, h, :],
                                 decr[:, :, :].rearrange("p a b -> p (a b)"), True, True)
                    ins.then_inc(S["colps"], 1)
                    pe.wait_ge(S["colsb"], 1)
                for h in range(H):
                    (attend_gla if l == 0 else attend_mlstm)(h)
                begun = finish_heads(l)
                pe.wait_ge(S["num_ready"], H if l == 0 else 3 * H)
                pe.sem_inc(S["heads_done"], 1)
                out_projection(l, begun)
                layer_norm(2 * l)
                route(l)
                gather(l)
                experts(l)
                combine(l)
                layer_norm(2 * l + 1)

        @block.scalar
        def _(act):
            act.wait_ge(S["c_in"], 16)
            f = act.activation
            f(scT[:, :, :], cT[:, :, :], ACT.Silu).then_inc(S["silu_c"], 1)
            for dst, src in SMALL:
                act.dma_start(dst, src).then_inc(S["small_in"], 16)
            steps = [0]
            n_pj = [0]

            def own(ins):
                steps[0] += 1
                ins.then_inc(S["act_step"], 1)
                act.wait_ge(S["act_step"], steps[0])

            def pj():
                n_pj[0] += 1
                act.wait_ge(S["pj_ready"], n_pj[0])
                return bank[(n_pj[0] - 1) % 2]

            def free(ins):
                ins.then_inc(S["pj_free"], 1)

            def project(l, h, n):
                if h >= H:
                    return
                b = h % 2
                if h >= 2 and n == 0:
                    act.wait_ge(S["num_sb"], l * H + h - 1)
                if h >= 2 and n == 5:
                    act.wait_ge(S["o_ready"], l * H + h - 1)
                o = pj()
                if n < 2:
                    ins = f((qT, kT)[n][:, b, :], o[:, 0:N], ACT.Copy, scale=float(DK) ** -0.5 if n == 0 else 1.0)
                elif n < 5:
                    ins = f(vt[:, b, n - 2, :], o[:, 0:DV], ACT.Copy)
                else:
                    ins = f(rT[:, b, n - 5, :], o[:, 0:N], ACT.Silu if l == 0 else ACT.Sigmoid)
                free(ins)

            def head_square(l, h):
                act.wait_ge(S["cent"], l * H + h + 1)
                f(nsq[:, :, :], num[:, :, :], ACT.Square).then_inc(S["sq_ready"], 1)

            def head_std(l, h):
                act.wait_ge(S["var_ready"], l * H + h + 1)
                if l * H + h >= 1:
                    act.wait_ge(S["o_ready"], l * H + h)
                f(rs, bank[4][:, 0:N], ACT.Sqrt, bias=epst[:, 0:1]).then_inc(S["std_ready"], 1)

            def attend_gla(h):
                for d in range(2):
                    act.wait_ge(S["kt_ready"], 2 * h + d + 1)
                    if h >= 1:
                        act.wait_ge(S["ds_ready"], N_STATES * h)
                    f(ktok[:, d, :, :], bank[7][:, 0:N], ACT.Copy).then_inc(S["kt_sb"], 1)
                if h >= 1:
                    head_square(0, h - 1)
                project(0, h + 1, 0)
                if h >= 1:
                    head_std(0, h - 1)
                for n in range(1, PJ_HEAD):
                    project(0, h + 1, n)
                act.wait_ge(S["num_ready"], h + 1)
                if h >= 1:
                    act.wait_ge(S["o_ready"], h)
                for m in range(MV):
                    ins = f(num[:, m, :], bank[2 + m][:, 0:N], ACT.Copy)
                ins.then_inc(S["num_sb"], 1)

            def take_sums(h, d):
                act.wait_ge(S["num_ready"], H + 2 * h + d + 1)
                if h >= 1:
                    act.wait_ge(S["o_ready"], H + h)
                for m in range(MV):
                    ins = f((num, nsq)[d][:, m, :], bank[2 + m][:, 0:N], ACT.Copy)
                ins.then_inc(S["num_cp"], 1)

            def attend_mlstm(h):
                b = h % 2
                act.wait_ge(S["kt_ready"], 2 * H + h + 1)
                if h >= 1:
                    act.wait_ge(S["ds_ready"], N_STATES * (H + h))
                for d in range(2):
                    for t in range(NT):
                        ins = f(ktok[:, d, t, :], bank[7][:, t * P:(t + 1) * P], ACT.Copy,
                                scale=cols[:, (2 + d) * NT + t, h:h + 1])
                ins.then_inc(S["kt_sb"], 1)
                for d in range(2):
                    e = 2 * h + d
                    if e >= 2:
                        act.wait_ge(S["am_ready"], 2 * H + e - 1)
                    o = pj()
                    for t in range(NT):
                        ins = f(expd[:, d, t * P:(t + 1) * P], o[:, t * P:(t + 1) * P], ACT.Exp, scale=-1.0,
                                bias=cols[:, d * NT + t, h:h + 1])
                    free(ins)
                    if e >= 2:
                        act.wait_ge(S["am_ready"], 2 * H + e - 1)
                    free(f(einb[:, d, :], pj()[:, 0:N], ACT.Copy))
                    if e >= 2:
                        act.wait_ge(S["den_free"], e - 1)
                    free(f(emt[:, d, :], pj()[:, 0:N], ACT.Copy))
                project(1, h + 1, 0)
                if h >= 1:
                    head_square(1, h - 1)
                    head_std(1, h - 1)
                for n in range(1, PJ_HEAD):
                    if n == 3:
                        take_sums(h, 0)
                    project(1, h + 1, n)
                take_sums(h, 1)

            def normalise(x):
                for k in range(KD):
                    act.wait_ge(S["lcent"], x * KD + k + 1)
                    f(hT[:, k, :], zT[:, k, :], ACT.Square).then_inc(S["lsq"], 1)
                act.wait_ge(S["lvar"], x + 1)
                f(rs, bank[5][:, 0:N], ACT.Sqrt, bias=epst[:, 0:1]).then_inc(S["lstd"], 1)
                for k in range(KD):
                    act.wait_ge(S["z_norm"], x * KD + k + 1)
                    if x < len(AFTER):
                        for c, a, z in STREAMS:
                            ins = f(hT[:, k, a:z], zT[:, k, a:z], ACT.Identity, scale=cg[:, k, c:c + 1], bias=cb[:, k, c:c + 1])
                        ins.then_inc(S["h_ready"], 1)
                    else:
                        f(xT[:, k, :], zT[:, k, :], ACT.Identity, scale=lng[:, x, k:k + 1], bias=lnb[:, x, k:k + 1])\
                            .then_inc(S["y_ready"], 1)

            def scaled_by_gate(l, x, p):
                act.wait_ge(S["mod_ready"], 2 if x == 1 else l + 1)
                for k in range(KD):
                    b = pj()
                    if x % 2 == 0 and k in OUT_BANK:
                        b = bank[OUT_BANK[k]]
                    for s, a, z in STREAMS:
                        ins = f(zT[:, k, a:z], b[:, a:z], ACT.Copy, scale=mod[:, l, p * KD + k, s:s + 1])
                    ins.then_inc(S["pj_free"], 1)
                    act.wait_ge(S["pj_free"], n_pj[0])
                    act.sem_inc(S["yscaled"], 1)

            for l in range(DEPTH):
                if l == 0:
                    with act.Fori(0, G_MOD[0] // G) as i:
                        for u in range(G):
                            act.wait_ge(used[0], i * G + (u + 1))
                            f(modrow[:, u, :], mod_banks[u][0:2, :], ACT.Copy).then_inc(S["mod_sb"], 1)
                if l == 0:
                    act.wait_ge(S["small_in"], N_SMALL)
                    act.wait_ge(S["consts"], N_CONST)
                    free(f(num[0:2 * RANK, 0, :], pj()[0:2 * RANK, 0:N], ACT.Copy))
                    act.wait_ge(S["pj_free"], n_pj[0])
                    act.sem_inc(S["gates_in"], 1)
                    for i in range(2 * H):
                        free(f(ea[:, i, :], pj()[:, 0:N], ACT.Identity, bias=bgate[:, i:i + 1]))
                    act.wait_ge(S["pj_free"], n_pj[0])
                    act.sem_inc(S["logit_sb"], 1)
                    own(f(eb, ea, ACT.Abs))
                    own(f(eb, eb, ACT.Exp, scale=-1.0))
                    f(eb, eb, ACT.Ln, bias=onet[:, 0:1]).then_inc(S["gate_sp"], 1)
                    for n in range(PJ_HEAD - MV):
                        project(l, 0, n)
                    act.wait_ge(S["gate_d"], 1)
                    f(ec[:, :, :], ea, ACT.Exp, scale=-1.0 / TAU).then_inc(S["e_ready"], 1)
                    f(eb, eb, ACT.Exp, scale=-1.0 / TAU).then_inc(S["e_ready"], 1)
                    f(ed, ed, ACT.Exp, scale=1.0 / TAU).then_inc(S["e_ready"], 1)
                    act.wait_ge(S["e_ready"], 1)
                    f(ea, ea, ACT.Exp, scale=1.0 / TAU).then_inc(S["e_ready"], 1)
                    for n in range(PJ_HEAD - MV, PJ_HEAD):
                        project(l, 0, n)
                else:
                    o = pj()
                    for y in range(4):
                        ins = f(graw[0:H, y, :], o[32 * y:32 * y + H, 0:N], ACT.Copy)
                    free(ins)
                    act.wait_ge(S["exp_in"], 1)
                    for d in range(2):
                        own(f(mir[0:H, d, :], graw[0:H, 1 + 2 * d, :], ACT.Abs))
                    own(f(mir[0:H], mir[0:H], ACT.Exp, scale=-1.0))
                    f(mir[0:H], mir[0:H], ACT.Ln, bias=onet[0:H, 0:1]).then_inc(S["exp_out"], 1)
                    for n in range(PJ_HEAD):
                        project(l, 0, n)
                    act.wait_ge(S["exp_in"], 2)
                    for r in (einr[0:H], ulr[0:H], decr[:, :, :]):
                        ins = f(r, r, ACT.Exp)
                    ins = f(mir[0:H], mir[0:H], ACT.Exp, scale=-1.0)
                    ins.then_inc(S["rows_ready"], 1)
                    act.wait_ge(S["colps"], 1)
                    f(cols[:, :, :], bank[7][:, 0:12 * H], ACT.Copy)
                    f(dec[:, :, :], bank[7][:, 64:64 + 2 * H * NCH], ACT.Copy).then_inc(S["colsb"], 1)
                    act.wait_ge(S["colsb"], 1)
                for h in range(H):
                    (attend_gla if l == 0 else attend_mlstm)(h)
                head_square(l, H - 1)
                head_std(l, H - 1)
                scaled_by_gate(l, 2 * l, 2)
                normalise(2 * l)
                for t in range(NT):
                    for q in range(2):
                        free(f(htok[:, t, q * 512:(q + 1) * 512], pj()[:, :], ACT.Copy))
                act.wait_ge(S["gexp_in"], 2 * l + 1)
                f(gsc[:, :, :], gsc[:, :, :], ACT.Exp).then_inc(S["gexp"], 1)
                act.wait_ge(S["gexp_in"], 2 * l + 2)
                f(R["dd"][:, :], R["dd"][:, :], ACT.Exp).then_inc(S["gexp"], 1)
                act.wait_ge(S["slots"], 2 * l + 1)
                for q in range(2):
                    for k in range(KD):
                        free(f(xg[:, k, q * N:(q + 1) * N], pj()[:, 0:N], ACT.Copy))
                act.wait_ge(S["pj_free"], n_pj[0])
                act.sem_inc(S["xg_ready"], 1)
                for c in range(SC):
                    free(f(cw[:, c, :], pj()[:, 0:N], ACT.Copy))
                act.wait_ge(S["pj_free"], n_pj[0])
                act.sem_inc(S["cw_ready"], 1)

                e0 = l * NE

                def gate(e, u):
                    act.wait_ge(S["gu_ready"], e + (e0 + 1))
                    if not (isinstance(e, int) and e0 + e < 2):
                        act.wait_ge(S["hid_ready"], e + (e0 - 1))
                    f(sg[:, u, :, :], bank[2 + u][:, 0:FE * CAP], ACT.Silu).then_inc(S["sg_ready"], 1)

                def keep_y(e, u):
                    off = act.value_load(offi[0:1, bass.ds(e, 1)], min_val=0, max_val=NS)
                    act.wait_ge(S["dn_ready"], e + (e0 + 1))
                    if not (isinstance(e, int) and e0 + e < 1):
                        act.wait_ge(S["ya_done"], e + e0)
                    f(yg[:, 0:4, bass.ds(off, CAP)], bank[4 + 2 * u][:, 0:4 * CAP].rearrange("p (k n) -> p k n", k=4),
                      ACT.Copy).then_inc(S["ya_done"], 1)

                gate(0, 0)
                gate(1, 1)
                keep_y(0, 0)
                with act.Fori(1, NE // G) as i:
                    gate(i * 2, 0)
                    keep_y(i * 2 - 1, 1)
                    gate(i * 2 + 1, 1)
                    keep_y(i * 2, 0)
                keep_y(NE - 1, 1)
                act.wait_ge(S["lists"], l + 1)
                n_ext = act.value_load(xlisti[0:1, 2 * MAXJ:2 * MAXJ + 1], min_val=0, max_val=MAXJ)
                with act.If(n_ext > 0):
                    act.wait_ge(S["ya_done"], e0 + NE)
                    with act.Fori(0, n_ext) as i:
                        off = act.value_load(xlisti[0:1, bass.ds(i + MAXJ, 1)], min_val=0, max_val=NS)
                        act.wait_ge(X[l]["gu"], i + 1)
                        f(sg[:, 0, :, :], bank[2][:, 0:FE * CAP], ACT.Silu).then_inc(X[l]["sg"], 1)
                        act.wait_ge(X[l]["dn"], i + 1)
                        f(yg[:, 0:4, bass.ds(off, CAP)], bank[4][:, 0:4 * CAP].rearrange("p (k n) -> p k n", k=4),
                          ACT.Copy).then_inc(X[l]["ya"], 1)
                        act.wait_ge(X[l]["ya"], i + 1)
                for c in range(SC):
                    for q in range(2):
                        free(f(ysl[:, c, q * 512:(q + 1) * 512], pj()[:, :], ACT.Copy))
                act.wait_ge(S["pj_free"], n_pj[0])
                act.sem_inc(S["ysl_ready"], 1)
                scaled_by_gate(l, 2 * l + 1, 5)
                normalise(2 * l + 1)

        @block.vector
        def _(dve):
            steps = [0]

            def own(ins):
                steps[0] += 1
                ins.then_inc(S["dve_step"], 1)
                dve.wait_ge(S["dve_step"], steps[0])

            def behind(ins):
                steps[0] += 1
                return ins.then_inc(S["dve_step"], 1)

            def catch_up():
                dve.wait_ge(S["dve_step"], steps[0])

            def modulation_ready(l, cols):
                own(dve.tensor_tensor(mod[:, l, :, :], cols[:, 0:12 * KD].rearrange("p (a b) -> p a b", b=2),
                                      modb[:, l, :].unsqueeze(2).broadcast_to([P, 6 * KD, 2]), ALU.add))
                behind(dve.tensor_scalar(mod[:, l, KD:2 * KD, :], mod[:, l, KD:2 * KD, :], 1.0, None, ALU.add))
                own(dve.tensor_scalar(mod[:, l, 4 * KD:5 * KD, :], mod[:, l, 4 * KD:5 * KD, :], 1.0, None, ALU.add))
                dve.sem_inc(S["mod_ready"], 1)

            def mod_chunk(i, m):
                dve.wait_ge(m2_landed[m], i * 16 + 16)
                if not isinstance(i, int):
                    dve.wait_ge(S["m2_used"], i * M2 + (m + 1 - M2))
                for k in range(KD):
                    if k >= 1:
                        dve.wait_ge(S["m2_step"], i * (M2 * (KD - 1)) + (m * (KD - 1) + k))
                    for x in range(2):
                        acc, w, c = m2acc[:, m, x, :], m2w[:, m, k, :], scT[:, k, x:x + 1]
                        if k == 0:
                            ins = dve.tensor_scalar(acc, w, c, None, ALU.mult)
                        else:
                            ins = dve.scalar_tensor_tensor(out=acc, in0=w, scalar=c, in1=acc, op0=ALU.mult, op1=ALU.add)
                    ins.then_inc(S["m2_step" if k < KD - 1 else "m2_acc"], 1)

            def modulate(l, p):
                for k in range(KD):
                    for s, a, z in STREAMS:
                        ins = dve.tensor_scalar(hT[:, k, a:z], xT[:, k, a:z], mod[:, l, (p + 1) * KD + k, s:s + 1],
                                                mod[:, l, p * KD + k, s:s + 1], ALU.mult, ALU.add)
                    ins.then_inc(S["h_ready"], 1)

            def residual(x):
                if x < len(AFTER):
                    l, p = AFTER[x]
                    scale, shift = (mod[:, l, i * KD:(i + 1) * KD, :] for i in (p + 1, p))
                    behind(dve.tensor_tensor(cg[:, :, :], scale, lng[:, x, :].unsqueeze(2).broadcast_to([P, KD, 2]), ALU.mult))
                    own(dve.tensor_tensor(cb[:, :, :], scale, lnb[:, x, :].unsqueeze(2).broadcast_to([P, KD, 2]), ALU.mult))
                    own(dve.tensor_tensor(cb[:, :, :], cb[:, :, :], shift, ALU.add))
                for k in range(KD):
                    dve.wait_ge(S["yscaled"], x * KD + k + 1)
                    dve.scalar_tensor_tensor(out=zT[:, k, :], in0=xT[:, k, :], scalar=ALPHA, in1=zT[:, k, :],
                                             op0=ALU.mult, op1=ALU.add).then_inc(S["z_ready"], 1)

            def normalise(x):
                dve.wait_ge(S["lmean"], x + 1)
                for k in range(KD):
                    dve.tensor_tensor(zT[:, k, :], zT[:, k, :], bank[4][:, 0:N], ALU.subtract).then_inc(S["lcent"], 1)
                dve.wait_ge(S["lstd"], x + 1)
                own(dve.reciprocal(rs, rs))
                for k in range(KD):
                    dve.tensor_tensor(zT[:, k, :], zT[:, k, :], rs, ALU.mult).then_inc(S["z_norm"], 1)
                if x < len(AFTER):
                    dve.wait_ge(S["z_norm"], (x + 1) * KD)
                    for k in range(KD):
                        behind(dve.tensor_scalar(xT[:, k, :], zT[:, k, :], lng[:, x, k:k + 1], lnb[:, x, k:k + 1], ALU.mult, ALU.add))
                    catch_up()

            def states(l, h, dirs, n_ds, between):
                step = 0
                for lat, d, s, n, more in chain_steps(dirs):
                    if not more:
                        continue
                    if s != step:
                        between(step)
                        step = s
                    i = n_ds[0]
                    n_ds[0] += 1
                    dve.wait_ge(S["ds_ready"], i + 1)
                    last = not lat and s == 1
                    new = sfin[:, h % 2, d, :] if last else st[:, 2 * lat + d, (s + 1) % 2, :]
                    old = (st0[:, d * H + h, :] if lat else None) if s == 0 else st[:, 2 * lat + d, s % 2, :]
                    bk, _ = state_places(l)[i - N_STATES * (l * H + h)]
                    up = bank[bk][:, 0:DV]
                    dc = dec[:, d * H + h, n:n + 1] if l == 0 else \
                        dec[:, :, :].rearrange("p a b -> p (a b)")[:, (h * 2 + d) * NCH + n:(h * 2 + d) * NCH + n + 1]
                    if last and l * H + h >= 2:
                        dve.wait_ge(out_state[h % 2], 32 * ((l * H + h) // 2))
                    if l == 1:
                        un = bank[bk][:, DV:DV + 1]
                        nnew = nfin[:, d * H + h:d * H + h + 1] if last else nb[:, lat, (s + 1) % 2, :]
                        nold = (nb0 if lat else None) if s == 0 else nb[:, lat, s % 2, :]
                        if nold is None:
                            behind(dve.tensor_copy(nnew, un.broadcast_to([P, P])))
                        elif last:
                            behind(dve.scalar_tensor_tensor(out=nnew, in0=nold[:, 0:1], scalar=dc, in1=un, op0=ALU.mult, op1=ALU.add))
                        else:
                            behind(dve.scalar_tensor_tensor(out=nnew, in0=nold, scalar=dc, in1=un.broadcast_to([P, P]),
                                                            op0=ALU.mult, op1=ALU.add))
                    if old is None:
                        ins = dve.tensor_copy(new, up)
                    else:
                        ins = dve.scalar_tensor_tensor(out=new, in0=old, scalar=dc, in1=up, op0=ALU.mult, op1=ALU.add)
                    ins.then_inc(S["state_ready"], 1)
                    dve.wait_ge(S["state_ready"], n_ds[0])

            def head_norm(l, h):
                b = h % 2
                if l == 0:
                    dve.wait_ge(S["num_sb"], h + 1)
                dve.wait_ge(S["mean_ready"], l * H + h + 1)
                for m in range(MV):
                    ins = dve.tensor_tensor(num[:, m, :], num[:, m, :], bank[4][:, 0:N], ALU.subtract)
                ins.then_inc(S["cent"], 1)

            def head_scale(l, h):
                b = h % 2
                dve.wait_ge(S["cent"], l * H + h + 1)
                dve.wait_ge(S["std_ready"], l * H + h + 1)
                own(dve.reciprocal(rs, rs))
                for m in range(MV):
                    behind(dve.scalar_tensor_tensor(out=num[:, m, :], in0=num[:, m, :], scalar=hng[:, l, 2 * h + m:2 * h + m + 1],
                                                    in1=rs, op0=ALU.mult, op1=ALU.mult))
                catch_up()
                for m in range(MV):
                    ins = dve.tensor_tensor(oT[:, 2 * h + m, :], num[:, m, :], rT[:, b, m, :], ALU.mult)
                ins.then_inc(S["o_ready"], 1)

            def mod_piece(i, u):
                dve.wait_ge(landed[u][2], i * 16 + 16)
                if not isinstance(i, int):
                    dve.wait_ge(S["m0_used"], i * G + (u + 1 - G))
                for k in range(KD):
                    if k >= 1:
                        dve.wait_ge(S["m0_step"], i * (G * (KD - 1)) + (u * (KD - 1) + k))
                    for x in range(2):
                        acc, w, c = m0acc[:, u, x, :], ring[:, u, 2, k * MODW:(k + 1) * MODW], scT[:, k, x:x + 1]
                        if k == 0:
                            ins = dve.tensor_scalar(acc, w, c, None, ALU.mult)
                        else:
                            ins = dve.scalar_tensor_tensor(out=acc, in0=w, scalar=c, in1=acc, op0=ALU.mult, op1=ALU.add)
                    ins.then_inc(S["m0_step" if k < KD - 1 else "m0_acc"], 1)

            n_ds = [0]
            dve.wait_ge(S["silu_c"], 1)
            for u in range(G):
                mod_piece(0, u)
            dve.wait_ge(S["small_in"], N_SMALL)
            dve.wait_ge(S["consts"], N_CONST)
            dve.wait_ge(S["x_in"], 16)
            q = KD // 2
            for k in range(q):
                v = xT[:, k, N_CTX:N].rearrange("p (r c) -> p r c", c=GRID_W)
                behind(dve.tensor_tensor(v, v, posr[:, k, :].unsqueeze(2).broadcast_to([P, N_LAT // GRID_W, GRID_W]), ALU.add))
                v = xT[:, q + k, N_CTX:N].rearrange("p (r c) -> p r c", c=GRID_W)
                behind(dve.tensor_tensor(v, v, posc[:, k:k + 1, :].broadcast_to([P, N_LAT // GRID_W, GRID_W]), ALU.add))
            catch_up()
            with dve.Fori(1, G_MOD[0] // G) as i:
                for u in range(G):
                    mod_piece(i, u)
            for l in range(DEPTH):
                if l == 0:
                    dve.wait_ge(S["m0_used"], G_MOD[0])
                    modulation_ready(0, bank[7])
                    modulate(0, 0)
                if l == 0:
                    dve.wait_ge(S["gate_sp"], 1)
                    own(dve.scalar_tensor_tensor(out=ea, in0=ea, scalar=0.0, in1=eb, op0=ALU.min, op1=ALU.subtract))
                    for d in range(2):
                        for h in range(H):
                            r = slice(None) if d == 0 else slice(None, None, -1)
                            behind(dve.tensor_tensor_scan(ed[:, d * H + h, r], keep[:, :], ea[:, d * H + h, r], 0.0,
                                                          ALU.mult, ALU.add))
                    catch_up()
                    for d in range(2):
                        v = [e[:, d * H:(d + 1) * H, :].rearrange("p a (n c) -> p (a n) c", c=CH) for e in (ea, eb, ed)]
                        ref, last = (CH // 2, CH - 1) if d == 0 else (CH - 1 - CH // 2, 0)
                        for dst, at in ((v[0], ref), (v[1], last)):
                            ins = behind(dve.tensor_tensor(dst, v[2], v[2][:, :, at:at + 1].broadcast_to([P, H * NCH, CH]), ALU.subtract))
                    catch_up()
                    dve.sem_inc(S["gate_d"], 1)
                else:
                    dve.wait_ge(S["pj_free"], N_PJ_L0 + 1)
                    own(dve.tensor_tensor(graw[0:H], graw[0:H], bgt[:, :].unsqueeze(2).broadcast_to([H, 4, N]), ALU.add))
                    dve.sem_inc(S["exp_in"], 1)
                    dve.wait_ge(S["exp_out"], 1)
                    g2 = graw[0:H].rearrange("p (d y) n -> p d y n", y=2)
                    own(dve.scalar_tensor_tensor(out=lf[0:H], in0=g2[:, :, 1, :], scalar=0.0, in1=mir[0:H], op0=ALU.min, op1=ALU.subtract))
                    for d in range(2):
                        r = slice(None) if d == 0 else slice(None, None, -1)
                        behind(dve.tensor_tensor_scan(bcum[0:H, d, r], keep[0:H, :], lf[0:H, d, r], 0.0, ALU.mult, ALU.add))
                    catch_up()
                    own(dve.tensor_tensor(urow[0:H], g2[:, :, 0, :], bcum[0:H], ALU.subtract))
                    for d in range(2):
                        r = slice(None) if d == 0 else slice(None, None, -1)
                        behind(dve.tensor_tensor_scan(wrow[0:H, d, r], fresh[:, :], urow[0:H, d, r], -BIG, ALU.add, ALU.max))
                    behind(dve.memset(mst[:, 0, :, 0], 0.0))
                    behind(dve.tensor_copy(mst[:, 1, :, 0], m0[:, :]))
                    catch_up()
                    for lat, d, s, n, more in chain_steps((0, 1)):
                        c = slice(n * CH, (n + 1) * CH)
                        last = n * CH + (CH - 1 if d == 0 else 0)
                        m = mst[:, lat, d, s:s + 1]
                        own(dve.tensor_scalar(wrow[0:H, d, c], wrow[0:H, d, c], m, None, ALU.max))
                        behind(dve.tensor_tensor(mst[:, lat, d, s + 1:s + 2], wrow[0:H, d, last:last + 1], bcum[0:H, d, last:last + 1], ALU.add))
                        behind(dve.tensor_scalar(einr[0:H, d, c], wrow[0:H, d, c], m, -1.0, ALU.subtract, ALU.mult))
                        behind(dve.tensor_scalar(ulr[0:H, d, c], urow[0:H, d, c], wrow[0:H, d, last:last + 1], None, ALU.subtract))
                        behind(dve.tensor_scalar(decr[:, d, n:n + 1], wrow[0:H, d, last:last + 1], m, -1.0, ALU.subtract, ALU.mult))
                        catch_up()
                    behind(dve.tensor_copy(mfin[:, :], mst[:, 0, :, 2]))
                    own(dve.tensor_tensor(mir[0:H], bcum[0:H], wrow[0:H], ALU.add))
                    dve.sem_inc(S["exp_in"], 1)
                    dve.wait_ge(S["colsb"], 1)

                def scale_gla(h, parts):
                    b = h % 2
                    dve.wait_ge(S["pj_free"], PJ_END[0][h] - PJ_HEAD + 2)
                    for part in parts:
                        for d in range(2):
                            for e, src in (((eb, kT), (ec, kT)), ((ea, qT), (ed, qT)))[part]:
                                ins = dve.tensor_tensor(e[:, d * H + h, :], e[:, d * H + h, :], src[:, b, :], ALU.mult)
                    if 1 in parts:
                        ins.then_inc(S["scaled"], 1)

                if l == 0:
                    dve.wait_ge(S["e_ready"], 2)
                    scale_gla(0, (0,))
                    dve.wait_ge(S["e_ready"], 4)
                    for d in range(2):
                        last = CH - 1 if d == 0 else 0
                        v = ed[:, d * H:(d + 1) * H, :].rearrange("p a (n c) -> p a n c", c=CH)
                        behind(dve.tensor_copy(dec[:, d * H:(d + 1) * H, :], v[:, :, :, last]))
                    catch_up()
                    scale_gla(0, (1,))
                for h in range(H):
                    b = h % 2
                    if l == 0:
                        for d in range(2):
                            dve.wait_ge(S["sc_ready"], 2 * h + d + 1)
                            if h >= 1:
                                dve.wait_ge(S["num_ready"], h)
                            dve.copy_predicated(am[:, d, :], causal[:, d, :, :].rearrange("p a b -> p (a b)").bitcast(I32),
                                                bank[5][:, 0:N]).then_inc(S["am_ready"], 1)
                        if h >= 1:
                            head_norm(l, h - 1)

                        def between(s):
                            if s == 0 and h >= 1:
                                head_scale(0, h - 1)
                            if s == 1 and h + 1 < H:
                                scale_gla(h + 1, (0,))

                        states(l, h, (0, 1), n_ds, between)
                        dve.sem_inc(S["fin_state"], 1)
                        if h + 1 < H:
                            scale_gla(h + 1, (1,))
                    else:
                        dve.wait_ge(S["sc_ready"], 2 * H + h + 1)
                        for d in range(2):
                            base = PJ_END[1][h] + 3 * d
                            dve.wait_ge(S["pj_free"], base + 1)
                            if h >= 1:
                                dve.wait_ge(S["num_ready"], H + 2 * h)
                            own(dve.tensor_tensor(dtmp, expd[:, d, :], bank[5][:, 0:N], ALU.mult))
                            if d == 0:
                                behind(dve.tensor_copy(nb0, n0[:, h:h + 1].broadcast_to([P, P])))
                            own(dve.copy_predicated(am[:, d, :], causal[:, d, :, :].rearrange("p a b -> p (a b)").bitcast(I32), dtmp))
                            dve.wait_ge(S["pj_free"], base + 2)
                            dve.tensor_tensor(qe[:, d, :], qT[:, b, :], einb[:, d, :], ALU.mult).then_inc(S["am_ready"], 1)
                        if h >= 1:
                            head_norm(l, h - 1)
                        for d in range(2):
                            e = 2 * h + d

                            def between(s):
                                if s == 0 and d == 0 and h >= 1:
                                    head_scale(1, h - 1)

                            states(l, h, (d,), n_ds, between)
                            dve.wait_ge(S["num_ready"], H + e + 1)
                            dve.wait_ge(S["pj_free"], PJ_END[1][h] + 3 * d + 3)
                            own(dve.scalar_tensor_tensor(out=rden, in0=bank[4][:, 0:N], scalar=-1.0, in1=emt[:, d, :], op0=ALU.mult, op1=ALU.max))
                            own(dve.tensor_tensor(rden, rden, bank[4][:, 0:N], ALU.max))
                            if d == 0:
                                own(dve.tensor_copy(nb0, n0[:, H + h:H + h + 1].broadcast_to([P, P])))
                            dve.sem_inc(S["den_free"], 1)
                            own(dve.reciprocal(rden, rden))
                            dve.wait_ge(S["num_cp"], e + 1)
                            dst = (num, nsq)[d]
                            own(dve.tensor_tensor(dst[:, :, :], dst[:, :, :], rden.unsqueeze(1).broadcast_to([P, MV, N]), ALU.mult))
                            if d == 1:
                                own(dve.tensor_tensor(num[:, :, :], num[:, :, :], nsq[:, :, :], ALU.add))
                                dve.sem_inc(S["num_sb"], 1)
                        dve.sem_inc(S["fin_state"], 1)
                head_norm(l, H - 1)
                head_scale(l, H - 1)
                if l == 1:
                    dve.sem_inc(S["fin_m"], 1)
                residual(2 * l)
                normalise(2 * l)

                def first(onehot, scores, top, pm, w):
                    behind(dve.tensor_reduce(top, scores, AX, ALU.max))
                    catch_up()
                    own(dve.tensor_tensor(onehot, scores, top.unsqueeze(2).broadcast_to([P, NT, w]), ALU.is_equal))
                    own(dve.tensor_tensor(onehot, onehot, ramp[:, EPG - w:EPG].unsqueeze(1).broadcast_to([P, NT, w]), ALU.mult))
                    own(dve.tensor_reduce(pm, onehot, AX, ALU.max))
                    own(dve.tensor_tensor(onehot, onehot, pm.unsqueeze(2).broadcast_to([P, NT, w]), ALU.is_equal))

                for b in range(2):
                    dve.wait_ge(out_state[b], 16 * H * (l + 1))
                dve.wait_ge(S["rt_ready"], l + 1)
                own(dve.tensor_copy(lgt[:, :, :], bank[4][:, 0:NT * (NGRP + NE)].rearrange("p (a b) -> p a b", a=NT)))
                gl = lgt[:, :, 0:NGRP]
                first(goh[:, :, :], gl, R["gmax"][:, :], R["gpm"][:, :], NGRP)
                own(dve.tensor_tensor(gsc[:, :, :], gl, R["gmax"][:, :].unsqueeze(2).broadcast_to([P, NT, NGRP]), ALU.subtract))
                dve.sem_inc(S["gexp_in"], 1)
                for t in range(NT):
                    behind(dve.tensor_tensor(e4[:, t], lgt[:, t, NGRP:].rearrange("p (g e) -> p g e", g=NGRP),
                                             goh[:, t, :].unsqueeze(2).broadcast_to([P, NGRP, EPG]), ALU.mult))
                catch_up()
                own(dve.tensor_reduce(es[:, :, :], e4[:, :, :, :].rearrange("p t g e -> p t e g"), AX, ALU.add))
                first(eoh[:, 0], es[:, :, :], R["m1"][:, :], R["pm"][:, :], EPG)
                own(dve.scalar_tensor_tensor(out=esc[:, :, :], in0=eoh[:, 0], scalar=-BIG, in1=es[:, :, :], op0=ALU.mult, op1=ALU.add))
                first(eoh[:, 1], esc[:, :, :], R["m2"][:, :], R["pm"][:, :], EPG)
                own(dve.tensor_tensor(R["dd"][:, :], R["m2"][:, :], R["m1"][:, :], ALU.subtract))
                dve.sem_inc(S["gexp_in"], 1)
                for y in range(2):
                    for t in range(NT):
                        behind(dve.tensor_tensor(o12[:, y, t, :].rearrange("p (g e) -> p g e", g=NGRP),
                                                 goh[:, t, :].unsqueeze(2).broadcast_to([P, NGRP, EPG]),
                                                 eoh[:, y, t, :].unsqueeze(1).broadcast_to([P, NGRP, EPG]), ALU.mult))
                catch_up()
                dve.tensor_tensor(mb[:, :, :], o12[:, 0], o12[:, 1], ALU.add).then_inc(S["assign"], 1)
                dve.wait_ge(S["gexp"], 2 * l + 2)
                own(dve.tensor_reduce(R["gsum"][:, :], gsc[:, :, :], AX, ALU.add))
                own(dve.reciprocal(R["gw"][:, :], R["gsum"][:, :]))
                own(dve.tensor_scalar(R["den"][:, :], R["dd"][:, :], 1.0, None, ALU.add))
                own(dve.reciprocal(R["den"][:, :], R["den"][:, :]))
                own(dve.tensor_tensor(R["w1"][:, :], R["gw"][:, :], R["den"][:, :], ALU.mult))
                own(dve.tensor_tensor(R["w2"][:, :], R["w1"][:, :], R["dd"][:, :], ALU.mult))
                dve.wait_ge(S["ranks"], l + 1)
                own(dve.tensor_copy(cnt[:, :], bank[5][:, NT * NE:(NT + 1) * NE]))
                own(dve.tensor_tensor_scan(cums[:, :], ones[:, 0:NE], cnt[:, :], 0.0, ALU.mult, ALU.add))
                own(dve.tensor_tensor(offs[:, :], cums[:, :], cnt[:, :], ALU.subtract))
                behind(dve.tensor_copy(offi[:, :], offs[0:1, :]))
                own(dve.tensor_tensor(slt[:, :, :], offs[:, :].unsqueeze(1).broadcast_to([P, NT, NE]),
                                      bank[5][:, 0:NT * NE].rearrange("p (a b) -> p a b", a=NT), ALU.add))
                for y in range(2):
                    own(dve.tensor_tensor(o12[:, y], o12[:, y], slt[:, :, :], ALU.mult))
                    own(dve.tensor_reduce(R[f"s{y + 1}"][:, :], o12[:, y], AX, ALU.add))
                for q in range(2):
                    c = slice(q * N, (q + 1) * N)
                    for t in range(NT):
                        behind(dve.tensor_scalar(sel[:, t, c], slot_f[:, c], R["s1"][:, t:t + 1], None, ALU.is_equal))
                    catch_up()
                    for t in range(NT):
                        behind(dve.scalar_tensor_tensor(out=sel[:, t, c], in0=slot_f[:, c], scalar=R["s2"][:, t:t + 1],
                                                        in1=sel[:, t, c], op0=ALU.is_equal, op1=ALU.add))
                    catch_up()
                    if q == 1:
                        own(dve.memset(xg[:, :, NS:NSP], 0.0))
                    dve.sem_inc(S["slots"], 1)
                for t in range(NT):
                    own(dve.tensor_scalar(pw[:, t, :], slot_f[:, :], R["s1"][:, t:t + 1], R["w1"][:, t:t + 1], ALU.is_equal, ALU.mult))
                    own(dve.tensor_scalar(htw, slot_f[:, :], R["s2"][:, t:t + 1], R["w2"][:, t:t + 1], ALU.is_equal, ALU.mult))
                    own(dve.tensor_tensor(pw[:, t, :], pw[:, t, :], htw, ALU.add))
                dve.sem_inc(S["pw_ready"], 1)
                ob = lambda a: a[0:1, :].unsqueeze(1).broadcast_to([1, MAXJ, NE])
                more, pos, start, key = xrow
                own(dve.tensor_tensor(more, ob(cnt), jcap[:, :, :], ALU.is_gt))
                flat = lambda a: a.rearrange("p a b -> p (a b)")
                behind(dve.memset(xone, 1.0))
                catch_up()
                own(dve.tensor_tensor_scan(flat(pos), xone, flat(more), 0.0, ALU.mult, ALU.add))
                own(dve.tensor_copy(xlist[:, 2 * MAXJ:2 * MAXJ + 1], flat(pos)[:, MAXJ * NE - 1:MAXJ * NE]))
                own(dve.tensor_tensor(key, pos, more, ALU.mult))
                own(dve.tensor_tensor(start, ob(offs), jcap[:, :, :], ALU.add))
                own(dve.tensor_scalar(xone[:, 0:NE], cums[0:1, :], float(-CAP), None, ALU.add))
                own(dve.tensor_tensor(start, start, ob(xone[:, 0:NE]), ALU.min))
                for i in range(MAXJ):
                    own(dve.scalar_tensor_tensor(out=pos, in0=key, scalar=float(i + 1), in1=eidx[:, :, :], op0=ALU.is_equal, op1=ALU.mult))
                    own(dve.tensor_reduce(xlist[:, i:i + 1], flat(pos), AX, ALU.add))
                    own(dve.scalar_tensor_tensor(out=pos, in0=key, scalar=float(i + 1), in1=start, op0=ALU.is_equal, op1=ALU.mult))
                    own(dve.tensor_reduce(xlist[:, MAXJ + i:MAXJ + i + 1], flat(pos), AX, ALU.add))
                own(dve.tensor_copy(xlisti[:, :], xlist[:, :]))
                dve.sem_inc(S["lists"], 1)

                e0 = l * NE

                def hidden(e, u):
                    dve.wait_ge(S["sg_ready"], e + (e0 + 1))
                    if not (isinstance(e, int) and e0 + e < 2):
                        dve.wait_ge(S["dn_ready"], e + (e0 - 1))
                    dve.tensor_tensor(hid[:, u, :, :].rearrange("p a b -> p (a b)"), sg[:, u, :, :].rearrange("p a b -> p (a b)"),
                                      bank[2 + u][:, FE * CAP:2 * FE * CAP], ALU.mult).then_inc(S["hid_ready"], 1)

                def keep_y(e, u):
                    off = dve.value_load(offi[0:1, bass.ds(e, 1)], min_val=0, max_val=NS)
                    dve.wait_ge(S["dn_ready"], e + (e0 + 1))
                    if not (isinstance(e, int) and e0 + e < 1):
                        dve.wait_ge(S["yd_done"], e + e0)
                    dve.tensor_copy(yg[:, 4:8, bass.ds(off, CAP)], bank[5 + 2 * u][:, 0:4 * CAP].rearrange("p (k n) -> p k n", k=4))\
                       .then_inc(S["yd_done"], 1)

                def chunk(i, m):
                    if l == 0:
                        mod_chunk(i, m)

                hidden(0, 0)
                chunk(0, 0)
                hidden(1, 1)
                chunk(0, 1)
                keep_y(0, 0)
                chunk(0, 2)
                with dve.Fori(1, NE // G) as i:
                    hidden(i * 2, 0)
                    keep_y(i * 2 - 1, 1)
                    chunk(i, 0)
                    hidden(i * 2 + 1, 1)
                    chunk(i, 1)
                    keep_y(i * 2, 0)
                    chunk(i, 2)
                keep_y(NE - 1, 1)
                n_ext = dve.value_load(xlisti[0:1, 2 * MAXJ:2 * MAXJ + 1], min_val=0, max_val=MAXJ)
                with dve.If(n_ext > 0):
                    dve.wait_ge(S["yd_done"], e0 + NE)
                    with dve.Fori(0, n_ext) as i:
                        off = dve.value_load(xlisti[0:1, bass.ds(i + MAXJ, 1)], min_val=0, max_val=NS)
                        dve.wait_ge(X[l]["sg"], i + 1)
                        dve.tensor_tensor(hid[:, 0, :, :].rearrange("p a b -> p (a b)"), sg[:, 0, :, :].rearrange("p a b -> p (a b)"),
                                          bank[2][:, FE * CAP:2 * FE * CAP], ALU.mult).then_inc(X[l]["hid"], 1)
                        dve.wait_ge(X[l]["dn"], i + 1)
                        dve.tensor_copy(yg[:, 4:8, bass.ds(off, CAP)], bank[5][:, 0:4 * CAP].rearrange("p (k n) -> p k n", k=4))\
                           .then_inc(X[l]["yd"], 1)
                        dve.wait_ge(X[l]["yd"], i + 1)
                if l == 0:
                    dve.wait_ge(S["m2_used"], N_M2)
                    modulation_ready(1, bank[0])
                residual(2 * l + 1)
                normalise(2 * l + 1)


def kernel(x_prompt, x_sample, state_gla_S, state_mlstm_C, state_mlstm_n, state_mlstm_m, c, c_ctx,
           gla_w_in, gla_w_gate, gla_b_gate, gla_norm_g, gla_w_out,
           mlstm_w_in, mlstm_b_gates, mlstm_norm_g, mlstm_w_out,
           adaln_w, adaln_b, ln_g, ln_b,
           moe_w_group, moe_b_group, moe_w_expert, moe_b_expert, moe_w_gate, moe_w_up, moe_w_down):
    import concourse.bacc as bacc
    from concourse.bass_utils import run_bass_kernel_spmd

    def feat(a):
        a = np.asarray(a)
        a = a.reshape(a.shape[:-1] + (a.shape[-1] // P, P))
        return np.moveaxis(a, -1, 0)

    def rows(a, cols):
        a = np.asarray(a)[:, cols]
        return a.reshape(-1, P, a.shape[1]).transpose(1, 0, 2).reshape(P, -1)

    def tokens(a):
        return np.asarray(a).reshape(-1, KD, P).transpose(2, 1, 0)

    r_ = np.r_
    w_mod = np.asarray(adaln_w[0]).reshape(KD, P, 3 * G_MOD[0], MODW).transpose(2, 1, 0, 3).reshape(3 * G_MOD[0], P, PIECE)
    w_mod1 = np.asarray(adaln_w[1]).reshape(KD, P, N_M2, P).transpose(2, 1, 0, 3).reshape(N_M2, P, D)
    w_in, w_out = [], []
    qk, vo = H * DK, 2 * H * DK
    ro = vo + H * DV
    for w in (gla_w_in, mlstm_w_in):
        for h in range(H):
            w_in.append(rows(w[0], r_[h * DK:(h + 1) * DK, qk + h * DK:qk + (h + 1) * DK]))
            w_in.append(rows(w[0], r_[vo + h * DV:vo + (h + 1) * DV]))
            w_in.append(rows(w[0], r_[ro + h * DV:ro + (h + 1) * DV]))
    go = ro + H * DV
    for w in (gla_w_out, mlstm_w_out):
        for q in range(G_OUT):
            a = q * D // G_OUT
            w_out.append(np.concatenate([rows(w[0], r_[a + sum(OUT_W[:j]):a + sum(OUT_W[:j + 1])]) for j in range(3)], 1))
    w_moe = np.stack([
        np.asarray(moe_w_gate).reshape(DEPTH, NE, KD, P, DE).transpose(0, 1, 3, 2, 4).reshape(DEPTH, NE, P, PIECE),
        np.asarray(moe_w_up).reshape(DEPTH, NE, KD, P, DE).transpose(0, 1, 3, 2, 4).reshape(DEPTH, NE, P, PIECE),
        np.asarray(moe_w_down).reshape(DEPTH, NE, FE, P, D).transpose(0, 1, 3, 2, 4).reshape(DEPTH, NE, P, PIECE)], 2)

    nf = D // 4
    freqs = np.exp(-np.log(10000.0) * np.arange(nf) / nf).astype(np.float32)

    def emb(n):
        a = np.arange(n, dtype=np.float32)[:, None] * freqs
        return np.concatenate([np.sin(a), np.cos(a)], -1).reshape(n, KD // 2, P).transpose(2, 1, 0)

    ins = {
        "xT": np.concatenate([tokens(x_prompt[0]), tokens(x_sample[0])], 2),
        "cT": tokens(np.stack([np.asarray(c_ctx), np.asarray(c[0])])),
        "modb": feat(adaln_b),
        "lng": feat(np.asarray(ln_g).reshape(2 * DEPTH, D)),
        "lnb": feat(np.asarray(ln_b).reshape(2 * DEPTH, D)),
        "hng": feat(np.stack([np.asarray(gla_norm_g[0]), np.asarray(mlstm_norm_g[0])])),
        "posr": emb(N_LAT // GRID_W), "posc": emb(GRID_W),
        "wglr": rows(gla_w_in[0], r_[go:go + 2 * RANK]).reshape(P, KD, 2 * RANK),
        "wgate": np.asarray(gla_w_gate[0]),
        "bgate": feat(np.asarray(gla_b_gate[0]).reshape(-1)),
        "wgt": np.stack([rows(mlstm_w_in[0], r_[go + H * y:go + H * (y + 1)]).reshape(P, KD, H) for y in range(4)]),
        "bgt": np.asarray(mlstm_b_gates[0]).T,
        "wrt": np.concatenate([np.asarray(moe_w_group), np.asarray(moe_w_expert)], 2)
                 .reshape(DEPTH, KD, P, NGRP + NE).transpose(2, 0, 1, 3),
        "brt": np.concatenate([np.asarray(moe_b_group), np.asarray(moe_b_expert)], 1)[None],
        "st_gla": np.asarray(state_gla_S[0, 0]).reshape(2 * H, DK, DV).transpose(1, 0, 2),
        "st_ml": np.asarray(state_mlstm_C[0, 0]).reshape(2 * H, DK, DV).transpose(1, 0, 2),
        "n0": np.asarray(state_mlstm_n[0, 0]).reshape(2 * H, DK).T,
        "m0": np.asarray(state_mlstm_m[0, 0]).T,
        "w_mod": w_mod, "w_mod1": w_mod1, "w_in": np.stack(w_in), "w_out": np.stack(w_out), "w_moe": w_moe.reshape(DEPTH * NE * 3, P, PIECE),
    }
    outs = {"y": (P, KD, N), "new_S": (2, H, DK, DV), "new_C": (2, H, DK, DV), "new_n": (DK, 2 * H), "new_m": (H, 2)}

    nc = bacc.Bacc("TRN2", target_bir_lowering=False, num_devices=1)
    ins = {n: np.ascontiguousarray(a) for n, a in ins.items()}
    A = {n: nc.dram_tensor("in_" + n, a.shape, mybir.dt.from_np(a.dtype), kind="ExternalInput").ap() for n, a in ins.items()}
    O = {n: nc.dram_tensor("out_" + n, s, F32, kind="ExternalOutput").ap() for n, s in outs.items()}
    backbone_step(nc, A, O)
    got = run_bass_kernel_spmd(nc, [{"in_" + n: a for n, a in ins.items()}], core_ids=[0]).results[0]
    y = got["out_y"].transpose(2, 1, 0).reshape(N, D)
    return (y[None, :N_CTX], y[None, N_CTX:], got["out_new_S"][None, None], got["out_new_C"][None, None],
            got["out_new_n"].T.reshape(1, 1, 2, H, DK), got["out_new_m"].T.reshape(1, 1, 2, H))
```
